# Optimizing a Trainium2 kernel written in Bass

```python
import jax, jax.numpy as jnp
from jax import lax
import numpy as np

D_MODEL = 1024
BATCH = 1
SEQ = 256
DEPTH = 2

MOBA_HEADS = 8
MOBA_HEAD_DIM = D_MODEL // 16
MOBA_WIDTH = MOBA_HEADS * MOBA_HEAD_DIM
MOBA_BLOCK = 256
MOBA_TOPK = 3
MOBA_Q_CHUNK = 64
ROPE_THETA = 10000.0
GLA_HEADS = 4
GLA_DK = D_MODEL // 16
GLA_DV = D_MODEL // 8
GLA_KW = GLA_HEADS * GLA_DK
GLA_VW = GLA_HEADS * GLA_DV
GLA_RANK = 16
GLA_TEMP = 16.0
GLA_CHUNK = 64
CONV_CH = D_MODEL // 2
CONV_WIDTH = 31
D_FF = 4 * D_MODEL
N_BRANCH = 3
EPS = 1e-6
NEG = -1e30
IN_SIZES = (MOBA_WIDTH, MOBA_WIDTH, MOBA_WIDTH,
            GLA_KW, GLA_KW, GLA_VW, GLA_RANK, GLA_VW,
            CONV_CH, CONV_CH,
            N_BRANCH * D_MODEL)
IN_WIDTH = sum(IN_SIZES)

kernel_name = 'hybrid_moba_gla_conformer_gated'

def rms_norm(x, g):
    xf = x.astype(jnp.float32)
    y = xf * lax.rsqrt(jnp.mean(xf * xf, axis=-1, keepdims=True) + EPS)
    return (y * g.astype(jnp.float32)).astype(x.dtype)

def layer_norm(x, g, b):
    xf = x.astype(jnp.float32)
    mu = jnp.mean(xf, axis=-1, keepdims=True)
    var = jnp.mean(jnp.square(xf - mu), axis=-1, keepdims=True)
    y = (xf - mu) * lax.rsqrt(var + EPS)
    return (y * g.astype(jnp.float32) + b.astype(jnp.float32)).astype(x.dtype)

def rope_tables(positions):
    half = MOBA_HEAD_DIM // 2
    inv_freq = ROPE_THETA ** (-jnp.arange(half, dtype=jnp.float32) / half)
    ang = positions.astype(jnp.float32)[..., None] * inv_freq
    return jnp.cos(ang)[:, :, None, :], jnp.sin(ang)[:, :, None, :]

def apply_rope(x, cos, sin):
    xf = x.astype(jnp.float32)
    x1, x2 = jnp.split(xf, 2, axis=-1)
    return jnp.concatenate([x1 * cos - x2 * sin, x2 * cos + x1 * sin], axis=-1).astype(x.dtype)

def gather_blocks(blocks, idx):
    return jax.vmap(jax.vmap(lambda t, i: t[i]))(blocks, idx)

def moba_attention(q, k, v):
    B, H, S, Dh = q.shape
    nb = -(-S // MOBA_BLOCK)
    pad = nb * MOBA_BLOCK - S
    kb = jnp.pad(k, ((0, 0), (0, 0), (0, pad), (0, 0))).reshape(B, H, nb, MOBA_BLOCK, Dh)
    vb = jnp.pad(v, ((0, 0), (0, 0), (0, pad), (0, 0))).reshape(B, H, nb, MOBA_BLOCK, Dh)
    kmean = jnp.mean(kb.astype(jnp.float32), axis=3)
    gate = jnp.einsum('bhsd,bhnd->bhsn', q.astype(jnp.float32), kmean)
    qblk = jnp.arange(S) // MOBA_BLOCK
    past = jnp.arange(nb)[None, :] < qblk[:, None]
    gate = jnp.where(past, gate, -jnp.inf)
    n_sel = min(MOBA_TOPK, nb)
    _, gidx = lax.top_k(gate, n_sel)
    sel_valid = jnp.arange(n_sel)[None, :] < qblk[:, None]
    scale = Dh ** -0.5
    n_qc = S // MOBA_Q_CHUNK

    def chunk(c):
        start = c * MOBA_Q_CHUNK
        qc = lax.dynamic_slice_in_dim(q, start, MOBA_Q_CHUNK, axis=2)
        idx = lax.dynamic_slice_in_dim(gidx, start, MOBA_Q_CHUNK, axis=2)
        valid = lax.dynamic_slice_in_dim(sel_valid, start, MOBA_Q_CHUNK, axis=0)
        own = start // MOBA_BLOCK
        k_own = lax.dynamic_index_in_dim(kb, own, axis=2, keepdims=False)
        v_own = lax.dynamic_index_in_dim(vb, own, axis=2, keepdims=False)
        qpos = start + jnp.arange(MOBA_Q_CHUNK)
        kpos = own * MOBA_BLOCK + jnp.arange(MOBA_BLOCK)
        s_own = jnp.einsum('bhqd,bhkd->bhqk', qc, k_own).astype(jnp.float32) * scale
        s_own = jnp.where(kpos[None, :] <= qpos[:, None], s_own, NEG)
        scores = [s_own]
        for i in range(n_sel):
            k_g = gather_blocks(kb, idx[..., i])
            s = jnp.einsum('bhqd,bhqkd->bhqk', qc, k_g).astype(jnp.float32) * scale
            scores.append(jnp.where(valid[:, i][:, None], s, NEG))
        p = jax.nn.softmax(jnp.concatenate(scores, axis=-1), axis=-1).astype(v.dtype)
        out = jnp.einsum('bhqk,bhkd->bhqd', p[..., :MOBA_BLOCK], v_own)
        for i in range(n_sel):
            v_g = gather_blocks(vb, idx[..., i])
            p_i = p[..., MOBA_BLOCK * (i + 1):MOBA_BLOCK * (i + 2)]
            out = out + jnp.einsum('bhqk,bhqkd->bhqd', p_i, v_g)
        return out

    out = lax.map(chunk, jnp.arange(n_qc))
    return out.transpose(1, 2, 0, 3, 4).reshape(B, H, S, Dh)

def gla_attention(q, k, v, g):
    B, H, S, dk = q.shape
    dv = v.shape[-1]
    nc = S // GLA_CHUNK

    def to_chunks(t):
        return t.astype(jnp.float32).reshape(B, H, nc, GLA_CHUNK, t.shape[-1]).transpose(2, 0, 1, 3, 4)

    qc, kc, vc, gc = to_chunks(q * (dk ** -0.5)), to_chunks(k), to_chunks(v), to_chunks(g)
    causal = jnp.tril(jnp.ones((GLA_CHUNK, GLA_CHUNK), dtype=bool))[:, :, None]

    def step(state, inp):
        qi, ki, vi, gi = inp
        G = jnp.cumsum(gi, axis=2)
        diff = G[:, :, :, None, :] - G[:, :, None, :, :]
        decay = jnp.exp(jnp.where(causal, diff, -jnp.inf))
        A = jnp.einsum('bhid,bhjd,bhijd->bhij', qi, ki, decay)
        o = jnp.einsum('bhij,bhjv->bhiv', A, vi) + jnp.einsum('bhid,bhdv->bhiv', qi * jnp.exp(G), state)
        G_last = G[:, :, -1:, :]
        k_dec = ki * jnp.exp(G_last - G)
        state = state * jnp.exp(G_last[:, :, 0, :])[..., None] + jnp.einsum('bhjd,bhjv->bhdv', k_dec, vi)
        return state, o

    state0 = jnp.zeros((B, H, dk, dv), jnp.float32)
    _, o = lax.scan(step, state0, (qc, kc, vc, gc))
    return o.transpose(1, 2, 0, 3, 4).reshape(B, H, S, dv)

def conformer_conv(a, gate, w_dw, b_dw, g_ln, b_ln):
    u = a * jax.nn.sigmoid(gate)
    y = lax.conv_general_dilated(u, w_dw[:, None, :].astype(u.dtype), window_strides=(1,),
                                 padding=((CONV_WIDTH - 1, 0),),
                                 dimension_numbers=('NWC', 'WIO', 'NWC'),
                                 feature_group_count=CONV_CH) + b_dw
    return jax.nn.silu(layer_norm(y, g_ln, b_ln))

def hybrid_mixer(xn, cos, sin, w_in, b_gate, w_gla_a2, b_gla_a, g_gla_norm, w_dw, b_dw,
                 g_conv_ln, b_conv_ln, w_moba_o, w_gla_o, w_conv_o, w_mix_out):
    B, S, _ = xn.shape
    z = xn @ w_in
    points, acc = [], 0
    for s in IN_SIZES[:-1]:
        acc += s
        points.append(acc)
    mq, mk, mv, lq, lk, lv, la, lr, ca, cg, gates = jnp.split(z, points, axis=-1)

    def moba_heads(t, rot):
        t = t.reshape(B, S, MOBA_HEADS, MOBA_HEAD_DIM)
        t = apply_rope(t, cos, sin) if rot else t
        return t.transpose(0, 2, 1, 3)
    ya = moba_attention(moba_heads(mq, True), moba_heads(mk, True), moba_heads(mv, False))
    ya = ya.transpose(0, 2, 1, 3).reshape(B, S, MOBA_WIDTH) @ w_moba_o

    logdecay = jax.nn.log_sigmoid((la @ w_gla_a2 + b_gla_a).astype(jnp.float32)) / GLA_TEMP
    def gla_heads(t, d):
        return t.reshape(B, S, GLA_HEADS, d).transpose(0, 2, 1, 3)
    ob = gla_attention(gla_heads(lq, GLA_DK), gla_heads(lk, GLA_DK), gla_heads(lv, GLA_DV),
                       gla_heads(logdecay, GLA_DK))
    ob = ob.transpose(0, 2, 1, 3).astype(xn.dtype)
    ob = rms_norm(ob, g_gla_norm) * jax.nn.silu(lr.reshape(B, S, GLA_HEADS, GLA_DV))
    yb = ob.reshape(B, S, GLA_VW) @ w_gla_o

    yc = conformer_conv(ca, cg, w_dw, b_dw, g_conv_ln, b_conv_ln) @ w_conv_o

    g_a, g_b, g_c = jnp.split(jax.nn.sigmoid(gates + b_gate), N_BRANCH, axis=-1)
    return (g_a * ya + g_b * yb + g_c * yc) @ w_mix_out

def sq_relu_mlp(xn, w_up, w_down):
    return jnp.square(jax.nn.relu(xn @ w_up)) @ w_down

def setup_inputs(seed: int = 0) -> dict:
    key = jax.random.key(seed)
    ks = jax.random.split(key, 24)
    f32 = jnp.float32

    def nrm(k, shape, fan_in):
        return jax.random.normal(k, shape, f32) * (fan_in ** -0.5)

    def gain(k, shape):
        return 1.0 + 0.02 * jax.random.normal(k, shape, f32)

    def bias(k, shape, s):
        return s * jax.random.normal(k, shape, f32)

    L = DEPTH
    return {
        'x': jax.random.normal(ks[0], (BATCH, SEQ, D_MODEL), f32),
        'positions': jnp.broadcast_to(jnp.arange(SEQ, dtype=jnp.int32), (BATCH, SEQ)),
        'g_mix_pre': gain(ks[1], (L, D_MODEL)),
        'w_in': nrm(ks[2], (L, D_MODEL, IN_WIDTH), D_MODEL),
        'b_gate': bias(ks[3], (L, N_BRANCH * D_MODEL), 0.1),
        'w_gla_a2': nrm(ks[4], (L, GLA_RANK, GLA_KW), GLA_RANK),
        'b_gla_a': bias(ks[5], (L, GLA_KW), 0.1),
        'g_gla_norm': gain(ks[6], (L, GLA_DV)),
        'w_dw': nrm(ks[7], (L, CONV_WIDTH, CONV_CH), CONV_WIDTH),
        'b_dw': bias(ks[8], (L, CONV_CH), 0.02),
        'g_conv_ln': gain(ks[9], (L, CONV_CH)),
        'b_conv_ln': bias(ks[10], (L, CONV_CH), 0.02),
        'w_moba_o': nrm(ks[11], (L, MOBA_WIDTH, D_MODEL), MOBA_WIDTH),
        'w_gla_o': nrm(ks[12], (L, GLA_VW, D_MODEL), GLA_VW),
        'w_conv_o': nrm(ks[13], (L, CONV_CH, D_MODEL), CONV_CH),
        'w_mix_out': nrm(ks[14], (L, D_MODEL, D_MODEL), D_MODEL),
        'g_mix_post': gain(ks[15], (L, D_MODEL)),
        'g_mlp_pre': gain(ks[16], (L, D_MODEL)),
        'w_mlp_up': nrm(ks[17], (L, D_MODEL, D_FF), D_MODEL),
        'w_mlp_down': nrm(ks[18], (L, D_FF, D_MODEL), D_FF),
        'g_mlp_post': gain(ks[19], (L, D_MODEL)),
    }

def reference(x, positions, g_mix_pre, w_in, b_gate, w_gla_a2, b_gla_a, g_gla_norm, w_dw, b_dw,
              g_conv_ln, b_conv_ln, w_moba_o, w_gla_o, w_conv_o, w_mix_out, g_mix_post,
              g_mlp_pre, w_mlp_up, w_mlp_down, g_mlp_post):
    cos, sin = rope_tables(positions)
    h = x
    for l in range(DEPTH):
        y = hybrid_mixer(rms_norm(h, g_mix_pre[l]), cos, sin, w_in[l], b_gate[l], w_gla_a2[l],
                         b_gla_a[l], g_gla_norm[l], w_dw[l], b_dw[l], g_conv_ln[l], b_conv_ln[l],
                         w_moba_o[l], w_gla_o[l], w_conv_o[l], w_mix_out[l])
        h = h + rms_norm(y, g_mix_post[l])
        y = sq_relu_mlp(rms_norm(h, g_mlp_pre[l]), w_mlp_up[l], w_mlp_down[l])
        h = h + rms_norm(y, g_mlp_post[l])
    return h


_drawn_inputs = setup_inputs


def setup_inputs(seed=0):
    import zlib

    import numpy as np

    out = dict(_drawn_inputs(seed))
    spreads = {}
    factors = {'g_gla_norm': 14.829,
     'g_conv_ln': 12.802,
     'b_conv_ln': 13.503,
     'g_mlp_pre': 3.018,
     'g_mlp_post': 3.361,
     'g_mix_post': 2.84}
    for name, (base, spread) in spreads.items():
        noise = np.random.default_rng([zlib.crc32(name.encode()), seed]).standard_normal(out[name].shape)
        drawn = base * np.exp(spread * noise) if base else spread * noise
        out[name] = __import__('jax').numpy.asarray(drawn.astype(out[name].dtype))
    for name, factor in factors.items():
        out[name] = (out[name] * factor).astype(out[name].dtype)
    return out
```

```python
from contextlib import ExitStack

import concourse.bass as bass
from concourse import mybir

F32 = mybir.dt.float32
F32R = mybir.dt.float32r
I32 = mybir.dt.int32
ACT = mybir.ActivationFunctionType
ALU = mybir.AluOpType
AX = mybir.AxisListType

P = 128
D = 1024
S = 256
T = S // P
DEPTH = 2
KC = D // P
EPS = 1e-6
NEG = -1e30
HEADS = 8
DH = 64
PAIRS = HEADS // 2
GH = 4
GDK = 64
GDV = 128
RANK = 16
CHUNK = 64
CH = 512
CC = CH // P
TAPS = 31
FF = 4096
HALF = DH // 2
COLS = 512
RAW_SLOTS = 5
SPLIT_SLOTS = 4
LEAD = 3

C_Q, C_K, C_V = 0, 512, 1024
C_LQK, C_LV, C_LA, C_LR, C_CA, C_CG, C_GATES = 1536, 2048, 2560, 2576, 3088, 3600, 4112

PACKED = [("g_mix_pre", KC), ("g_mlp_pre", KC), ("b_gla", 2), ("g_ln", CC), ("b_ln", CC), ("b_dw", CC),
          ("w_dw", CC * TAPS)]
PACK_AT = {}
_at = 0
for _n, _w in PACKED:
    PACK_AT[_n] = _at
    _at += _w
PACK_W = _at

GROUPS = (
    [("ca", "w_in", C_CA, D, "act"), ("cg", "w_in", C_CG, D, "act"), ("lqk", "w_in", C_LQK, D, "act"),
     ("lv", "w_in", C_LV, D, "act"), ("mq", "w_in", C_Q, D, "act"), ("mk", "w_in", C_K, D, "act"),
     ("mv", "w_in", C_V, D, "act"), ("lr", "w_in", C_LR, D, "act")]
    + [g for b, w in enumerate(("w_moba_o", "w_gla_o", "w_conv_o"))
       for g in [(f"g{b}{c}", "w_in", C_GATES + b * D + c * COLS, D, "act") for c in range(2)]
       + [(f"w{b}{c}", w, c * COLS, CH, f"branch{b}") for c in range(2)]]
    + [(f"mo{c}", "w_mix_out", c * COLS, D, "act") for c in range(2)]
    + [(f"up{c}", "w_mlp_up", c * COLS, D, "act") for c in range(FF // COLS)]
    + [(f"dn{c}", "w_mlp_down", c * COLS, FF, "hid") for c in range(2)]
)
GROUP_NO = {g[0]: i for i, g in enumerate(GROUPS)}
STRIPS = []
for _g in GROUPS[:-2]:
    _n = _g[3] // 256
    STRIPS += [(_g[0], j, j == 0, j == _n - 1) for j in range(_n)]
for _j in range(FF // 256):
    STRIPS += [(f"dn{c}", _j, _j == 0, _j == FF // 256 - 1) for c in range(2)]
NS = len(STRIPS)
LAST_STRIP = {g: u for u, (g, j, first, last) in enumerate(STRIPS) if last}
assert NS % RAW_SLOTS == 0 and NS % SPLIT_SLOTS == 0 and len(GROUPS) % 2 == 0

LEVELS = [0, 32, 16, 8, 4, 2, 1]

JOBS_OF = {
    "xpose_pre": [f"xp{i}" for i in range(4)], "la": ["la"], "la_turn": ["laT"], "decay": ["dec0", "dec1"],
    "u_turn": ["uT0", "uT1"], "l_turn": ["lT0", "lT1"], "q_turn": ["qT0", "qT1"], "k_turn": ["kT0", "kT1"],
    "kd_turn": ["kdT"], "g_turn": ["gT0", "gT1"], "ln_mean": ["mu"], "ln_var": ["var"],
    "mix_turn": [f"mT{i}" for i in range(4)], "xpose_mlp": [f"xm{i}" for i in range(4)],
}
for _i in range(len(LEVELS)):
    JOBS_OF[f"level_mul{_i}"] = [f"lev{_i}_{hh}" for hh in range(2)]
for _i in range(3):
    JOBS_OF[f"state{_i}"] = [f"st{_i}"]
for _i in range(2):
    JOBS_OF[f"g_out{_i}"] = [f"go{_i}"]
for _i in range(PAIRS):
    JOBS_OF[f"scores{_i}"] = [f"s0_{_i}", f"s1_{_i}"]
    JOBS_OF[f"probs{_i}"] = [f"pa_{_i}", f"pb_{_i}"]
    JOBS_OF[f"values{_i}"] = [f"o_{_i}"]
for _i in range(8):
    JOBS_OF[f"hid_turn{_i}"] = [f"h0_{_i}", f"h1_{_i}"]

AFTER = {
    0: ["la"], 1: ["la_turn"], 2: ["decay"], 3: ["decay_b"],
    8: ["u_turn"], 12: ["l_turn", "scan"],
    13: ["level_mul0", "level_exp1"], 14: ["level_sel0", "level_mul1", "level_exp2"],
    15: ["level_sel1", "level_mul2", "level_exp3"], 16: ["level_sel2", "level_mul3", "level_exp4"],
    17: ["level_sel3", "level_mul4", "level_exp5"], 18: ["level_sel4", "level_mul5", "level_exp6"],
    19: ["level_sel5", "level_mul6"], 20: ["level_sel6"], 21: ["q_turn", "inter_exp"], 22: ["inter_mul"],
    23: ["kd_turn"], 24: ["state0"], 25: ["k_turn", "state1"], 26: ["state2"],
    28: ["scores0"], 29: ["probs0"], 30: ["values0", "scores1"], 31: ["probs1"],
    32: ["values1", "scores2"], 33: ["probs2", "g_out0", "g_out1"], 34: ["g_rstd", "g_scale", "values2", "scores3"],
    35: ["probs3"], 36: ["values3"], 37: ["g_turn"],
    60: ["ln_mean"], 62: ["ln_var"],
}

ROW_BLOCKS = [(0, 1), (3, 4), (1, 3), (4, 6)]


def build_plan():
    taps = list(range(TAPS))
    free = [9, 10, 11] + list(range(24, 28)) + [38, 39] + list(range(38, 60))
    spots = {}
    for i, k in enumerate(taps):
        spots.setdefault(free[min(i, len(free) - 1)], []).append(k)
    plan = ["pre_norm", "xpose_pre"]
    plan += [("split", u) for u in range(LEAD)]
    for u, (g, j, first, last) in enumerate(STRIPS):
        if g == "w20" and j == 0:
            plan.append("ln_out")
        if g == "mo0" and j == 0:
            plan.append("mix_turn")
        if g == "up0" and j == 0:
            plan += ["post_mix", "mlp_norm", "xpose_mlp"]
        if g == "dn0" and j == 0:
            plan.append("hid_turn7")
        plan.append(("strip", u))
        if u + LEAD < NS:
            plan.append(("split", u + LEAD))
        if last and not g.startswith(("mo", "dn")):
            plan.append(("evac", g))
        if g.startswith("up") and j == 0 and g != "up0":
            plan.append(f"hid_turn{int(g[2]) - 1}")
        plan += AFTER.get(u, [])
        plan += [("tap", k) for k in spots.get(u, [])]
    plan.append("post_mlp")
    return plan


PLAN = build_plan()
JOBS = [j for step in PLAN if isinstance(step, str) for j in JOBS_OF.get(step, [])]
assert len(set(JOBS)) == len(JOBS) == sum(len(v) for v in JOBS_OF.values())
JOB_BANKS = 4
JOBS_PER_BANK = len(JOBS) // JOB_BANKS
assert len(JOBS) % JOB_BANKS == 0, len(JOBS)
JOB_NO = {j: i for i, j in enumerate(JOBS)}


class Signal:

    def __init__(self, sem, per_layer, primed=0):
        self.sem, self.per_layer, self.primed = sem, per_layer, primed

    def at(self, layer, k):
        assert 1 <= k + self.primed
        return self.sem, layer * self.per_layer + (k + self.primed)


def trunk(nc, x, positions, inv_freq, packed, w_in, b_gate, w_a2, g_gla, w_moba_o, w_gla_o, w_conv_o,
          w_mix_out, g_mix_post, w_up, w_down, g_mlp_post, out):
    weights = {"w_in": w_in, "w_moba_o": w_moba_o, "w_gla_o": w_gla_o, "w_conv_o": w_conv_o,
               "w_mix_out": w_mix_out, "w_mlp_up": w_up, "w_mlp_down": w_down}
    ctx = ExitStack()
    with ctx:
        def sb(name, shape, dt=F32, where=ctx):
            return where.enter_context(nc.sbuf_tensor(name, shape, dt))

        def signal(name, per_layer, primed=0):
            return Signal(ctx.enter_context(nc.semaphore(name)), per_layer, primed)

        resid = sb("resid", [P, T, D])
        xs = sb("xs", [P, T, D])
        act_h = sb("act_h", [P, KC, S], F32R)
        act_l = sb("act_l", [P, KC, S], F32R)
        raw = sb("raw", [P, RAW_SLOTS, 2, COLS])
        w_h = sb("w_h", [P, SPLIT_SLOTS, 2, COLS], F32R)
        w_l = sb("w_l", [P, SPLIT_SLOTS, 2, COLS], F32R)
        pk = sb("pk", [P, PACK_W])
        a2 = sb("a2", [RANK, 2 * P])
        bg = sb("bg", [P, D])
        gpost = sb("gpost", [P, D])
        ggla = sb("ggla", [P, GDV])
        la_raw = sb("la_raw", [P, KC, RANK])
        la_h = sb("la_h", [P, KC, RANK], F32R)
        la_l = sb("la_l", [P, KC, RANK], F32R)
        la_nat = sb("la_nat", [P, T, RANK])
        laT = sb("laT", [RANK, S])
        ident = sb("ident", [P, P])
        over_ch = sb("over_ch", [P, P])
        causal = sb("causal", [P, 3, P])
        keep = sb("keep", [P, 2 * S])
        lmask = sb("lmask", [P, len(LEVELS), P], mybir.dt.int16)
        cos_t = sb("cos_t", [P, T, HALF])
        sin_t = sb("sin_t", [P, T, HALF])
        aT = sb("aT", [P, 2, 2 * T, P])
        tmp = sb("tmp", [P, T, COLS])
        stats = sb("stats", [P, 96])
        inv_f = sb("inv_f", [P, HALF])
        pos_i = sb("pos_i", [P, T], I32)
        pos_f = sb("pos_f", [P, T])
        rt = tmp[:].rearrange("p t n -> p (t n)")[:, 0:5 * T * HALF].rearrange("p (i t n) -> p i t n", i=5, t=T)
        mixers = ExitStack()
        qT = sb("qT", [P, PAIRS, S], where=mixers)
        kT = sb("kT", [P, PAIRS, S], where=mixers)
        v = sb("v", [P, T, COLS], where=mixers)
        pr = sb("pr", [P, 2, 6, P], where=mixers)
        prT = sb("prT", [P, 6, P], where=mixers)
        brT_h = [sb(f"br{i}_h", [P, CC, S], F32R, mixers) for i in range(2)]
        brT_l = [sb(f"br{i}_l", [P, CC, S], F32R, mixers) for i in range(2)]
        lqT = sb("lqT", [P, 2, S], where=mixers)
        lkT = sb("lkT", [P, 2, S], where=mixers)
        lv = sb("lv", [P, T, COLS], where=mixers)
        cum = sb("cum", [P, 2, S], where=mixers)
        ex = sb("ex", [P, 2, S], where=mixers)
        qs = sb("qs", [P, 2, 2, S], where=mixers)
        ks = sb("ks", [P, 2, 2, S], where=mixers)
        eG = sb("eG", [P, 2, S], where=mixers)
        qg = sb("qg", [P, 2, S], where=mixers)
        kdn = sb("kdn", [P, T, 2 * P], where=mixers)
        state = sb("state", [P, 3, 2, P], where=mixers)
        slr = sb("slr", [P, T, COLS], where=mixers)
        u_nat = sb("u_nat", [P, T, COLS], where=mixers)
        cgs = sb("cgs", [P, T, COLS], where=mixers)
        uT = sb("uT", [P, CC, TAPS - 1 + S], where=mixers)
        acc = sb("acc", [P, CC, S], where=mixers)
        gate = sb("gate", [P, T, D], where=mixers)
        mixers.close()
        hid_h = sb("hid_h", [P, FF // P, S], F32R)
        hid_l = sb("hid_l", [P, FF // P, S], F32R)
        hid = sb("hid", [P, 2, T, COLS])

        bank = [ctx.enter_context(nc.psum_tensor(f"bank{i}", [P, COLS], F32)) for i in range(8)]

        def param(name, i=0, n=1):
            return pk[:, PACK_AT[name] + i:PACK_AT[name] + i + n]

        decay = cgs[:, 0, :].rearrange("p (a s) -> p a s", a=2)
        decay_e = cgs[:, 1, :].rearrange("p (a s) -> p a s", a=2)
        square = u_nat[:, :, :].rearrange("p t n -> p (t n)").rearrange("p (c s) -> p c s", c=CC)
        var, rst, rsc = (cgs[:, i // 2, (i % 2) * S:(i % 2) * S + S] for i in range(3))

        x_in = signal("x_in", 0)
        pos_in = signal("pos_in", 0)
        freq_in = signal("freq_in", 0)
        raw_in = [signal(f"raw_in{i}", 16 * NS // RAW_SLOTS) for i in range(RAW_SLOTS)]
        strip_hi = signal("strip_hi", NS)
        strip_split = signal("strip_split", NS, RAW_SLOTS)
        strip_used = signal("strip_used", NS, SPLIT_SLOTS)
        acc_read = [signal(f"acc_read{i}", len(GROUPS) // 2, 1) for i in range(4)]
        job_done = [signal(f"job_done{i}", JOBS_PER_BANK) for i in range(JOB_BANKS)]
        job_read = [signal(f"job_read{i}", JOBS_PER_BANK, 1) for i in range(JOB_BANKS)]
        job_hi = signal("job_hi", 4 + 4 + 4 + 2 + PAIRS + 16)
        pk_in = signal("pk_in", 16)
        a2_in = signal("a2_in", 16)
        bg_in = signal("bg_in", 48)
        gpost_in = signal("gpost_in", 32)
        ggla_in = signal("ggla_in", 16)
        la_in = signal("la_in", 16)
        consts = signal("consts", 0)
        pool_steps = signal("pool_steps", 0)
        angles = signal("angles", 0)
        rope_in = signal("rope_in", 0)
        setup_v = signal("setup_v", 0)
        passed = signal("passed", 0)
        layer_in = signal("layer_in", 1)
        squares = signal("squares", 2 * T)
        xs_in = signal("xs_in", 2)
        la_hi = signal("la_hi", 1)
        la_split = signal("la_split", 1)
        decay_exp = signal("decay_exp", 3)
        cg_sig = signal("cg_sig", 1)
        u_in = signal("u_in", 1)
        rope_out = signal("rope_out", 2)
        expo = signal("expo", 7)
        expd = signal("expd", 7)
        cum_in = signal("cum_in", 1)
        eg_in = signal("eg_in", 1)
        scaled = signal("scaled", 7)
        state_in = signal("state_in", 3)
        p_in = signal("p_in", PAIRS)
        p_exp = signal("p_exp", PAIRS)
        p_norm = signal("p_norm", PAIRS)
        g_squares = signal("g_squares", T)
        lr_sig = signal("lr_sig", T)
        g_ready = signal("g_ready", 1)
        gate_in = signal("gate_in", 6)
        gate_sig = signal("gate_sig", 6)
        mix_in = signal("mix_in", 1)
        taps_in = signal("taps_in", 1)
        centred = signal("centred", 1)
        ch_sq = signal("ch_sq", 1)
        ln_in = signal("ln_in", 1)
        ln_sig = signal("ln_sig", 1)
        silu_in = signal("silu_in", 1)
        conv_hi = signal("conv_hi", 1)
        conv_split = signal("conv_split", 1)
        y_squares = signal("y_squares", 2)
        resid_in = signal("resid_in", 2)
        hid_sq = signal("hid_sq", 8)
        out_in = signal("out_in", 0)
        V_STEPS, A_STEPS = 420, 20
        v_steps = signal("v_steps", V_STEPS)
        a_steps = signal("a_steps", A_STEPS)

        def job_bank(job):
            return JOB_NO[job] % JOB_BANKS

        def job_ps(job):
            return bank[4 + job_bank(job)]

        def job_k(job):
            return JOB_NO[job] // JOB_BANKS + 1

        def group_bank(g, t):
            return 2 * (GROUP_NO[g] % 2) + t

        def group_ps(g, t):
            return bank[group_bank(g, t)]

        def group_k(g):
            return GROUP_NO[g] // 2 + 1

        def heads(ap, n):
            return ap.rearrange("p (h n) -> p h n", h=n)

        block = ctx.enter_context(nc.Block())

        @block.sync
        def _(sp):
            sp.dma_start(resid[:], x.rearrange("b (t p) d -> p (b t) d", p=P)).then_inc(x_in.sem, 16)
            with sp.Fori(0, DEPTH) as l:
                for u, (g, j, first, last) in enumerate(STRIPS):
                    _, w, c0, _, _ = GROUPS[GROUP_NO[g]]
                    sp.wait_ge(*strip_split.at(l, u + 1 - RAW_SLOTS))
                    sp.sem_inc(passed.sem, 1)
                    src = weights[w][bass.ds(l, 1), 256 * j:256 * j + 256, c0:c0 + COLS]
                    sp.dma_start(raw[:, u % RAW_SLOTS], src.rearrange("l (c p) n -> p (l c) n", p=P))\
                        .then_inc(raw_in[u % RAW_SLOTS].sem, 16)
            sp.wait_ge(*resid_in.at(DEPTH - 1, 2))
            sp.dma_start(out.rearrange("b (t p) d -> p (b t) d", p=P), resid[:]).then_inc(out_in.sem, 16)
            sp.wait_ge(out_in.sem, 16)

        @block.gpsimd
        def _(pool):
            pool.dma_start(inv_f[:], inv_freq).then_inc(freq_in.sem, 16)
            pool.dma_start(pos_i[:], positions).then_inc(pos_in.sem, 16)

            def load(l, first):
                if not first:
                    pool.wait_ge(*la_split.at(l - 1, 1))
                pool.dma_start(la_raw[:], w_in[bass.ds(l, 1), :, C_LA:C_LA + RANK]
                               .rearrange("l (c p) n -> p (l c) n", p=P)).then_inc(la_in.sem, 16)
                if not first:
                    for j in JOBS_OF["xpose_mlp"]:
                        pool.wait_ge(*job_read[job_bank(j)].at(l - 1, job_k(j)))
                pool.dma_start(pk[:], packed[bass.ds(l, 1)].rearrange("l p n -> p (l n)")).then_inc(pk_in.sem, 16)
                pool.dma_start(a2[:], w_a2[bass.ds(l, 1)].rearrange("l r n -> r (l n)")).then_inc(a2_in.sem, 16)
                pool.dma_start(ggla[:], g_gla[bass.ds(l, 1), :].partition_broadcast(P)).then_inc(ggla_in.sem, 16)
                for b in range(3):
                    if b:
                        for t in range(T):
                            pool.wait_ge(*acc_read[group_bank(f"g{b-1}1", t)].at(l, group_k(f"g{b-1}1")))
                    pool.dma_start(bg[:], b_gate[bass.ds(l, 1), b * D:(b + 1) * D].partition_broadcast(P))\
                        .then_inc(bg_in.sem, 16)
                    if b == 0:
                        if not first:
                            pool.wait_ge(*resid_in.at(l - 1, 2))
                        pool.dma_start(gpost[:], g_mix_post[bass.ds(l, 1), :].partition_broadcast(P))\
                            .then_inc(gpost_in.sem, 16)
                pool.wait_ge(*resid_in.at(l, 1))
                pool.dma_start(gpost[:], g_mlp_post[bass.ds(l, 1), :].partition_broadcast(P))\
                    .then_inc(gpost_in.sem, 16)

            steps = 0

            def own(ins):
                nonlocal steps
                ins.then_inc(pool_steps.sem, 1)
                steps += 1
                pool.wait_ge(pool_steps.sem, steps)

            own(pool.memset(ident[:], 0.0))
            own(pool.affine_select(out=ident[:], in_=ident[:], compare_op=ALU.not_equal, fill=1.0, base=0,
                                   pattern=[[-1, P]], channel_multiplier=1))
            own(pool.memset(over_ch[:], 1.0 / CH))
            own(pool.memset(causal[:], 0.0))
            for i in (0, 2):
                own(pool.affine_select(out=causal[:, i, :], in_=causal[:, i, :], compare_op=ALU.is_ge, fill=NEG,
                                       base=0, pattern=[[-1, P]], channel_multiplier=1))
            own(pool.memset(keep[:], 1.0))
            own(pool.memset(heads(keep[:], 2 * S // CHUNK)[:, :, 0:1], 0.0))
            own(pool.memset(aT[:], 0.0))
            own(pool.memset(uT[:, :, 0:TAPS - 1], 0.0))
            own(pool.memset(lmask[:], 1))
            for n, s in enumerate(LEVELS):
                if s == 0:
                    own(pool.affine_select(out=lmask[:, n, :], in_=lmask[:, n, :], compare_op=ALU.is_equal,
                                           fill=0.0, base=0, pattern=[[-1, P]], channel_multiplier=1))
                    continue
                m = lmask[:, n, :].rearrange("p (b h s) -> p b h s", h=2, s=s)
                own(pool.memset(m[:, :, 0, :], 0))
                own(pool.affine_select(out=m[:, :, 1, :], in_=m[:, :, 1, :], compare_op=ALU.is_ge, fill=0.0,
                                       base=0, pattern=[[-2 * s, P // (2 * s)], [0, s]], channel_multiplier=1))
                own(pool.affine_select(out=m[:, :, 1, :], in_=m[:, :, 1, :], compare_op=ALU.is_ge, fill=0.0,
                                       base=s - 1, pattern=[[2 * s, P // (2 * s)], [0, s]],
                                       channel_multiplier=-1))
            pool.sem_inc(consts.sem, 1)
            load(0, True)
            with pool.Fori(1, DEPTH) as l:
                load(l, False)

        @block.scalar
        def _(act):
            act.sem_inc(strip_used.sem, SPLIT_SLOTS)
            act.wait_ge(angles.sem, 1)
            act.activation(cos_t[:], cos_t[:], ACT.Sin).then_inc(rope_in.sem, 1)
            act.activation(sin_t[:], sin_t[:], ACT.Sin).then_inc(rope_in.sem, 1)
            act.wait_ge(x_in.sem, 16)
            act.wait_ge(consts.sem, 1)

            with act.Fori(0, DEPTH) as l:
                a_count = 0
                hi_count = 0

                def job_wait(job):
                    act.wait_ge(*job_done[job_bank(job)].at(l, job_k(job)))

                def group_wait(g):
                    act.wait_ge(*strip_used.at(l, LAST_STRIP[g] + 1))

                def own(ins):
                    nonlocal a_count
                    ins.then_inc(a_steps.sem, 1)
                    a_count += 1
                    act.wait_ge(*a_steps.at(l, a_count))

                def row_squares(src, dst):
                    return act.activation(tmp[:].rearrange("p t n -> p (t n)")[:, 0:src.shape[-1]], src,
                                          ACT.Square, accum_out=dst)

                def turn_hi(jobs, dst, gains=None):
                    for i, job in enumerate(jobs):
                        job_wait(job)
                        if gains is None:
                            act.activation(dst[:, 2 * i:2 * i + 2, :], heads(job_ps(job)[:], 2), ACT.Copy)\
                                .then_inc(job_hi.sem, 1)
                        else:
                            for c in range(2):
                                last = act.activation(dst[:, 2 * i + c, :], job_ps(job)[:, c * S:c * S + S],
                                                      ACT.Copy, scale=param(gains, 2 * i + c))
                            last.then_inc(job_hi.sem, 1)

                for step in PLAN:
                    kind, arg = step if isinstance(step, tuple) else (step, None)
                    if kind == "split":
                        act.wait_ge(*raw_in[arg % RAW_SLOTS].at(l, 16 * (arg // RAW_SLOTS + 1)))
                        act.wait_ge(*strip_used.at(l, arg + 1 - SPLIT_SLOTS))
                        act.activation(w_h[:, arg % SPLIT_SLOTS], raw[:, arg % RAW_SLOTS], ACT.Copy)\
                            .then_inc(strip_hi.sem, 1)
                    elif kind == "evac":
                        g = arg
                        group_wait(g)
                        if g in ("ca", "lqk", "lv", "mv"):
                            dst = {"ca": u_nat, "lqk": u_nat, "lv": lv, "mv": v}[g]
                            for t in range(T):
                                act.activation(dst[:, t, :], group_ps(g, t)[:], ACT.Copy)\
                                    .then_inc(acc_read[group_bank(g, t)].sem, 1)
                        elif g == "cg":
                            for t in range(T):
                                act.activation(cgs[:, t, :], group_ps(g, t)[:], ACT.Sigmoid)\
                                    .then_inc(acc_read[group_bank(g, t)].sem, 1)
                        elif g == "lr":
                            for t in range(T):
                                act.activation(slr[:, t, :], group_ps(g, t)[:], ACT.Sigmoid)\
                                    .then_inc(lr_sig.sem, 1)
                        elif g[0] == "g":
                            n = 2 * int(g[1]) + int(g[2])
                            c = int(g[2]) * COLS
                            act.wait_ge(*gate_in.at(l, n + 1))
                            act.activation(gate[:, :, c:c + COLS], gate[:, :, c:c + COLS], ACT.Sigmoid)\
                                .then_inc(gate_sig.sem, 1)
                        elif g.startswith("up"):
                            n = int(g[2])
                            for t in range(T):
                                act.activation(hid[:, n % 2, t, :], group_ps(g, t)[:], ACT.Relu)\
                                    .then_inc(acc_read[group_bank(g, t)].sem, 1)
                    elif kind in ("pre_norm", "mlp_norm"):
                        n = 0 if kind == "pre_norm" else 1
                        if n:
                            act.wait_ge(*resid_in.at(l, 1))
                        else:
                            act.wait_ge(layer_in.sem, l + 1)
                        for t in range(T):
                            row_squares(resid[:, t, :], stats[:, t:t + 1]).then_inc(squares.sem, 1)
                            act.wait_ge(*squares.at(l, T * n + t + 1))
                    elif kind == "xpose_pre":
                        act.wait_ge(*pk_in.at(l, 16))
                        turn_hi(JOBS_OF[kind], act_h, "g_mix_pre")
                    elif kind == "xpose_mlp":
                        turn_hi(JOBS_OF[kind], act_h, "g_mlp_pre")
                    elif kind == "mix_turn":
                        turn_hi(JOBS_OF[kind], act_h)
                    elif kind == "la":
                        act.wait_ge(*la_in.at(l, 16))
                        act.activation(la_h[:], la_raw[:], ACT.Copy).then_inc(la_hi.sem, 1)
                        job_wait("la")
                        act.activation(la_nat[:].rearrange("p t r -> p (t r)"), job_ps("la")[:, 0:T * RANK],
                                       ACT.Copy).then_inc(job_read[job_bank("la")].sem, 1)
                    elif kind == "la_turn":
                        job_wait("laT")
                        act.activation(laT[:], job_ps("laT")[0:RANK, 0:S], ACT.Copy)\
                            .then_inc(job_read[job_bank("laT")].sem, 1)
                    elif kind == "decay_b":
                        for i in range(2):
                            act.wait_ge(*job_read[job_bank(f"dec{i}")].at(l, job_k(f"dec{i}")))
                        act.activation(decay_e, decay, ACT.Abs).then_inc(decay_exp.sem, 1)
                        act.wait_ge(*decay_exp.at(l, 1))
                        act.activation(decay_e, decay_e, ACT.Exp, scale=-1.0).then_inc(decay_exp.sem, 1)
                        act.wait_ge(*decay_exp.at(l, 2))
                        act.activation(decay_e, decay_e, ACT.Ln, bias=1.0).then_inc(decay_exp.sem, 1)
                    elif kind == "u_turn":
                        for i, job in enumerate(JOBS_OF[kind]):
                            job_wait(job)
                            act.activation(uT[:, 2 * i:2 * i + 2, TAPS - 1:], heads(job_ps(job)[:], 2), ACT.Copy)\
                                .then_inc(job_read[job_bank(job)].sem, 1)
                    elif kind == "l_turn":
                        job_wait("lT0")
                        act.activation(lqT[:], heads(job_ps("lT0")[:], 2), ACT.Copy, scale=GDK ** -0.5)\
                            .then_inc(job_read[job_bank("lT0")].sem, 1)
                        job_wait("lT1")
                        act.activation(lkT[:], heads(job_ps("lT1")[:], 2), ACT.Copy)\
                            .then_inc(job_read[job_bank("lT1")].sem, 1)
                    elif kind.startswith("level_exp"):
                        n = int(kind[9:])
                        act.wait_ge(*expo.at(l, n))
                        act.activation(ex[:], ex[:], ACT.Exp, scale=1.0 / 16.0).then_inc(expd.sem, 1)
                    elif kind == "inter_exp":
                        act.wait_ge(*cum_in.at(l, 1))
                        act.activation(eG[:], cum[:], ACT.Exp, scale=1.0 / 16.0).then_inc(eg_in.sem, 1)
                        act.wait_ge(*expo.at(l, 7))
                        act.activation(ex[:], ex[:], ACT.Exp, scale=1.0 / 16.0).then_inc(expd.sem, 1)
                    elif kind in ("q_turn", "k_turn"):
                        dst = qT if kind == "q_turn" else kT
                        for i, job in enumerate(JOBS_OF[kind]):
                            job_wait(job)
                            act.activation(dst[:, 2 * i:2 * i + 2, :], heads(job_ps(job)[:], 2), ACT.Copy)\
                                .then_inc(job_read[job_bank(job)].sem, 1)
                    elif kind == "kd_turn":
                        job_wait("kdT")
                        act.activation(kdn[:], heads(job_ps("kdT")[:], T), ACT.Copy)\
                            .then_inc(job_read[job_bank("kdT")].sem, 1)
                    elif kind.startswith("g_out"):
                        hh = int(kind[5:])
                        job_wait(f"go{hh}")
                        for i in range(2 * T):
                            last = act.activation(tmp[:, hh, i * GDV:(i + 1) * GDV],
                                                  job_ps(f"go{hh}")[:, i * GDV:(i + 1) * GDV], ACT.Square,
                                                  accum_out=stats[:, 16 + 4 * hh + i:17 + 4 * hh + i])
                        last.then_inc(g_squares.sem, 1)
                    elif kind == "g_turn":
                        turn_hi(JOBS_OF[kind], brT_h[1])
                    elif kind.startswith("scores"):
                        p = int(kind[6:])
                        act.wait_ge(*p_in.at(l, p + 1))
                        for i, (lo, hi) in enumerate(ROW_BLOCKS):
                            last = act.activation(pr[:, p % 2, lo:hi, :], pr[:, p % 2, lo:hi, :], ACT.Exp,
                                                  bias=stats[:, 40 + 4 * (p % 2) + i:41 + 4 * (p % 2) + i],
                                                  scale=DH ** -0.5,
                                                  accum_out=stats[:, 48 + 4 * (p % 2) + i:49 + 4 * (p % 2) + i])
                        last.then_inc(p_exp.sem, 1)
                    elif kind.startswith("probs"):
                        p = int(kind[5:])
                        for job, lo, hi in ((f"pa_{p}", 0, 4), (f"pb_{p}", 4, 6)):
                            job_wait(job)
                            act.activation(prT[:, lo:hi, :], heads(job_ps(job)[:, 0:(hi - lo) * P], hi - lo),
                                           ACT.Copy).then_inc(job_read[job_bank(job)].sem, 1)
                    elif kind.startswith("values"):
                        p = int(kind[6:])
                        job_wait(f"o_{p}")
                        act.activation(brT_h[0][:, p, :], job_ps(f"o_{p}")[:, 0:S], ACT.Copy)\
                            .then_inc(job_hi.sem, 1)
                    elif kind == "ln_var":
                        act.wait_ge(*centred.at(l, 1))
                        act.activation(square, acc[:], ACT.Square).then_inc(ch_sq.sem, 1)
                    elif kind == "ln_out":
                        act.wait_ge(*ln_in.at(l, 1))
                        for c in range(CC):
                            last = act.activation(acc[:, c, :], acc[:, c, :], ACT.Identity,
                                                  scale=param("g_ln", c), bias=param("b_ln", c))
                        own(last)
                        act.activation(square, acc[:], ACT.Sigmoid).then_inc(ln_sig.sem, 1)
                        act.wait_ge(*silu_in.at(l, 1))
                        act.wait_ge(*strip_used.at(l, LAST_STRIP["w01"] + 1))
                        act.activation(brT_h[0][:], acc[:], ACT.Copy).then_inc(conv_hi.sem, 1)
                    elif kind in ("post_mix", "post_mlp"):
                        a, b = ("mo0", "mo1") if kind == "post_mix" else ("dn0", "dn1")
                        group_wait(b)
                        for c, g in enumerate((a, b)):
                            for t in range(T):
                                last = row_squares(group_ps(g, t)[:], stats[:, 4 + 2 * t + c:5 + 2 * t + c])
                                if (c, t) != (1, T - 1):
                                    own(last)
                        last.then_inc(y_squares.sem, 1)
                    elif kind.startswith("hid_turn"):
                        n = int(kind[8:])
                        turn_hi(JOBS_OF[kind], hid_h[:, 4 * n:4 * n + 4])
                act.wait_ge(*a_steps.at(l, a_count))
                act.sem_inc(a_steps.sem, A_STEPS - a_count)

        @block.vector
        def _(dve):
            dve.sem_inc(strip_split.sem, RAW_SLOTS)
            for i in range(4):
                dve.sem_inc(acc_read[i].sem, 1)
                dve.sem_inc(job_read[i].sem, 1)

            n_setup = 0

            def own(ins):
                nonlocal n_setup
                ins.then_inc(setup_v.sem, 1)
                n_setup += 1
                dve.wait_ge(setup_v.sem, n_setup)

            TWO_PI = 6.283185307179586
            SMALL = 710.0 - 113 * TWO_PI
            ROUND = 12582912.0
            C1 = 6.28125
            C2 = 0.0019350051879882812
            C3 = TWO_PI - C1 - C2
            LIMIT = 3.1415925
            dve.wait_ge(freq_in.sem, 16)
            dve.wait_ge(pos_in.sem, 16)
            own(dve.tensor_copy(pos_f[:], pos_i[:]))
            ang, k0, k1, kk, off = (rt[:, i] for i in range(5))
            for t in range(T):
                own(dve.tensor_scalar(ang[:, t, :], inv_f[:], pos_f[:, t:t + 1], None, ALU.mult))
            big = 710.0 * 4096
            own(dve.tensor_scalar(k0, ang, 1.0 / big, ROUND, ALU.mult, ALU.add))
            own(dve.tensor_scalar(k0, k0, ROUND, None, ALU.subtract))
            own(dve.scalar_tensor_tensor(out=ang, in0=k0, scalar=-big, in1=ang, op0=ALU.mult, op1=ALU.add))
            own(dve.tensor_scalar(k1, ang, 1.0 / 710.0, ROUND, ALU.mult, ALU.add))
            own(dve.tensor_scalar(k1, k1, ROUND, None, ALU.subtract))
            own(dve.scalar_tensor_tensor(out=ang, in0=k1, scalar=-710.0, in1=ang, op0=ALU.mult, op1=ALU.add))
            own(dve.scalar_tensor_tensor(out=kk, in0=k0, scalar=4096.0, in1=k1, op0=ALU.mult, op1=ALU.add))
            own(dve.tensor_scalar(kk, kk, SMALL, None, ALU.mult))
            own(dve.tensor_tensor(k1, ang, kk, ALU.add))
            for dst, turn, shift in ((sin_t, 0.0, 0.0), (cos_t, 0.25, TWO_PI / 4)):
                own(dve.tensor_scalar(k0, k1, 1.0 / TWO_PI, turn, ALU.mult, ALU.add))
                own(dve.tensor_scalar(k0, k0, ROUND, ROUND, ALU.add, ALU.subtract))
                own(dve.scalar_tensor_tensor(out=off, in0=k0, scalar=-C1, in1=ang, op0=ALU.mult, op1=ALU.add))
                own(dve.scalar_tensor_tensor(out=off, in0=k0, scalar=-C2, in1=off, op0=ALU.mult, op1=ALU.add))
                own(dve.scalar_tensor_tensor(out=off, in0=k0, scalar=-C3, in1=off, op0=ALU.mult, op1=ALU.add))
                own(dve.tensor_tensor(off, off, kk, ALU.add))
                own(dve.tensor_scalar(off, off, shift, LIMIT, ALU.add, ALU.min))
                own(dve.tensor_scalar(dst[:], off, -LIMIT, None, ALU.max))
            dve.sem_inc(angles.sem, 1)
            dve.wait_ge(x_in.sem, 16)
            dve.wait_ge(consts.sem, 1)
            dve.wait_ge(rope_in.sem, 2)
            dve.sem_inc(layer_in.sem, 1)

            with dve.Fori(0, DEPTH) as l:
                count = 0
                hi_count = 0

                def step_done(ins):
                    nonlocal count
                    ins.then_inc(v_steps.sem, 1)
                    count += 1
                    return count

                def after(k):
                    dve.wait_ge(*v_steps.at(l, k))

                def chain(ins):
                    after(step_done(ins))

                def job_wait(job):
                    dve.wait_ge(*job_done[job_bank(job)].at(l, job_k(job)))

                def group_wait(g):
                    dve.wait_ge(*strip_used.at(l, LAST_STRIP[g] + 1))

                def rsqrt(v_, y, s_):
                    chain(dve.tensor_scalar(y.bitcast(I32), v_.bitcast(I32), -0.5, 1597463007.0,
                                            ALU.mult, ALU.add))
                    for _ in range(3):
                        chain(dve.scalar_tensor_tensor(out=s_, in0=v_, scalar=-0.5, in1=y, op0=ALU.mult,
                                                       op1=ALU.mult))
                        chain(dve.tensor_tensor(s_, s_, y, ALU.mult))
                        chain(dve.scalar_tensor_tensor(out=y, in0=s_, scalar=1.5, in1=y, op0=ALU.add,
                                                       op1=ALU.mult))

                def turn_lo(jobs, hi, lo, gains=None):
                    nonlocal hi_count
                    for i, job in enumerate(jobs):
                        hi_count += 1
                        dve.wait_ge(*job_hi.at(l, hi_count))
                        if gains is None:
                            last = dve.tensor_tensor(lo[:, 2 * i:2 * i + 2, :], heads(job_ps(job)[:], 2),
                                                     hi[:, 2 * i:2 * i + 2, :].bitcast(F32), ALU.subtract)
                        else:
                            for c in range(2):
                                last = dve.scalar_tensor_tensor(
                                    out=lo[:, 2 * i + c, :], in0=job_ps(job)[:, c * S:c * S + S],
                                    scalar=param(gains, 2 * i + c), in1=hi[:, 2 * i + c, :].bitcast(F32),
                                    op0=ALU.mult, op1=ALU.subtract)
                        last.then_inc(job_read[job_bank(job)].sem, 1)

                for step in PLAN:
                    kind, arg = step if isinstance(step, tuple) else (step, None)
                    if kind == "split":
                        dve.wait_ge(*strip_hi.at(l, arg + 1))
                        dve.tensor_tensor(w_l[:, arg % SPLIT_SLOTS], raw[:, arg % RAW_SLOTS],
                                          w_h[:, arg % SPLIT_SLOTS].bitcast(F32), ALU.subtract)\
                            .then_inc(strip_split.sem, 1)
                    elif kind == "evac":
                        g = arg
                        if g == "cg":
                            for t in range(T):
                                dve.wait_ge(*acc_read[group_bank("ca", t)].at(l, group_k("ca")))
                                dve.wait_ge(*acc_read[group_bank("cg", t)].at(l, group_k("cg")))
                            dve.tensor_tensor(u_nat[:], u_nat[:], cgs[:], ALU.mult).then_inc(u_in.sem, 1)
                        elif g in ("mq", "mk"):
                            group_wait(g)
                            at = 0 if g == "mq" else 512
                            for t in range(T):
                                src = heads(group_ps(g, t)[:], 2 * HEADS)
                                c_b = cos_t[:, t:t + 1, :].to_broadcast([P, 2 * HEADS, HALF])
                                s_b = sin_t[:, t:t + 1, :].to_broadcast([P, 2 * HEADS, HALF])
                                xc = tmp[:, 0, :]
                                xn = tmp[:, 1, :]
                                if t:
                                    after(count)
                                elif g == "mk":
                                    dve.wait_ge(*rope_out.at(l, 1))
                                step_done(dve.tensor_tensor(heads(xc, 2 * HEADS), src, c_b, ALU.mult))
                                dve.tensor_tensor(heads(xn, 2 * HEADS), src, s_b, ALU.mult)\
                                    .then_inc(acc_read[group_bank(g, t)].sem, 1)
                                after(count)
                                dve.wait_ge(*acc_read[group_bank(g, t)].at(l, group_k(g)))
                                xc4 = xc.rearrange("p (h two n) -> p h two n", two=2, n=HALF)
                                xn4 = xn.rearrange("p (h two n) -> p h two n", two=2, n=HALF)
                                dst = xs[:, t, at:at + 512].rearrange("p (h two n) -> p h two n", two=2, n=HALF)
                                dve.tensor_tensor(dst[:, :, 0, :], xc4[:, :, 0, :], xn4[:, :, 1, :], ALU.subtract)
                                last = dve.tensor_tensor(dst[:, :, 1, :], xc4[:, :, 1, :], xn4[:, :, 0, :],
                                                         ALU.add)
                                if t == 0:
                                    step_done(last)
                            last.then_inc(rope_out.sem, 1)
                        elif g == "lr":
                            for t in range(T):
                                dve.wait_ge(*lr_sig.at(l, t + 1))
                                dve.tensor_tensor(slr[:, t, :], slr[:, t, :], group_ps(g, t)[:], ALU.mult)\
                                    .then_inc(acc_read[group_bank(g, t)].sem, 1)
                            if True:
                                dve.wait_ge(*ggla_in.at(l, 16))
                                for t in range(T):
                                    dve.wait_ge(*acc_read[group_bank(g, t)].at(l, group_k(g)))
                                    step_done(dve.tensor_tensor(
                                        heads(slr[:, t, :], GH), heads(slr[:, t, :], GH),
                                        ggla[:, :].rearrange("p (a n) -> p a n", a=1).to_broadcast([P, GH, GDV]),
                                        ALU.mult))
                        elif g[0] == "g":
                            b, c = int(g[1]), int(g[2])
                            group_wait(g)
                            dve.wait_ge(*bg_in.at(l, 16 * (b + 1)))
                            for t in range(T):
                                last = dve.tensor_tensor(gate[:, t, c * COLS:(c + 1) * COLS], group_ps(g, t)[:],
                                                         bg[:, c * COLS:(c + 1) * COLS], ALU.add)
                                last.then_inc(acc_read[group_bank(g, t)].sem, 1)
                            for t in range(T):
                                dve.wait_ge(*acc_read[group_bank(g, t)].at(l, group_k(g)))
                            dve.sem_inc(gate_in.sem, 1)
                        elif g[0] == "w":
                            b, c = int(g[1]), int(g[2])
                            group_wait(g)
                            dve.wait_ge(*gate_sig.at(l, 2 * b + c + 1))
                            for t in range(T):
                                gt = gate[:, t, c * COLS:(c + 1) * COLS]
                                mix = xs[:, t, c * COLS:(c + 1) * COLS]
                                dve.tensor_tensor(mix if b == 0 else tmp[:, t, :], group_ps(g, t)[:], gt,
                                                  ALU.mult).then_inc(acc_read[group_bank(g, t)].sem, 1)
                            for t in range(T):
                                mix = xs[:, t, c * COLS:(c + 1) * COLS]
                                dve.wait_ge(*acc_read[group_bank(g, t)].at(l, group_k(g)))
                                if b:
                                    last = dve.tensor_tensor(mix, mix, tmp[:, t, :], ALU.add)
                                    if b == 2 and c == 1 and t == T - 1:
                                        last.then_inc(mix_in.sem, 1)
                                    else:
                                        chain(last)
                        elif g.startswith("up"):
                            n = int(g[2])
                            for t in range(T):
                                dve.wait_ge(*acc_read[group_bank(g, t)].at(l, group_k(g)))
                            dve.tensor_tensor(hid[:, n % 2], hid[:, n % 2], hid[:, n % 2], ALU.mult)\
                                .then_inc(hid_sq.sem, 1)
                    elif kind in ("pre_norm", "mlp_norm"):
                        n = 0 if kind == "pre_norm" else 1
                        dve.wait_ge(*squares.at(l, T * (n + 1)))
                        chain(dve.tensor_scalar(stats[:, 8:10], stats[:, 0:2], 1.0 / D, EPS, ALU.mult, ALU.add))
                        rsqrt(stats[:, 8:10], stats[:, 10:12], stats[:, 12:14])
                        for t in range(T):
                            last = dve.tensor_scalar(xs[:, t, :], resid[:, t, :], stats[:, 10 + t:11 + t], None,
                                                     ALU.mult)
                        last.then_inc(xs_in.sem, 1)
                    elif kind == "xpose_pre":
                        dve.wait_ge(*pk_in.at(l, 16))
                        turn_lo(JOBS_OF[kind], act_h, act_l, "g_mix_pre")
                    elif kind == "xpose_mlp":
                        turn_lo(JOBS_OF[kind], act_h, act_l, "g_mlp_pre")
                    elif kind == "mix_turn":
                        turn_lo(JOBS_OF[kind], act_h, act_l)
                    elif kind == "la":
                        dve.wait_ge(*la_hi.at(l, 1))
                        dve.tensor_tensor(la_l[:], la_raw[:], la_h[:].bitcast(F32), ALU.subtract)\
                            .then_inc(la_split.sem, 1)
                    elif kind == "decay":
                        for i in range(2):
                            job = f"dec{i}"
                            job_wait(job)
                            dve.tensor_scalar(decay[:, i, :], job_ps(job)[:, 0:S], param("b_gla", i), None, ALU.add)\
                                .then_inc(job_read[job_bank(job)].sem, 1)
                    elif kind == "decay_b":
                        dve.wait_ge(*decay_exp.at(l, 3))
                        step_done(dve.scalar_tensor_tensor(out=ex[:], in0=decay, scalar=0.0, in1=decay_e,
                                                           op0=ALU.min, op1=ALU.subtract))
                        after(count)
                        dve.tensor_tensor_scan(cum[:].rearrange("p a s -> p (a s)"), keep[:],
                                               ex[:].rearrange("p a s -> p (a s)"), 0.0, ALU.mult, ALU.add)\
                            .then_inc(cum_in.sem, 1)
                        dve.wait_ge(*cum_in.at(l, 1))
                    elif kind == "scan":
                        pass
                    elif kind.startswith("level_exp"):
                        n = int(kind[9:])
                        s = LEVELS[n]
                        g4 = cum[:].rearrange("p a (b h s) -> p (a b) h s", h=2, s=s)
                        e4 = ex[:].rearrange("p a (b h s) -> p (a b) h s", h=2, s=s)
                        if n > 1:
                            dve.wait_ge(*scaled.at(l, n - 1))
                        ref = g4[:, :, 0, s - 1:s].broadcast_to([P, 2 * S // (2 * s), s])
                        dve.tensor_tensor(e4[:, :, 0, :], ref, g4[:, :, 0, :], ALU.subtract)
                        dve.tensor_tensor(e4[:, :, 1, :], g4[:, :, 1, :], ref, ALU.subtract).then_inc(expo.sem, 1)
                    elif kind.startswith("level_mul"):
                        n = int(kind[9:])
                        if n:
                            dve.wait_ge(*expd.at(l, n))
                            for job in ("lT0", "lT1"):
                                dve.wait_ge(*job_read[job_bank(job)].at(l, job_k(job)))
                            dve.tensor_tensor(qs[:, n % 2], lqT[:], ex[:], ALU.mult)
                            dve.tensor_tensor(ks[:, n % 2], lkT[:], ex[:], ALU.mult).then_inc(scaled.sem, 1)
                    elif kind.startswith("level_sel"):
                        n = int(kind[9:])
                        for hh in range(2):
                            job = f"lev{n}_{hh}"
                            job_wait(job)
                            dve.sem_inc(passed.sem, 1)
                            dve.copy_predicated(aT[:, hh], lmask[:, n:n + 1, :].to_broadcast([P, 2 * T, P]),
                                                heads(job_ps(job)[:], 2 * T)).then_inc(job_read[job_bank(job)].sem, 1)
                    elif kind == "inter_exp":
                        dve.wait_ge(*scaled.at(l, 6))
                        g3 = cum[:].rearrange("p a (b c) -> p (a b) c", c=CHUNK)
                        end = g3[:, :, CHUNK - 1:CHUNK].broadcast_to([P, 2 * S // CHUNK, CHUNK])
                        dve.tensor_tensor(ex[:].rearrange("p a (b c) -> p (a b) c", c=CHUNK), end, g3,
                                          ALU.subtract).then_inc(expo.sem, 1)
                    elif kind == "inter_mul":
                        dve.wait_ge(*eg_in.at(l, 1))
                        dve.tensor_tensor(qg[:], lqT[:], eG[:], ALU.mult)
                        dve.wait_ge(*expd.at(l, 7))
                        dve.tensor_tensor(ks[:, 1], lkT[:], ex[:], ALU.mult).then_inc(scaled.sem, 1)
                    elif kind.startswith("state"):
                        c = int(kind[5:])
                        job_wait(f"st{c}")
                        for p in range(2):
                            ps = job_ps(f"st{c}")[:, p * P:(p + 1) * P]
                            if c == 0:
                                last = dve.tensor_copy(state[:, 0, p, :], ps)
                            else:
                                last = dve.scalar_tensor_tensor(
                                    out=state[:, c, p, :], in0=state[:, c - 1, p, :],
                                    scalar=eG[:, p, c * CHUNK + CHUNK - 1:c * CHUNK + CHUNK], in1=ps,
                                    op0=ALU.mult, op1=ALU.add)
                            if p == 0:
                                step_done(last)
                        last.then_inc(state_in.sem, 1)
                        dve.wait_ge(*state_in.at(l, c + 1))
                        dve.sem_inc(job_read[job_bank(f"st{c}")].sem, 1)
                    elif kind == "g_rstd":
                        dve.wait_ge(*g_squares.at(l, T))
                        n = T * GH
                        chain(dve.tensor_scalar(stats[:, 24:24 + n], stats[:, 16:16 + n], 1.0 / GDV, EPS,
                                                ALU.mult, ALU.add))
                        rsqrt(stats[:, 24:24 + n], stats[:, 32:32 + n], stats[:, 16:16 + n])
                    elif kind == "g_scale":
                        for hh in range(2):
                            for i in range(2 * T):
                                t, h = i // 2, 2 * (i % 2) + hh
                                blk = slr[:, t, h * GDV:(h + 1) * GDV]
                                at = 32 + 4 * hh + i
                                last = dve.scalar_tensor_tensor(
                                    out=blk, in0=job_ps(f"go{hh}")[:, i * GDV:(i + 1) * GDV],
                                    scalar=stats[:, at:at + 1], in1=blk, op0=ALU.mult, op1=ALU.mult)
                            last.then_inc(job_read[job_bank(f"go{hh}")].sem, 1)
                    elif kind == "g_turn":
                        turn_lo(JOBS_OF[kind], brT_h[1], brT_l[1])
                    elif kind.startswith("scores"):
                        p = int(kind[6:])
                        b = p % 2
                        for hh in range(2):
                            job_wait(f"s{hh}_{p}")
                            dve.tensor_tensor(pr[:, b, 3 * hh:3 * hh + 3, :],
                                              heads(job_ps(f"s{hh}_{p}")[:, 0:3 * P], 3), causal[:],
                                              ALU.add).then_inc(job_read[job_bank(f"s{hh}_{p}")].sem, 1)
                        for hh in range(2):
                            dve.wait_ge(*job_read[job_bank(f"s{hh}_{p}")].at(l, job_k(f"s{hh}_{p}")))
                        rows = pr[:, b].rearrange("p (h c) n -> p h c n", h=2)
                        step_done(dve.tensor_reduce(stats[:, 56:58], rows[:, :, 0, :], AX.X, ALU.max))
                        step_done(dve.tensor_reduce(stats[:, 58:60],
                                                    rows[:, :, 1:3, :].rearrange("p h c n -> p h (c n)"),
                                                    AX.X, ALU.max))
                        after(count)
                        dve.tensor_scalar(stats[:, 40 + 4 * b:44 + 4 * b], stats[:, 56:60], -(DH ** -0.5), None,
                                          ALU.mult).then_inc(p_in.sem, 1)
                    elif kind.startswith("probs"):
                        p = int(kind[5:])
                        b = p % 2
                        dve.wait_ge(*p_exp.at(l, p + 1))
                        chain(dve.reciprocal(stats[:, 60:64], stats[:, 48 + 4 * b:52 + 4 * b]))
                        for i, (lo, hi) in enumerate(ROW_BLOCKS):
                            last = dve.tensor_scalar(pr[:, b, lo:hi, :], pr[:, b, lo:hi, :],
                                                     stats[:, 60 + i:61 + i], None, ALU.mult)
                        last.then_inc(p_norm.sem, 1)
                    elif kind.startswith("values"):
                        p = int(kind[6:])
                        hi_count += 1
                        dve.wait_ge(*job_hi.at(l, hi_count))
                        dve.tensor_tensor(brT_l[0][:, p, :], job_ps(f"o_{p}")[:, 0:S],
                                          brT_h[0][:, p, :].bitcast(F32), ALU.subtract)\
                            .then_inc(job_read[job_bank(f"o_{p}")].sem, 1)
                    elif kind == "tap":
                        k = arg
                        if k == 0:
                            for job in JOBS_OF["u_turn"]:
                                dve.wait_ge(*job_read[job_bank(job)].at(l, job_k(job)))
                            base = count
                        for c in range(CC):
                            w_k = param("w_dw", c * TAPS + k)
                            if k == 0:
                                step_done(dve.tensor_scalar(acc[:, c, :], uT[:, c, 0:S], w_k, param("b_dw", c),
                                                            ALU.mult, ALU.add))
                                tap_no = {} if c == 0 else tap_no
                                tap_no[c] = count
                            else:
                                after(tap_no[c])
                                ins = dve.scalar_tensor_tensor(out=acc[:, c, :], in0=uT[:, c, k:k + S], scalar=w_k,
                                                               in1=acc[:, c, :], op0=ALU.mult, op1=ALU.add)
                                if k == TAPS - 1 and c == CC - 1:
                                    ins.then_inc(taps_in.sem, 1)
                                else:
                                    tap_no[c] = step_done(ins)
                    elif kind == "ln_mean":
                        job_wait("mu")
                        dve.tensor_tensor(acc[:], acc[:], job_ps("mu")[:, 0:S].rearrange("p (a n) -> p a n", a=1)
                                          .to_broadcast([P, CC, S]), ALU.subtract).then_inc(centred.sem, 1)
                        dve.wait_ge(*centred.at(l, 1))
                        dve.sem_inc(job_read[job_bank("mu")].sem, 1)
                    elif kind == "ln_var":
                        job_wait("var")
                        dve.tensor_scalar(var, job_ps("var")[:, 0:S], EPS, None, ALU.add)\
                            .then_inc(job_read[job_bank("var")].sem, 1)
                        dve.wait_ge(*job_read[job_bank("var")].at(l, job_k("var")))
                        rsqrt(var, rst, rsc)
                        dve.tensor_tensor(acc[:], acc[:], rst.rearrange("p (a n) -> p a n", a=1)
                                          .to_broadcast([P, CC, S]), ALU.mult).then_inc(ln_in.sem, 1)
                    elif kind == "ln_out":
                        dve.wait_ge(*ln_sig.at(l, 1))
                        dve.tensor_tensor(acc[:], acc[:], square, ALU.mult).then_inc(silu_in.sem, 1)
                        dve.wait_ge(*conv_hi.at(l, 1))
                        dve.tensor_tensor(brT_l[0][:], acc[:], brT_h[0][:].bitcast(F32), ALU.subtract)\
                            .then_inc(conv_split.sem, 1)
                    elif kind in ("post_mix", "post_mlp"):
                        n, gs = (0, ("mo0", "mo1")) if kind == "post_mix" else (1, ("dn0", "dn1"))
                        dve.wait_ge(*y_squares.at(l, n + 1))
                        y2 = stats[:, 4:8].rearrange("p (t c) -> p t c", c=2)
                        chain(dve.tensor_tensor(stats[:, 8:10], y2[:, :, 0], y2[:, :, 1], ALU.add))
                        chain(dve.tensor_scalar(stats[:, 8:10], stats[:, 8:10], 1.0 / D, EPS, ALU.mult, ALU.add))
                        rsqrt(stats[:, 8:10], stats[:, 10:12], stats[:, 12:14])
                        dve.wait_ge(*gpost_in.at(l, 16 * (n + 1)))
                        for t in range(T):
                            for c, g in enumerate(gs):
                                dve.scalar_tensor_tensor(out=tmp[:, c, :], in0=group_ps(g, t)[:],
                                                         scalar=stats[:, 10 + t:11 + t],
                                                         in1=gpost[:, c * COLS:(c + 1) * COLS], op0=ALU.mult,
                                                         op1=ALU.mult).then_inc(acc_read[group_bank(g, t)].sem, 1)
                            for c, g in enumerate(gs):
                                dve.wait_ge(*acc_read[group_bank(g, t)].at(l, group_k(g)))
                            last = dve.tensor_tensor(resid[:, t, :], resid[:, t, :],
                                                     tmp[:].rearrange("p t n -> p (t n)"), ALU.add)
                            if t == 0:
                                chain(last)
                        last.then_inc(resid_in.sem, 1)
                        if n:
                            dve.wait_ge(*resid_in.at(l, 2))
                            dve.sem_inc(layer_in.sem, 1)
                    elif kind.startswith("hid_turn"):
                        n = int(kind[8:])
                        turn_lo(JOBS_OF[kind], hid_h[:, 4 * n:4 * n + 4], hid_l[:, 4 * n:4 * n + 4])
                after(count)
                assert count < V_STEPS, count
                dve.sem_inc(v_steps.sem, V_STEPS - count)

        @block.tensor
        def _(pe):
            pe.wait_ge(consts.sem, 1)
            with pe.Fori(0, DEPTH) as l:

                def job_start(job):
                    pe.wait_ge(*job_read[job_bank(job)].at(l, job_k(job) - 1))
                    return job_ps(job)

                def job_end(job, last):
                    last.then_inc(job_done[job_bank(job)].sem, 1)

                def jobs_read(jobs, before=None):
                    for job in {job_bank(j_): j_ for j_ in jobs}.values():
                        if before is None or job_bank(job) != job_bank(before):
                            pe.wait_ge(*job_read[job_bank(job)].at(l, job_k(job)))

                def turn(jobs, src):
                    for i, job in enumerate(jobs):
                        ps = job_start(job)
                        for c in range(2):
                            for t in range(T):
                                last = pe.transpose(ps[:, c * S + t * P:c * S + (t + 1) * P],
                                                    src[:, t, (2 * i + c) * P:(2 * i + c + 1) * P], ident[:])
                        job_end(job, last)

                for step in PLAN:
                    kind, arg = step if isinstance(step, tuple) else (step, None)
                    if kind == "strip":
                        u = arg
                        g, j, first, last_of = STRIPS[u]
                        lhs = GROUPS[GROUP_NO[g]][4]
                        if first:
                            if lhs == "branch0":
                                jobs_read([f"o_{p}" for p in range(PAIRS)])
                            elif lhs == "branch1":
                                jobs_read(JOBS_OF["g_turn"])
                            elif lhs == "branch2":
                                pe.wait_ge(*conv_split.at(l, 1))
                            elif g in ("ca", "mo0", "up0"):
                                jobs_read(JOBS_OF[{"ca": "xpose_pre", "mo0": "mix_turn", "up0": "xpose_mlp"}[g]])
                            elif g == "dn0":
                                jobs_read([j_ for n in range(8) for j_ in JOBS_OF[f"hid_turn{n}"]])
                            for t in range(T):
                                pe.wait_ge(*acc_read[group_bank(g, t)].at(l, group_k(g) - 1))
                        a_h, a_l = {"act": (act_h, act_l), "branch0": (brT_h[0], brT_l[0]),
                                    "branch1": (brT_h[1], brT_l[1]), "branch2": (brT_h[0], brT_l[0]),
                                    "hid": (hid_h, hid_l)}[lhs]
                        pe.wait_ge(*strip_split.at(l, u + 1))
                        for t in range(T):
                            ps = group_ps(g, t)[:]
                            for c in range(2):
                                s_h = a_h[:, 2 * j + c, t * P:(t + 1) * P]
                                s_l = a_l[:, 2 * j + c, t * P:(t + 1) * P]
                                r_h = w_h[:, u % SPLIT_SLOTS, c, :]
                                r_l = w_l[:, u % SPLIT_SLOTS, c, :]
                                pe.matmul(ps, s_h, r_h, start=first and c == 0, stop=False)
                                pe.matmul(ps, s_h, r_l, start=False, stop=False)
                                last = pe.matmul(ps, s_l, r_h, start=False, stop=last_of and c == 1)
                        last.then_inc(strip_used.sem, 1)
                    elif kind == "xpose_pre":
                        pe.wait_ge(*xs_in.at(l, 1))
                        turn(JOBS_OF[kind], xs)
                    elif kind == "xpose_mlp":
                        pe.wait_ge(*xs_in.at(l, 2))
                        turn(JOBS_OF[kind], xs)
                    elif kind == "mix_turn":
                        pe.wait_ge(*mix_in.at(l, 1))
                        turn(JOBS_OF[kind], xs)
                    elif kind == "la":
                        ps = job_start("la")
                        pe.wait_ge(*la_split.at(l, 1))
                        for t in range(T):
                            for c in range(KC):
                                s_h = act_h[:, c, t * P:(t + 1) * P]
                                s_l = act_l[:, c, t * P:(t + 1) * P]
                                dst = ps[:, t * RANK:(t + 1) * RANK]
                                pe.matmul(dst, s_h, la_h[:, c, :], start=c == 0, stop=False)
                                pe.matmul(dst, s_h, la_l[:, c, :], start=False, stop=False)
                                last = pe.matmul(dst, s_l, la_h[:, c, :], start=False, stop=c == KC - 1)
                        job_end("la", last)
                    elif kind == "la_turn":
                        ps = job_start("laT")
                        jobs_read(["la"], "laT")
                        for t in range(T):
                            last = pe.transpose(ps[0:RANK, t * P:(t + 1) * P], la_nat[:, t, :], ident[:])
                        job_end("laT", last)
                    elif kind == "decay":
                        jobs_read(["laT"], "dec0")
                        pe.wait_ge(*a2_in.at(l, 16))
                        for i in range(2):
                            ps = job_start(f"dec{i}")
                            job_end(f"dec{i}", pe.matmul(ps[:, 0:S], a2[:, i * P:(i + 1) * P], laT[:],
                                                         start=True, stop=True))
                    elif kind == "u_turn":
                        pe.wait_ge(*u_in.at(l, 1))
                        turn(JOBS_OF[kind], u_nat)
                    elif kind == "l_turn":
                        for t in range(T):
                            pe.wait_ge(*acc_read[group_bank("lqk", t)].at(l, group_k("lqk")))
                        turn(JOBS_OF[kind], u_nat)
                    elif kind.startswith("level_mul"):
                        n = int(kind[9:])
                        if n:
                            pe.wait_ge(*scaled.at(l, n))
                        else:
                            jobs_read(["lT0", "lT1"], "lev0_0")
                        q_, k_ = (qs[:, n % 2], ks[:, n % 2]) if n else (lqT, lkT)
                        for hh in range(2):
                            ps = job_start(f"lev{n}_{hh}")
                            rows = slice(GDK * hh, GDK * hh + GDK)
                            for i in range(2 * T):
                                t, p = i // 2, i % 2
                                last = pe.matmul(ps[:, i * P:(i + 1) * P], k_[rows, p, t * P:(t + 1) * P],
                                                 q_[rows, p, t * P:(t + 1) * P], start=True, stop=True)
                            job_end(f"lev{n}_{hh}", last)
                    elif kind == "kd_turn":
                        pe.wait_ge(*scaled.at(l, 7))
                        ps = job_start("kdT")
                        for t in range(T):
                            for p in range(2):
                                last = pe.transpose(ps[:, t * S + p * P:t * S + (p + 1) * P],
                                                    ks[:, 1, p, t * P:(t + 1) * P], ident[:])
                        job_end("kdT", last)
                    elif kind.startswith("state"):
                        c = int(kind[5:])
                        ps = job_start(f"st{c}")
                        jobs_read(["kdT"], f"st{c}")
                        for t in range(T):
                            pe.wait_ge(*acc_read[group_bank("lv", t)].at(l, group_k("lv")))
                        pe.sem_inc(passed.sem, 1)
                        rows = slice(CHUNK * (c % 2), CHUNK * (c % 2) + CHUNK)
                        for h in range(GH):
                            p, hh = h // 2, h % 2
                            last = pe.matmul(ps[GDK * hh:GDK * hh + GDK, p * P:(p + 1) * P],
                                             kdn[rows, c // 2, h * GDK:(h + 1) * GDK],
                                             lv[rows, c // 2, h * GDV:(h + 1) * GDV], start=True, stop=True)
                        job_end(f"st{c}", last)
                    elif kind.startswith("g_out"):
                        hh = int(kind[5:])
                        ps = job_start(f"go{hh}")
                        if hh == 0:
                            pe.wait_ge(*state_in.at(l, 3))
                            jobs_read([f"lev{len(LEVELS) - 1}_{i}" for i in range(2)], "go0")
                        rows = slice(GDK * hh, GDK * hh + GDK)
                        for i in range(2 * T):
                            t, p = i // 2, i % 2
                            h = 2 * p + hh
                            cols = slice(i * GDV, (i + 1) * GDV)
                            pe.matmul(ps[:, cols], aT[:, hh, i, :], lv[:, t, h * GDV:(h + 1) * GDV], start=True,
                                      stop=False, skip_group_check=True)
                            for c in range(2 * t, 2 * t + 2):
                                if c:
                                    o_rows = slice(CHUNK * (c % 2), CHUNK * (c % 2) + CHUNK)
                                    last = pe.matmul(ps[o_rows, cols], qg[rows, p, c * CHUNK:(c + 1) * CHUNK],
                                                     state[rows, c - 1, p, :], start=False, stop=c % 2 == 1,
                                                     skip_group_check=True)
                        job_end(f"go{hh}", last)
                    elif kind == "g_turn":
                        jobs_read(["go0", "go1"], "gT0")
                        turn(JOBS_OF[kind], slr)
                    elif kind in ("q_turn", "k_turn"):
                        n = 0 if kind == "q_turn" else 1
                        pe.wait_ge(*rope_out.at(l, n + 1))
                        turn(JOBS_OF[kind], xs[:, :, n * 512:n * 512 + 512])
                    elif kind.startswith("scores"):
                        p = int(kind[6:])
                        if p == 0:
                            jobs_read(JOBS_OF["q_turn"] + JOBS_OF["k_turn"], "s0_0")
                        for hh in range(2):
                            job = f"s{hh}_{p}"
                            ps = job_start(job)
                            rows = slice(DH * hh, DH * hh + DH)
                            for t in range(T):
                                last = pe.matmul(ps[:, t * P:t * P + (t + 1) * P], qT[rows, p, t * P:(t + 1) * P],
                                                 kT[rows, p, 0:(t + 1) * P], start=True, stop=True)
                            job_end(job, last)
                    elif kind.startswith("probs"):
                        p = int(kind[5:])
                        pe.wait_ge(*p_norm.at(l, p + 1))
                        for job, lo, hi in ((f"pa_{p}", 0, 4), (f"pb_{p}", 4, 6)):
                            ps = job_start(job)
                            for i in range(lo, hi):
                                last = pe.transpose(ps[:, (i - lo) * P:(i - lo + 1) * P], pr[:, p % 2, i, :], ident[:])
                            job_end(job, last)
                    elif kind.startswith("values"):
                        p = int(kind[6:])
                        jobs_read([f"pa_{p}", f"pb_{p}"], f"o_{p}")
                        if p == 0:
                            for t in range(T):
                                pe.wait_ge(*acc_read[group_bank("mv", t)].at(l, group_k("mv")))
                        ps = job_start(f"o_{p}")
                        for hh in range(2):
                            h = 2 * p + hh
                            o_rows = slice(DH * hh, DH * hh + DH)
                            cols = slice(h * DH, (h + 1) * DH)
                            pe.matmul(ps[o_rows, 0:P], v[:, 0, cols], prT[:, 3 * hh, :], start=True, stop=True,
                                      skip_group_check=True)
                            pe.matmul(ps[o_rows, P:S], v[:, 0, cols], prT[:, 3 * hh + 1, :], start=True, stop=False,
                                      skip_group_check=True)
                            last = pe.matmul(ps[o_rows, P:S], v[:, 1, cols], prT[:, 3 * hh + 2, :], start=False,
                                             stop=True, skip_group_check=True)
                        job_end(f"o_{p}", last)
                    elif kind == "ln_mean":
                        pe.wait_ge(*taps_in.at(l, 1))
                        ps = job_start("mu")
                        for c in range(CC):
                            last = pe.matmul(ps[:, 0:S], over_ch[:], acc[:, c, :], start=c == 0, stop=c == CC - 1)
                        job_end("mu", last)
                    elif kind == "ln_var":
                        pe.wait_ge(*ch_sq.at(l, 1))
                        ps = job_start("var")
                        for c in range(CC):
                            last = pe.matmul(ps[:, 0:S], over_ch[:], square[:, c, :], start=c == 0,
                                             stop=c == CC - 1)
                        job_end("var", last)
                    elif kind.startswith("hid_turn"):
                        n = int(kind[8:])
                        pe.wait_ge(*hid_sq.at(l, n + 1))
                        turn(JOBS_OF[kind], hid[:, n % 2])


_IN_ORDER = ["x", "positions", "inv_freq", "packed", "w_in", "b_gate", "w_gla_a2", "g_gla_norm", "w_moba_o",
             "w_gla_o", "w_conv_o", "w_mix_out", "g_mix_post", "w_mlp_up", "w_mlp_down", "g_mlp_post"]


def kernel(**inputs):
    import numpy as np
    import concourse.bacc as bacc
    from concourse.bass_utils import run_bass_kernel_spmd

    def chunks(a):
        a = np.asarray(a)
        a = a.reshape(a.shape[:-1] + (a.shape[-1] // P, P))
        a = np.moveaxis(a, -1, 1)
        return np.moveaxis(a, -1, 2).reshape(a.shape[0], P, -1)

    data = {k: np.ascontiguousarray(v) for k, v in inputs.items()}
    data["positions"] = np.ascontiguousarray(data["positions"].reshape(T, P).T)
    freq = np.float32(10000.0) ** (-np.arange(HALF, dtype=np.float32) / np.float32(HALF))
    data["inv_freq"] = np.ascontiguousarray(np.broadcast_to(freq.astype(np.float32), (P, HALF)))
    data["packed"] = np.ascontiguousarray(np.concatenate(
        [chunks(data[n]) for n in ("g_mix_pre", "g_mlp_pre", "b_gla_a", "g_conv_ln", "b_conv_ln", "b_dw", "w_dw")],
        axis=-1))
    nc = bacc.Bacc("TRN2", target_bir_lowering=False, num_devices=1)
    arrays, args = {}, []
    for name in _IN_ORDER:
        arrays[name + "_dram"] = data[name]
        args.append(nc.dram_tensor(name + "_dram", data[name].shape, mybir.dt.from_np(data[name].dtype),
                                   kind="ExternalInput").ap())
    out = nc.dram_tensor("out_dram", (1, S, D), F32, kind="ExternalOutput").ap()
    trunk(nc, *args, out)
    r = run_bass_kernel_spmd(nc, [arrays], core_ids=[0])
    return r.results[0]["out_dram"]
```

```python
from contextlib import ExitStack

import concourse.bass as bass
from concourse import mybir

F32 = mybir.dt.float32
F32R = mybir.dt.float32r
I32 = mybir.dt.int32
ACT = mybir.ActivationFunctionType
ALU = mybir.AluOpType
AX = mybir.AxisListType

P = 128
D = 1024
S = 256
T = S // P
DEPTH = 2
KC = D // P
EPS = 1e-6
NEG = -1e30
HEADS = 8
DH = 64
PAIRS = HEADS // 2
GH = 4
GDK = 64
GDV = 128
RANK = 16
CHUNK = 64
CH = 512
CC = CH // P
TAPS = 31
FF = 4096
HALF = DH // 2
COLS = 512
RAW_SLOTS = 5
SPLIT_SLOTS = 5

C_Q, C_K, C_V = 0, 512, 1024
C_LQK, C_LV, C_LA, C_LR, C_CA, C_CG, C_GATES = 1536, 2048, 2560, 2576, 3088, 3600, 4112

PACKED = [("g_mix_pre", KC), ("g_mlp_pre", KC), ("b_gla", 2), ("g_ln", CC), ("b_ln", CC), ("b_dw", CC),
          ("w_dw", CC * TAPS)]
PACK_AT = {}
_at = 0
for _n, _w in PACKED:
    PACK_AT[_n] = _at
    _at += _w
PACK_W = _at

BRANCHES = (1, 0, 2)
GROUPS = (
    [("ca", "w_in", C_CA, D, "act"), ("cg", "w_in", C_CG, D, "act"), ("lqk", "w_in", C_LQK, D, "act"),
     ("lv", "w_in", C_LV, D, "act"), ("lr", "w_in", C_LR, D, "act"), ("mq", "w_in", C_Q, D, "act"),
     ("mk", "w_in", C_K, D, "act"), ("mv", "w_in", C_V, D, "act")]
    + [g for b, w in zip(BRANCHES, ("w_gla_o", "w_moba_o", "w_conv_o"))
       for g in [(f"g{b}{c}", "w_in", C_GATES + b * D + c * COLS, D, "act") for c in range(2)]
       + [(f"w{b}{c}", w, c * COLS, CH, f"branch{b}") for c in range(2)]]
    + [(f"mo{c}", "w_mix_out", c * COLS, D, "act") for c in range(2)]
    + [(f"up{c}", "w_mlp_up", c * COLS, D, "act") for c in range(FF // COLS)]
    + [(f"dn{c}", "w_mlp_down", c * COLS, FF, "hid") for c in range(2)]
)
GROUP_NO = {g[0]: i for i, g in enumerate(GROUPS)}
STRIPS = []
for _g in GROUPS[:-2]:
    _n = _g[3] // 256
    STRIPS += [(_g[0], j, j == 0, j == _n - 1) for j in range(_n)]
for _j in range(FF // 256):
    STRIPS += [(f"dn{c}", _j, _j == 0, _j == FF // 256 - 1) for c in range(2)]
NS = len(STRIPS)
LAST_STRIP = {g: u for u, (g, j, first, last) in enumerate(STRIPS) if last}
assert NS % RAW_SLOTS == 0 and NS % SPLIT_SLOTS == 0 and len(GROUPS) % 2 == 0

LEVELS = [0, 32, 16, 8, 4, 2, 1]

JOBS_OF = {
    "la": ["la"], "la_turn": ["laT"], "decay": ["dec0", "dec1"],
    "u_turn": ["uT0", "uT1"], "l_turn": ["lT0", "lT1"], "q_turn": ["qT0", "qT1"], "k_turn": ["kT0", "kT1"],
    "kd_turn": ["kdT"], "g_turn": ["gT0", "gT1"], "g_out": ["go0", "go1"], "ln_mean": ["mu"], "ln_var": ["var"],
}
for _t in range(T):
    for _name in ("pre_turn", "mix_turn", "mlp_turn"):
        JOBS_OF[f"{_name}{_t}"] = [f"{_name}{_t}_{i}" for i in range(2)]
for _i in range(len(LEVELS)):
    JOBS_OF[f"level{_i}"] = [f"lev{_i}_{hh}" for hh in range(2)]
for _i in range(3):
    JOBS_OF[f"state{_i}"] = [f"st{_i}"]
for _i in range(PAIRS):
    JOBS_OF[f"scores{_i}"] = [f"s0_{_i}", f"s1_{_i}"]
    JOBS_OF[f"probs{_i}"] = [f"pa_{_i}", f"pb_{_i}"]
    JOBS_OF[f"values{_i}"] = [f"o_{_i}"]
for _i in range(8):
    JOBS_OF[f"hid_turn{_i}"] = [f"h0_{_i}", f"h1_{_i}"]

AFTER = {}


def place(u, *steps):
    AFTER.setdefault(u, []).extend(steps)


place(2, "la_round")
place(4, "la")
place(5, ("use", "la"), "la_turn")
place(6, ("use", "la_turn"), "decay")
place(7, ("use", "decay"))
place(8, "cumulate", "u_turn")
place(9, ("use", "u_turn"), ("tap", 0))
place(12, "l_turn", "level_sub1", "level_sub2")
place(13, ("use", "l_turn"))
for _i in range(1, len(LEVELS) + 1):
    _u = 12 + 2 * _i
    if _i < len(LEVELS):
        place(_u, f"level_mul{_i}")
        place(_u + 1, f"level{_i}")
        if _i + 2 <= len(LEVELS):
            place(_u, f"level_sub{_i + 2}")
    if _i == 1:
        place(_u, "level0")
        place(_u + 1, ("use", "level0"))
    else:
        place(_u, ("use", f"level{_i - 1}"))
place(26, "q_turn", "inter_mul")
place(27, ("use", "q_turn"), "kd_turn")
place(28, ("use", "kd_turn"))
place(29, "k_turn", "state0")
place(30, ("use", "k_turn"), ("use", "state0"), "state1")
place(31, ("use", "state1"), "state2")
place(32, ("use", "state2"))
place(33, "g_out", ("use", "g_out"))
place(34, "g_rstd", "g_scale")
for _i in range(PAIRS):
    _u = 34 + 4 * _i
    place(_u, f"scores{_i}")
    place(_u + 1, ("use", f"scores{_i}"))
    place(_u + 2, f"norm{_i}")
    place(_u + 4, f"probs{_i}", ("use", f"probs{_i}"))
    place(_u + 5, f"values{_i}", ("use", f"values{_i}"))
place(36, "g_turn")
place(37, ("use", "g_turn"))
place(55, "ln_mean")
place(56, ("use", "ln_mean"))
place(57, "ln_var")
place(58, ("use", "ln_var"))
place(59, "ln_affine")
place(60, "ln_silu")
place(61, "ln_hi")
place(62, "ln_lo")
for _i in range(8):
    place(LAST_STRIP[f"up{_i}"] + 2, f"hid_turn{_i}", ("use", f"hid_turn{_i}"))

COST = {"evac_mq": 3.7, "evac_mk": 3.7, "evac_lr": 2.4, "evac_cg": 1.1, "evac_g": 1.2, "evac_w": 2.3,
        "decay": 0.8, "cumulate": 1.2, "level_sub": 0.7, "level_mul": 1.2, "level": 1.2, "inter_mul": 1.2,
        "state": 0.5, "g_rstd": 0.8, "g_scale": 2.1, "g_turn": 1.2, "scores": 1.9, "norm": 0.2, "values": 0.3}
SPLIT_COST, TAP_COST = 1.13, 1.5
FIRST_TAP, LAST_TAP = 10, 53

ROW_BLOCKS = [(0, 1), (3, 4), (1, 3), (4, 6)]


def tap_spots():
    load = {}
    for u in range(FIRST_TAP, LAST_TAP + 1):
        g, _, _, last = STRIPS[u]
        steps = [s if isinstance(s, str) else s[1] for s in AFTER.get(u, []) if s not in JOBS_OF]
        load[u] = SPLIT_COST + sum(COST.get(s.rstrip("0123456789"), 0.0) for s in steps)
        if last:
            load[u] += COST.get("evac_" + (g[0] if g[1].isdigit() else g), 0.0)
    pace = 2.6
    while True:
        spots, tap, ahead = {}, 1, 0.0
        for u in load:
            ahead = max(ahead + load[u] - pace, -1.0)
            while tap < TAPS and ahead + TAP_COST <= 0.75:
                ahead += TAP_COST
                spots.setdefault(u, []).append(tap)
                tap += 1
        if tap == TAPS:
            return spots
        pace += 0.02


def build_plan():
    between = {
        "ca": (2, ["pre_turn1", ("use", "pre_turn1"), "squares0", "rstd0"]),
        "w20": (4, [("evac", ("w20", (0,))), ("evac", ("w21", (0,)))]),
        "mo0": (3, ["mix_turn1", ("use", "mix_turn1")]),
        "mo1": (4, ["post_mix0"]),
        "up0": (3, ["mlp_turn1", ("use", "mlp_turn1"), "squares1", "rstd1"]),
        "dn0": (4, ["post_mlp0"]),
    }
    taken = {"w20": (3, ("use", "mix_turn0")), "mo1": (2, ("use", "mlp_turn0"))}
    behind = {
        "w20": ["mix_turn0", ("evac", ("w20", (1,))), ("evac", ("w21", (1,)))],
        "mo1": ["mlp_turn0", "post_mix1"],
        "dn0": ["post_mlp1"],
    }
    by_tile = {LAST_STRIP[g] - 3: g for g in ("ca", "mo0", "mo1", "up0")}
    by_tile[LAST_STRIP["w21"] - 3] = "w20"
    by_tile[NS - 4] = "dn0"
    spots = tap_spots()

    def rest(u):
        steps = []
        if u + SPLIT_SLOTS < NS:
            steps.append(("hi", u + SPLIT_SLOTS))
        if u + SPLIT_SLOTS - 1 < NS:
            steps.append(("lo", u + SPLIT_SLOTS - 1))
        g, _, _, last = STRIPS[u]
        if last and g not in ("w20", "w21", "mo0", "mo1", "dn0", "dn1"):
            steps.append(("evac", (g, tuple(range(T)))))
        return steps + AFTER.get(u, []) + [("tap", k) for k in spots.get(u, [])]

    plan = []
    for u in range(SPLIT_SLOTS):
        plan += [("hi", u)] + ([("lo", u)] if u < SPLIT_SLOTS - 1 else [])
        if u == 0:
            plan += ["pre_turn0", ("use", "pre_turn0")]
    u = 0
    while u < NS:
        if u in by_tile:
            block, g = range(u, u + 4), by_tile[u]
            n, steps = between[g]
            plan += [("mm", (v, 0)) for v in block[:n]] + steps + [("mm", (v, 0)) for v in block[n:]]
            for v in block:
                plan += [("mm", (v, 1))] + rest(v)
                if g in taken and v == u + taken[g][0] - 1:
                    plan.append(taken[g][1])
            plan += behind.get(g, [])
            u += 4
        else:
            plan += [("mm", (u, 0)), ("mm", (u, 1))] + rest(u)
            u += 1
    return plan


PLAN = build_plan()
JOBS = [j for step in PLAN if isinstance(step, str) for j in JOBS_OF.get(step, [])]
assert len(set(JOBS)) == len(JOBS) == sum(len(v) for v in JOBS_OF.values())
JOB_BANKS = 4
JOBS_PER_BANK = len(JOBS) // JOB_BANKS
assert len(JOBS) % JOB_BANKS == 0, len(JOBS)
JOB_NO = {j: i for i, j in enumerate(JOBS)}
for _step, _jobs in JOBS_OF.items():
    for _j in _jobs:
        if JOB_NO[_j] + JOB_BANKS < len(JOBS):
            _next = JOBS[JOB_NO[_j] + JOB_BANKS]
            _start = PLAN.index(next(s for s in JOBS_OF if _next in JOBS_OF[s]))
            assert PLAN.index("g_scale" if _step == "g_out" else ("use", _step)) < _start, (_j, _next)


class Signal:

    def __init__(self, sem, per_layer, primed=0):
        self.sem, self.per_layer, self.primed = sem, per_layer, primed

    def at(self, layer, k):
        assert 1 <= k + self.primed
        return self.sem, layer * self.per_layer + (k + self.primed)


def trunk(nc, x, positions, inv_freq, packed, w_in, b_gate, w_a2, g_gla, w_moba_o, w_gla_o, w_conv_o,
          w_mix_out, g_mix_post, w_up, w_down, g_mlp_post, out):
    weights = {"w_in": w_in, "w_moba_o": w_moba_o, "w_gla_o": w_gla_o, "w_conv_o": w_conv_o,
               "w_mix_out": w_mix_out, "w_mlp_up": w_up, "w_mlp_down": w_down}
    ctx = ExitStack()
    with ctx:
        def sb(name, shape, dt=F32, where=ctx):
            return where.enter_context(nc.sbuf_tensor(name, shape, dt))

        def signal(name, per_layer, primed=0):
            return Signal(ctx.enter_context(nc.semaphore(name)), per_layer, primed)

        resid = sb("resid", [P, T, D])
        xs = sb("xs", [P, T, D])
        act_h = sb("act_h", [P, KC, S], F32R)
        act_l = sb("act_l", [P, KC, S], F32R)
        raw = sb("raw", [P, RAW_SLOTS, 2, COLS])
        w_h = sb("w_h", [P, SPLIT_SLOTS, 2, COLS], F32R)
        w_l = sb("w_l", [P, SPLIT_SLOTS, 2, COLS], F32R)
        pk = sb("pk", [P, PACK_W])
        a2 = sb("a2", [2 * RANK, 2 * P])
        bg = sb("bg", [P, D])
        gpost = sb("gpost", [P, D])
        ggla = sb("ggla", [P, GDV])
        la_raw = sb("la_raw", [P, KC, RANK])
        la_w = sb("la_w", [P, KC, 2, RANK], F32R)
        la_nat = sb("la_nat", [P, T, 2 * RANK])
        laT = sb("laT", [2 * RANK, S])
        ident = sb("ident", [P, P])
        over_ch = sb("over_ch", [P, P])
        causal = sb("causal", [P, 3, P])
        keep = sb("keep", [P, 2 * S])
        lmask = sb("lmask", [P, len(LEVELS), P], mybir.dt.int16)
        cos_t = sb("cos_t", [P, T, HALF])
        sin_t = sb("sin_t", [P, T, HALF])
        aT = sb("aT", [P, 2, 2 * T, P])
        tmp = sb("tmp", [P, T, COLS])
        stats = sb("stats", [P, 96])
        inv_f = sb("inv_f", [P, HALF])
        pos_i = sb("pos_i", [P, T], I32)
        pos_f = sb("pos_f", [P, T])
        rt = tmp[:].rearrange("p t n -> p (t n)")[:, 0:5 * T * HALF].rearrange("p (i t n) -> p i t n", i=5, t=T)
        mixers = ExitStack()
        qT = sb("qT", [P, PAIRS, S], where=mixers)
        kT = sb("kT", [P, PAIRS, S], where=mixers)
        v = sb("v", [P, T, COLS], where=mixers)
        brT_h = [sb(f"br{i}_h", [P, CC, S], F32R, mixers) for i in range(2)]
        brT_l = [sb(f"br{i}_l", [P, CC, S], F32R, mixers) for i in range(2)]
        lqT = sb("lqT", [P, 2, S], where=mixers)
        lkT = sb("lkT", [P, 2, S], where=mixers)
        lv = sb("lv", [P, T, COLS], where=mixers)
        cum = sb("cum", [P, 2, S], where=mixers)
        ex = sb("ex", [P, 2, S], where=mixers)
        shared = sb("shared", [P, 5 * COLS], where=mixers)
        qs, ks = (shared[:, i * 1024:(i + 1) * 1024].rearrange("p (b a s) -> p b a s", b=2, a=2) for i in range(2))
        kdn = shared[:, 2048:].rearrange("p (t n) -> p t n", t=T)
        pr = shared[:, 0:12 * P].rearrange("p (b i n) -> p b i n", b=2, i=6)
        prT = shared[:, 12 * P:18 * P].rearrange("p (i n) -> p i n", i=6)
        eG = sb("eG", [P, 2, S], where=mixers)
        qg = sb("qg", [P, 2, S], where=mixers)
        state = sb("state", [P, 3, 2, P], where=mixers)
        slr = sb("slr", [P, T, COLS], where=mixers)
        u_nat = sb("u_nat", [P, T, COLS], where=mixers)
        cgs = sb("cgs", [P, T, COLS], where=mixers)
        uT = sb("uT", [P, CC, S], where=mixers)
        acc = sb("acc", [P, CC, S], where=mixers)
        gate = sb("gate", [P, T, D], where=mixers)
        mixers.close()
        hid_h = sb("hid_h", [P, FF // P, S], F32R)
        hid_l = sb("hid_l", [P, FF // P, S], F32R)
        hid = sb("hid", [P, 2, T, COLS])

        bank = [ctx.enter_context(nc.psum_tensor(f"bank{i}", [P, COLS], F32)) for i in range(8)]

        def param(name, i=0, n=1):
            return pk[:, PACK_AT[name] + i:PACK_AT[name] + i + n]

        decay = cgs[:, 0, :].rearrange("p (a s) -> p a s", a=2)
        decay_e = cgs[:, 1, :].rearrange("p (a s) -> p a s", a=2)
        square = u_nat[:, :, :].rearrange("p t n -> p (t n)").rearrange("p (c s) -> p c s", c=CC)
        exps = [ex[:], decay]
        var, rst, rsc = (cgs[:, i // 2, (i % 2) * S:(i % 2) * S + S] for i in range(3))

        x_in = [signal(f"x_in{t}", 0) for t in range(T)]
        tile0_done = signal("tile0_done", len(GROUPS))
        pos_in = signal("pos_in", 0)
        freq_in = signal("freq_in", 0)
        raw_in = [signal(f"raw_in{i}", 16 * NS // RAW_SLOTS) for i in range(RAW_SLOTS)]
        strip_hi = signal("strip_hi", NS)
        strip_split = signal("strip_split", NS, RAW_SLOTS)
        strip_used = signal("strip_used", NS, SPLIT_SLOTS)
        acc_read = [signal(f"acc_read{i}", len(GROUPS) // 2, 1) for i in range(4)]
        job_done = [signal(f"job_done{i}", JOBS_PER_BANK) for i in range(JOB_BANKS)]
        job_read = [signal(f"job_read{i}", JOBS_PER_BANK, 1) for i in range(JOB_BANKS)]
        job_hi = signal("job_hi", 3 * 2 * T + 2 + PAIRS + 16)
        pk_in = signal("pk_in", 16)
        a2_in = signal("a2_in", 32)
        bg_in = signal("bg_in", 48)
        gpost_in = signal("gpost_in", 32)
        ggla_in = signal("ggla_in", 16)
        la_in = signal("la_in", 16)
        consts = signal("consts", 0)
        ident_in = signal("ident_in", 0)
        pool_steps = signal("pool_steps", 0)
        angles = signal("angles", 0)
        rope_in = signal("rope_in", 0)
        setup_v = signal("setup_v", 0)
        passed = signal("passed", 0)
        layer_in = signal("layer_in", T)
        squares = signal("squares", 2 * T)
        rstd_in = signal("rstd_in", 2)
        la_hi = signal("la_hi", 1)
        la_split = signal("la_split", 1)
        decay_exp = signal("decay_exp", 3)
        cg_sig = signal("cg_sig", 1)
        u_in = signal("u_in", 1)
        rope_out = signal("rope_out", 2)
        expo = signal("expo", 7)
        expd = signal("expd", 7)
        cum_in = signal("cum_in", 1)
        eg_in = signal("eg_in", 1)
        scaled = signal("scaled", 7)
        state_in = signal("state_in", 3)
        p_in = signal("p_in", PAIRS)
        p_exp = signal("p_exp", PAIRS)
        p_recip = signal("p_recip", PAIRS)
        p_norm = signal("p_norm", PAIRS)
        tap0 = signal("tap0", 1)
        g_squares = signal("g_squares", 2)
        lr_sig = signal("lr_sig", T)
        g_ready = signal("g_ready", 1)
        gate_in = signal("gate_in", 6)
        gate_sig = signal("gate_sig", 6)
        mix_in = signal("mix_in", T)
        taps_in = signal("taps_in", 1)
        centred = signal("centred", 1)
        ch_sq = signal("ch_sq", 1)
        ln_in = signal("ln_in", 1)
        ln_sig = signal("ln_sig", 1)
        silu_in = signal("silu_in", 1)
        conv_hi = signal("conv_hi", 1)
        conv_split = signal("conv_split", 1)
        y_squares = signal("y_squares", 4 * T)
        gained = signal("gained", 4 * T)
        resid_in = signal("resid_in", 2 * T)
        hid_sq = signal("hid_sq", 8)
        out_in = signal("out_in", 0)
        V_STEPS, A_STEPS = 420, 30
        v_steps = signal("v_steps", V_STEPS)
        a_steps = signal("a_steps", A_STEPS)

        def job_bank(job):
            return JOB_NO[job] % JOB_BANKS

        def job_ps(job):
            return bank[4 + job_bank(job)]

        def job_k(job):
            return JOB_NO[job] // JOB_BANKS + 1

        def group_bank(g, t):
            return 2 * (GROUP_NO[g] % 2) + t

        def group_ps(g, t):
            return bank[group_bank(g, t)]

        def group_k(g):
            return GROUP_NO[g] // 2 + 1

        def heads(ap, n):
            return ap.rearrange("p (h n) -> p h n", h=n)

        block = ctx.enter_context(nc.Block())

        @block.sync
        def _(sp):
            for t in range(T):
                sp.dma_start(resid[:, t, :], x[0, t * P:(t + 1) * P, :]).then_inc(x_in[t].sem, 16)
            with sp.Fori(0, DEPTH) as l:
                for u, (g, j, first, last) in enumerate(STRIPS):
                    _, w, c0, _, _ = GROUPS[GROUP_NO[g]]
                    sp.wait_ge(*strip_split.at(l, u + 1 - RAW_SLOTS))
                    sp.sem_inc(passed.sem, 1)
                    src = weights[w][bass.ds(l, 1), 256 * j:256 * j + 256, c0:c0 + COLS]
                    sp.dma_start(raw[:, u % RAW_SLOTS], src.rearrange("l (c p) n -> p (l c) n", p=P))\
                        .then_inc(raw_in[u % RAW_SLOTS].sem, 16)
            for t in range(T):
                sp.wait_ge(*resid_in.at(DEPTH - 1, T + t + 1))
                sp.dma_start(out[0, t * P:(t + 1) * P, :], resid[:, t, :]).then_inc(out_in.sem, 16)
            sp.wait_ge(out_in.sem, 16 * T)

        @block.gpsimd
        def _(pool):
            pool.dma_start(pk[:], packed[0]).then_inc(pk_in.sem, 16)
            pool.dma_start(inv_f[:], inv_freq).then_inc(freq_in.sem, 16)
            pool.dma_start(pos_i[:], positions).then_inc(pos_in.sem, 16)

            def load(l, first):
                if not first:
                    pool.wait_ge(*la_split.at(l - 1, 1))
                pool.dma_start(la_raw[:], w_in[bass.ds(l, 1), :, C_LA:C_LA + RANK]
                               .rearrange("l (c p) n -> p (l c) n", p=P)).then_inc(la_in.sem, 16)
                if not first:
                    for j in JOBS_OF["mlp_turn1"]:
                        pool.wait_ge(*job_read[job_bank(j)].at(l - 1, job_k(j)))
                    pool.dma_start(pk[:], packed[bass.ds(l, 1)].rearrange("l p n -> p (l n)")).then_inc(pk_in.sem, 16)
                for i in range(2):
                    pool.dma_start(a2[i * RANK:(i + 1) * RANK, :], w_a2[bass.ds(l, 1)].rearrange("l r n -> r (l n)"))\
                        .then_inc(a2_in.sem, 16)
                pool.dma_start(ggla[:], g_gla[bass.ds(l, 1), :].partition_broadcast(P)).then_inc(ggla_in.sem, 16)
                for n, b in enumerate(BRANCHES):
                    if n:
                        g = f"g{BRANCHES[n - 1]}1"
                        for t in range(T):
                            pool.wait_ge(*acc_read[group_bank(g, t)].at(l, group_k(g)))
                    pool.dma_start(bg[:], b_gate[bass.ds(l, 1), b * D:(b + 1) * D].partition_broadcast(P))\
                        .then_inc(bg_in.sem, 16)
                    if n == 0:
                        if not first:
                            pool.wait_ge(*resid_in.at(l - 1, 2 * T))
                        pool.dma_start(gpost[:], g_mix_post[bass.ds(l, 1), :].partition_broadcast(P))\
                            .then_inc(gpost_in.sem, 16)
                pool.wait_ge(*resid_in.at(l, T))
                pool.dma_start(gpost[:], g_mlp_post[bass.ds(l, 1), :].partition_broadcast(P))\
                    .then_inc(gpost_in.sem, 16)

            steps = 0

            def own(ins):
                nonlocal steps
                ins.then_inc(pool_steps.sem, 1)
                steps += 1
                pool.wait_ge(pool_steps.sem, steps)

            own(pool.memset(ident[:], 0.0))
            own(pool.affine_select(out=ident[:], in_=ident[:], compare_op=ALU.not_equal, fill=1.0, base=0,
                                   pattern=[[-1, P]], channel_multiplier=1))
            pool.sem_inc(ident_in.sem, 1)
            for t in range(T):
                pool.wait_ge(x_in[t].sem, 16)
                pool.sem_inc(layer_in.sem, 1)
            own(pool.memset(over_ch[:], 1.0 / CH))
            own(pool.memset(causal[:], 0.0))
            for i in (0, 2):
                own(pool.affine_select(out=causal[:, i, :], in_=causal[:, i, :], compare_op=ALU.is_ge, fill=NEG,
                                       base=0, pattern=[[-1, P]], channel_multiplier=1))
            own(pool.memset(keep[:], 1.0))
            own(pool.memset(heads(keep[:], 2 * S // CHUNK)[:, :, 0:1], 0.0))
            own(pool.memset(aT[:], 0.0))
            own(pool.memset(lmask[:], 1))
            for n, s in enumerate(LEVELS):
                if s == 0:
                    own(pool.affine_select(out=lmask[:, n, :], in_=lmask[:, n, :], compare_op=ALU.is_equal,
                                           fill=0.0, base=0, pattern=[[-1, P]], channel_multiplier=1))
                    continue
                m = lmask[:, n, :].rearrange("p (b h s) -> p b h s", h=2, s=s)
                own(pool.memset(m[:, :, 0, :], 0))
                own(pool.affine_select(out=m[:, :, 1, :], in_=m[:, :, 1, :], compare_op=ALU.is_ge, fill=0.0,
                                       base=0, pattern=[[-2 * s, P // (2 * s)], [0, s]], channel_multiplier=1))
                own(pool.affine_select(out=m[:, :, 1, :], in_=m[:, :, 1, :], compare_op=ALU.is_ge, fill=0.0,
                                       base=s - 1, pattern=[[2 * s, P // (2 * s)], [0, s]],
                                       channel_multiplier=-1))
            pool.sem_inc(consts.sem, 1)
            load(0, True)
            with pool.Fori(1, DEPTH) as l:
                load(l, False)

        @block.scalar
        def _(act):
            act.sem_inc(strip_used.sem, SPLIT_SLOTS)
            act.wait_ge(angles.sem, 1)
            act.activation(cos_t[:], cos_t[:], ACT.Sin).then_inc(rope_in.sem, 1)
            act.activation(sin_t[:], sin_t[:], ACT.Sin).then_inc(rope_in.sem, 1)
            with act.Fori(0, DEPTH) as l:
                a_count = 0
                hi_count = 0

                def job_wait(job):
                    act.wait_ge(*job_done[job_bank(job)].at(l, job_k(job)))

                def group_wait(g, t):
                    if t == 0:
                        act.wait_ge(*tile0_done.at(l, GROUP_NO[g] + 1))
                    else:
                        act.wait_ge(*strip_used.at(l, LAST_STRIP[g] + 1))

                def own(ins):
                    nonlocal a_count
                    ins.then_inc(a_steps.sem, 1)
                    a_count += 1
                    act.wait_ge(*a_steps.at(l, a_count))

                def row_squares(src, t, c, dst):
                    return act.activation(xs[:, t, c:c + src.shape[-1]], src, ACT.Square, accum_out=dst)

                def turn_hi(jobs, dst):
                    for i, job in enumerate(jobs):
                        job_wait(job)
                        act.activation(dst[:, 2 * i:2 * i + 2, :], heads(job_ps(job)[:], 2), ACT.Copy)\
                            .then_inc(job_hi.sem, 1)

                def tile_hi(jobs, t, gains=None):
                    for i, job in enumerate(jobs):
                        job_wait(job)
                        if gains is None:
                            last = act.activation(act_h[:, 4 * i:4 * i + 4, t * P:(t + 1) * P],
                                                  heads(job_ps(job)[:], 4), ACT.Copy, scale=0.5)
                        else:
                            for c in range(4):
                                last = act.activation(act_h[:, 4 * i + c, t * P:(t + 1) * P],
                                                      job_ps(job)[:, c * P:(c + 1) * P], ACT.Copy,
                                                      scale=param(gains, 4 * i + c))
                        last.then_inc(job_hi.sem, 1)

                def rstd(t):
                    return stats[:, 64 + t:65 + t]

                def half_rstd(t):
                    return stats[:, 66 + t:67 + t]

                for step in PLAN:
                    kind, arg = step if isinstance(step, tuple) else (step, None)
                    n = int(kind[-1]) if kind[-1].isdigit() else None
                    if kind == "hi":
                        act.wait_ge(*raw_in[arg % RAW_SLOTS].at(l, 16 * (arg // RAW_SLOTS + 1)))
                        act.wait_ge(*strip_used.at(l, arg + 1 - SPLIT_SLOTS))
                        act.activation(w_h[:, arg % SPLIT_SLOTS], raw[:, arg % RAW_SLOTS], ACT.Copy)\
                            .then_inc(strip_hi.sem, 1)
                    elif kind == "evac":
                        g, tiles = arg
                        if g == "ca":
                            act.wait_ge(*rstd_in.at(l, 1))
                        elif g == "up0":
                            act.wait_ge(*rstd_in.at(l, 2))
                        if g in ("ca", "lqk", "lv", "mv"):
                            dst = {"ca": u_nat, "lqk": u_nat, "lv": lv, "mv": v}[g]
                            for t in tiles:
                                group_wait(g, t)
                                act.activation(dst[:, t, :], group_ps(g, t)[:], ACT.Copy, scale=rstd(t))\
                                    .then_inc(acc_read[group_bank(g, t)].sem, 1)
                        elif g == "cg":
                            for t in tiles:
                                group_wait(g, t)
                                act.activation(cgs[:, t, :], group_ps(g, t)[:], ACT.Tanh, scale=half_rstd(t))\
                                    .then_inc(acc_read[group_bank(g, t)].sem, 1)
                        elif g == "lr":
                            for t in tiles:
                                group_wait(g, t)
                                act.activation(slr[:, t, :], group_ps(g, t)[:], ACT.Tanh, scale=half_rstd(t))\
                                    .then_inc(lr_sig.sem, 1)
                        elif g[0] == "g":
                            c = int(g[2])
                            act.wait_ge(*gate_in.at(l, 2 * BRANCHES.index(int(g[1])) + c + 1))
                            act.activation(gate[:, :, c * COLS:(c + 1) * COLS], gate[:, :, c * COLS:(c + 1) * COLS],
                                           ACT.Tanh, scale=0.5).then_inc(gate_sig.sem, 1)
                        elif g.startswith("up"):
                            for t in tiles:
                                group_wait(g, t)
                                act.activation(hid[:, int(g[2]) % 2, t, :], group_ps(g, t)[:], ACT.Relu,
                                               scale=rstd(t)).then_inc(acc_read[group_bank(g, t)].sem, 1)
                    elif kind.startswith("squares"):
                        for t in range(T):
                            if n:
                                act.wait_ge(*resid_in.at(l, t + 1))
                            else:
                                act.wait_ge(*layer_in.at(l, t + 1))
                            row_squares(resid[:, t, :], t, 0, stats[:, t:t + 1]).then_inc(squares.sem, 1)
                            act.wait_ge(*squares.at(l, T * n + t + 1))
                    elif kind == "la_round":
                        act.wait_ge(*la_in.at(l, 16))
                        act.activation(la_w[:, :, 0, :], la_raw[:], ACT.Copy).then_inc(la_hi.sem, 1)
                    elif kind == "cumulate":
                        for i in range(2):
                            act.wait_ge(*job_read[job_bank(f"dec{i}")].at(l, job_k(f"dec{i}")))
                        act.activation(decay_e, decay, ACT.Abs).then_inc(decay_exp.sem, 1)
                        act.wait_ge(*decay_exp.at(l, 1))
                        act.activation(decay_e, decay_e, ACT.Exp, scale=-1.0).then_inc(decay_exp.sem, 1)
                        act.wait_ge(*decay_exp.at(l, 2))
                        act.activation(decay_e, decay_e, ACT.Ln, bias=1.0).then_inc(decay_exp.sem, 1)
                    elif kind == "tap" and arg == 0:
                        for c in range(CC):
                            last = act.activation(acc[:, c, :], uT[:, c, :], ACT.Identity,
                                                  scale=param("w_dw", c * TAPS + TAPS - 1), bias=param("b_dw", c))
                        last.then_inc(tap0.sem, 1)
                    elif kind.startswith("level_sub"):
                        act.wait_ge(*expo.at(l, n))
                        act.activation(exps[n % 2], exps[n % 2], ACT.Exp, scale=1.0 / 16.0).then_inc(expd.sem, 1)
                        if n == len(LEVELS):
                            act.activation(eG[:], cum[:], ACT.Exp, scale=1.0 / 16.0).then_inc(eg_in.sem, 1)
                    elif kind.startswith("norm"):
                        act.wait_ge(*p_recip.at(l, n + 1))
                        for i, (lo, hi) in enumerate(ROW_BLOCKS):
                            last = act.activation(pr[:, n % 2, lo:hi, :], pr[:, n % 2, lo:hi, :], ACT.Copy,
                                                  scale=stats[:, 68 + 4 * (n % 2) + i:69 + 4 * (n % 2) + i])
                        last.then_inc(p_norm.sem, 1)
                    elif kind == "ln_affine":
                        act.wait_ge(*ln_in.at(l, 1))
                        for c in range(CC):
                            last = act.activation(acc[:, c, :], acc[:, c, :], ACT.Identity,
                                                  scale=param("g_ln", c), bias=param("b_ln", c))
                        own(last)
                        act.activation(square, acc[:], ACT.Tanh, scale=0.5).then_inc(ln_sig.sem, 1)
                    elif kind == "ln_hi":
                        act.wait_ge(*silu_in.at(l, 1))
                        act.wait_ge(*strip_used.at(l, LAST_STRIP["w11"] + 1))
                        act.activation(brT_h[1][:], acc[:], ACT.Copy, scale=0.5).then_inc(conv_hi.sem, 1)
                    elif kind.startswith(("post_mix", "post_mlp")):
                        m, gs = (0, ("mo0", "mo1")) if kind[:-1] == "post_mix" else (1, ("dn0", "dn1"))
                        k = 2 * (T * m + n)
                        for c, g in enumerate(gs):
                            group_wait(g, n)
                            if c:
                                act.wait_ge(*gained.at(l, k + 1))
                            row_squares(group_ps(g, n)[:], n, c * COLS, stats[:, 4 + 2 * n + c:5 + 2 * n + c])\
                                .then_inc(y_squares.sem, 1)
                        act.wait_ge(*y_squares.at(l, k + 2))
                    elif kind == "use":
                        jobs = JOBS_OF[arg]
                        n = int(arg[-1]) if arg[-1].isdigit() else None
                        if arg.startswith("pre_turn"):
                            if n == 0:
                                act.wait_ge(*pk_in.at(l, 16))
                            tile_hi(jobs, n, "g_mix_pre")
                        elif arg.startswith("mlp_turn"):
                            tile_hi(jobs, n, "g_mlp_pre")
                        elif arg.startswith("mix_turn"):
                            tile_hi(jobs, n)
                        elif arg == "la":
                            job_wait("la")
                            for t in range(T):
                                last = act.activation(la_nat[:, t, :], job_ps("la")[:, 2 * t * RANK:2 * (t + 1) * RANK],
                                                      ACT.Copy, scale=rstd(t))
                            last.then_inc(job_read[job_bank("la")].sem, 1)
                        elif arg == "la_turn":
                            job_wait("laT")
                            act.activation(laT[:], job_ps("laT")[0:2 * RANK, 0:S], ACT.Copy)\
                                .then_inc(job_read[job_bank("laT")].sem, 1)
                        elif arg in ("u_turn", "q_turn", "k_turn"):
                            dst = {"u_turn": uT, "q_turn": qT, "k_turn": kT}[arg]
                            for i, job in enumerate(jobs):
                                job_wait(job)
                                last = act.activation(dst[:, 2 * i:2 * i + 2, :], heads(job_ps(job)[:], 2), ACT.Copy,
                                                      scale=0.5 if arg == "u_turn" else 1.0)
                                last.then_inc(job_read[job_bank(job)].sem, 1)
                            if arg == "u_turn":
                                for job in jobs:
                                    act.wait_ge(*job_read[job_bank(job)].at(l, job_k(job)))
                        elif arg == "l_turn":
                            job_wait("lT0")
                            act.activation(lqT[:], heads(job_ps("lT0")[:], 2), ACT.Copy, scale=GDK ** -0.5)\
                                .then_inc(job_read[job_bank("lT0")].sem, 1)
                            job_wait("lT1")
                            act.activation(lkT[:], heads(job_ps("lT1")[:], 2), ACT.Copy)\
                                .then_inc(job_read[job_bank("lT1")].sem, 1)
                        elif arg == "kd_turn":
                            job_wait("kdT")
                            act.activation(kdn, heads(job_ps("kdT")[:], T), ACT.Copy)\
                                .then_inc(job_read[job_bank("kdT")].sem, 1)
                        elif arg == "g_out":
                            for hh in range(2):
                                job_wait(f"go{hh}")
                                for i in range(2 * T):
                                    last = act.activation(tmp[:, hh, i * GDV:(i + 1) * GDV],
                                                          job_ps(f"go{hh}")[:, i * GDV:(i + 1) * GDV], ACT.Square,
                                                          accum_out=stats[:, 16 + 4 * hh + i:17 + 4 * hh + i])
                                last.then_inc(g_squares.sem, 1)
                        elif arg == "g_turn":
                            turn_hi(jobs, brT_h[1])
                        elif arg.startswith("scores"):
                            b = n % 2
                            act.wait_ge(*p_in.at(l, n + 1))
                            for i, (lo, hi) in enumerate(ROW_BLOCKS):
                                last = act.activation(pr[:, b, lo:hi, :], pr[:, b, lo:hi, :], ACT.Exp,
                                                      bias=stats[:, 40 + 4 * b + i:41 + 4 * b + i],
                                                      scale=DH ** -0.5,
                                                      accum_out=stats[:, 48 + 4 * b + i:49 + 4 * b + i])
                            last.then_inc(p_exp.sem, 1)
                        elif arg.startswith("probs"):
                            for job, lo, hi in ((f"pa_{n}", 0, 4), (f"pb_{n}", 4, 6)):
                                job_wait(job)
                                act.activation(prT[:, lo:hi, :], heads(job_ps(job)[:, 0:(hi - lo) * P], hi - lo),
                                               ACT.Copy).then_inc(job_read[job_bank(job)].sem, 1)
                        elif arg.startswith("values"):
                            job_wait(f"o_{n}")
                            act.activation(brT_h[0][:, n, :], job_ps(f"o_{n}")[:, 0:S], ACT.Copy)\
                                .then_inc(job_hi.sem, 1)
                        elif arg == "ln_mean":
                            act.wait_ge(*centred.at(l, 1))
                            act.activation(square, acc[:], ACT.Square).then_inc(ch_sq.sem, 1)
                        elif arg.startswith("hid_turn"):
                            turn_hi(jobs, hid_h[:, 4 * n:4 * n + 4])
                act.wait_ge(*a_steps.at(l, a_count))
                act.sem_inc(a_steps.sem, A_STEPS - a_count)

        @block.vector
        def _(dve):
            dve.sem_inc(strip_split.sem, RAW_SLOTS)
            for i in range(4):
                dve.sem_inc(acc_read[i].sem, 1)
                dve.sem_inc(job_read[i].sem, 1)

            n_setup = 0

            def own(ins):
                nonlocal n_setup
                ins.then_inc(setup_v.sem, 1)
                n_setup += 1
                dve.wait_ge(setup_v.sem, n_setup)

            TWO_PI = 6.283185307179586
            SMALL = 710.0 - 113 * TWO_PI
            ROUND = 12582912.0
            C1 = 6.28125
            C2 = 0.0019350051879882812
            C3 = TWO_PI - C1 - C2
            LIMIT = 3.1415925
            dve.wait_ge(freq_in.sem, 16)
            dve.wait_ge(pos_in.sem, 16)
            own(dve.tensor_copy(pos_f[:], pos_i[:]))
            ang, k0, k1, kk, off = (rt[:, i] for i in range(5))
            for t in range(T):
                own(dve.tensor_scalar(ang[:, t, :], inv_f[:], pos_f[:, t:t + 1], None, ALU.mult))
            big = 710.0 * 4096
            own(dve.tensor_scalar(k0, ang, 1.0 / big, ROUND, ALU.mult, ALU.add))
            own(dve.tensor_scalar(k0, k0, ROUND, None, ALU.subtract))
            own(dve.scalar_tensor_tensor(out=ang, in0=k0, scalar=-big, in1=ang, op0=ALU.mult, op1=ALU.add))
            own(dve.tensor_scalar(k1, ang, 1.0 / 710.0, ROUND, ALU.mult, ALU.add))
            own(dve.tensor_scalar(k1, k1, ROUND, None, ALU.subtract))
            own(dve.scalar_tensor_tensor(out=ang, in0=k1, scalar=-710.0, in1=ang, op0=ALU.mult, op1=ALU.add))
            own(dve.scalar_tensor_tensor(out=kk, in0=k0, scalar=4096.0, in1=k1, op0=ALU.mult, op1=ALU.add))
            own(dve.tensor_scalar(kk, kk, SMALL, None, ALU.mult))
            own(dve.tensor_tensor(k1, ang, kk, ALU.add))
            for dst, turn, shift in ((sin_t, 0.0, 0.0), (cos_t, 0.25, TWO_PI / 4)):
                own(dve.tensor_scalar(k0, k1, 1.0 / TWO_PI, turn, ALU.mult, ALU.add))
                own(dve.tensor_scalar(k0, k0, ROUND, ROUND, ALU.add, ALU.subtract))
                own(dve.scalar_tensor_tensor(out=off, in0=k0, scalar=-C1, in1=ang, op0=ALU.mult, op1=ALU.add))
                own(dve.scalar_tensor_tensor(out=off, in0=k0, scalar=-C2, in1=off, op0=ALU.mult, op1=ALU.add))
                own(dve.scalar_tensor_tensor(out=off, in0=k0, scalar=-C3, in1=off, op0=ALU.mult, op1=ALU.add))
                own(dve.tensor_tensor(off, off, kk, ALU.add))
                own(dve.tensor_scalar(off, off, shift, LIMIT, ALU.add, ALU.min))
                own(dve.tensor_scalar(dst[:], off, -LIMIT, None, ALU.max))
            dve.sem_inc(angles.sem, 1)
            dve.wait_ge(consts.sem, 1)
            dve.wait_ge(rope_in.sem, 2)

            with dve.Fori(0, DEPTH) as l:
                count = 0
                hi_count = 0

                def step_done(ins):
                    nonlocal count
                    ins.then_inc(v_steps.sem, 1)
                    count += 1
                    return count

                def after(k):
                    dve.wait_ge(*v_steps.at(l, k))

                def chain(ins):
                    after(step_done(ins))

                def job_wait(job):
                    dve.wait_ge(*job_done[job_bank(job)].at(l, job_k(job)))

                def group_wait(g, t):
                    if t == 0:
                        dve.wait_ge(*tile0_done.at(l, GROUP_NO[g] + 1))
                    else:
                        dve.wait_ge(*strip_used.at(l, LAST_STRIP[g] + 1))

                def rstd(t):
                    return stats[:, 64 + t:65 + t]

                def rsqrt(v_, y, s_):
                    chain(dve.tensor_scalar(y.bitcast(I32), v_.bitcast(I32), -0.5, 1597463007.0,
                                            ALU.mult, ALU.add))
                    for _ in range(3):
                        chain(dve.scalar_tensor_tensor(out=s_, in0=v_, scalar=-0.5, in1=y, op0=ALU.mult,
                                                       op1=ALU.mult))
                        chain(dve.tensor_tensor(s_, s_, y, ALU.mult))
                        chain(dve.scalar_tensor_tensor(out=y, in0=s_, scalar=1.5, in1=y, op0=ALU.add,
                                                       op1=ALU.mult))

                def turn_lo(jobs, hi, lo):
                    nonlocal hi_count
                    for i, job in enumerate(jobs):
                        hi_count += 1
                        dve.wait_ge(*job_hi.at(l, hi_count))
                        dve.tensor_tensor(lo[:, 2 * i:2 * i + 2, :], heads(job_ps(job)[:], 2),
                                          hi[:, 2 * i:2 * i + 2, :].bitcast(F32), ALU.subtract)\
                            .then_inc(job_read[job_bank(job)].sem, 1)

                def tile_lo(jobs, t, gains=None):
                    nonlocal hi_count
                    for i, job in enumerate(jobs):
                        hi_count += 1
                        dve.wait_ge(*job_hi.at(l, hi_count))
                        cols = slice(t * P, (t + 1) * P)
                        if gains is None:
                            last = dve.scalar_tensor_tensor(
                                out=act_l[:, 4 * i:4 * i + 4, cols], in0=heads(job_ps(job)[:], 4), scalar=0.5,
                                in1=act_h[:, 4 * i:4 * i + 4, cols].bitcast(F32), op0=ALU.mult, op1=ALU.subtract)
                        else:
                            for c in range(4):
                                last = dve.scalar_tensor_tensor(
                                    out=act_l[:, 4 * i + c, cols], in0=job_ps(job)[:, c * P:(c + 1) * P],
                                    scalar=param(gains, 4 * i + c), in1=act_h[:, 4 * i + c, cols].bitcast(F32),
                                    op0=ALU.mult, op1=ALU.subtract)
                        last.then_inc(job_read[job_bank(job)].sem, 1)

                tap_no = {}
                for step in PLAN:
                    kind, arg = step if isinstance(step, tuple) else (step, None)
                    n = int(kind[-1]) if kind[-1].isdigit() else None
                    if kind == "lo":
                        dve.wait_ge(*strip_hi.at(l, arg + 1))
                        dve.tensor_tensor(w_l[:, arg % SPLIT_SLOTS], raw[:, arg % RAW_SLOTS],
                                          w_h[:, arg % SPLIT_SLOTS].bitcast(F32), ALU.subtract)\
                            .then_inc(strip_split.sem, 1)
                    elif kind == "evac":
                        g, tiles = arg
                        if g == "cg":
                            for t in tiles:
                                dve.wait_ge(*acc_read[group_bank("ca", t)].at(l, group_k("ca")))
                                dve.wait_ge(*acc_read[group_bank("cg", t)].at(l, group_k("cg")))
                            dve.scalar_tensor_tensor(out=u_nat[:], in0=cgs[:], scalar=1.0, in1=u_nat[:], op0=ALU.add,
                                                     op1=ALU.mult).then_inc(u_in.sem, 1)
                        elif g in ("mq", "mk"):
                            at = 0 if g == "mq" else 512
                            for t in tiles:
                                src = heads(group_ps(g, t)[:], 2 * HEADS)
                                c_b = cos_t[:, t:t + 1, :].to_broadcast([P, 2 * HEADS, HALF])
                                s_b = sin_t[:, t:t + 1, :].to_broadcast([P, 2 * HEADS, HALF])
                                xc = tmp[:, 0, :]
                                xn = tmp[:, 1, :]
                                if t:
                                    after(count)
                                elif g == "mk":
                                    dve.wait_ge(*rope_out.at(l, 1))
                                group_wait(g, t)
                                step_done(dve.scalar_tensor_tensor(out=heads(xc, 2 * HEADS), in0=src, scalar=rstd(t),
                                                                   in1=c_b, op0=ALU.mult, op1=ALU.mult))
                                dve.scalar_tensor_tensor(out=heads(xn, 2 * HEADS), in0=src, scalar=rstd(t), in1=s_b,
                                                         op0=ALU.mult, op1=ALU.mult)\
                                    .then_inc(acc_read[group_bank(g, t)].sem, 1)
                                after(count)
                                dve.wait_ge(*acc_read[group_bank(g, t)].at(l, group_k(g)))
                                xc4 = xc.rearrange("p (h two n) -> p h two n", two=2, n=HALF)
                                xn4 = xn.rearrange("p (h two n) -> p h two n", two=2, n=HALF)
                                dst = xs[:, t, at:at + 512].rearrange("p (h two n) -> p h two n", two=2, n=HALF)
                                dve.tensor_tensor(dst[:, :, 0, :], xc4[:, :, 0, :], xn4[:, :, 1, :], ALU.subtract)
                                last = dve.tensor_tensor(dst[:, :, 1, :], xc4[:, :, 1, :], xn4[:, :, 0, :],
                                                         ALU.add)
                                if t == 0:
                                    step_done(last)
                            last.then_inc(rope_out.sem, 1)
                        elif g == "lr":
                            dve.wait_ge(*ggla_in.at(l, 16))
                            for t in tiles:
                                dve.wait_ge(*lr_sig.at(l, t + 1))
                                step_done(dve.scalar_tensor_tensor(
                                    out=heads(slr[:, t, :], GH), in0=heads(slr[:, t, :], GH), scalar=1.0,
                                    in1=ggla[:, :].rearrange("p (a n) -> p a n", a=1).to_broadcast([P, GH, GDV]),
                                    op0=ALU.add, op1=ALU.mult))
                            for t in tiles:
                                after(count - T + 1 + t)
                                dve.scalar_tensor_tensor(out=slr[:, t, :], in0=group_ps(g, t)[:], scalar=rstd(t),
                                                         in1=slr[:, t, :], op0=ALU.mult, op1=ALU.mult)\
                                    .then_inc(acc_read[group_bank(g, t)].sem, 1)
                        elif g[0] == "g":
                            b, c = BRANCHES.index(int(g[1])), int(g[2])
                            dve.wait_ge(*bg_in.at(l, 16 * (b + 1)))
                            for t in tiles:
                                group_wait(g, t)
                                dve.scalar_tensor_tensor(out=gate[:, t, c * COLS:(c + 1) * COLS],
                                                         in0=group_ps(g, t)[:], scalar=rstd(t),
                                                         in1=bg[:, c * COLS:(c + 1) * COLS], op0=ALU.mult,
                                                         op1=ALU.add).then_inc(acc_read[group_bank(g, t)].sem, 1)
                            for t in tiles:
                                dve.wait_ge(*acc_read[group_bank(g, t)].at(l, group_k(g)))
                            dve.sem_inc(gate_in.sem, 1)
                        elif g[0] == "w":
                            b, c = BRANCHES.index(int(g[1])), int(g[2])
                            dve.wait_ge(*gate_sig.at(l, 2 * b + c + 1))
                            for t in tiles:
                                group_wait(g, t)
                                dve.scalar_tensor_tensor(
                                    out=tmp[:, t, :] if b else xs[:, t, c * COLS:(c + 1) * COLS],
                                    in0=gate[:, t, c * COLS:(c + 1) * COLS], scalar=1.0, in1=group_ps(g, t)[:],
                                    op0=ALU.add, op1=ALU.mult).then_inc(acc_read[group_bank(g, t)].sem, 1)
                            for t in tiles:
                                mix = xs[:, t, c * COLS:(c + 1) * COLS]
                                dve.wait_ge(*acc_read[group_bank(g, t)].at(l, group_k(g)))
                                if b:
                                    last = dve.tensor_tensor(mix, mix, tmp[:, t, :], ALU.add)
                                    if (b, c) == (2, 1):
                                        last.then_inc(mix_in.sem, 1)
                                    else:
                                        chain(last)
                        elif g.startswith("up"):
                            for t in tiles:
                                dve.wait_ge(*acc_read[group_bank(g, t)].at(l, group_k(g)))
                            h = hid[:, int(g[2]) % 2]
                            dve.tensor_tensor(h, h, h, ALU.mult).then_inc(hid_sq.sem, 1)
                    elif kind.startswith("rstd"):
                        dve.wait_ge(*squares.at(l, T * (n + 1)))
                        chain(dve.tensor_scalar(stats[:, 2:4], stats[:, 0:2], 1.0 / D, EPS, ALU.mult, ALU.add))
                        rsqrt(stats[:, 2:4], stats[:, 64:66], stats[:, 66:68])
                        chain(dve.tensor_scalar(stats[:, 66:68], stats[:, 64:66], 0.5, None, ALU.mult))
                        dve.sem_inc(rstd_in.sem, 1)
                    elif kind == "la_round":
                        dve.wait_ge(*la_hi.at(l, 1))
                        dve.tensor_tensor(la_w[:, :, 1, :], la_raw[:], la_w[:, :, 0, :].bitcast(F32), ALU.subtract)\
                            .then_inc(la_split.sem, 1)
                    elif kind == "cumulate":
                        dve.wait_ge(*decay_exp.at(l, 3))
                        chain(dve.scalar_tensor_tensor(out=ex[:], in0=decay, scalar=0.0, in1=decay_e,
                                                       op0=ALU.min, op1=ALU.subtract))
                        dve.tensor_tensor_scan(cum[:].rearrange("p a s -> p (a s)"), keep[:],
                                               ex[:].rearrange("p a s -> p (a s)"), 0.0, ALU.mult, ALU.add)\
                            .then_inc(cum_in.sem, 1)
                        dve.wait_ge(*cum_in.at(l, 1))
                    elif kind.startswith("level_sub"):
                        if n > 2:
                            dve.wait_ge(*scaled.at(l, n - 2))
                        if n == len(LEVELS):
                            g3 = cum[:].rearrange("p a (b c) -> p (a b) c", c=CHUNK)
                            end = g3[:, :, CHUNK - 1:CHUNK].broadcast_to([P, 2 * S // CHUNK, CHUNK])
                            dve.tensor_tensor(exps[n % 2].rearrange("p a (b c) -> p (a b) c", c=CHUNK), end, g3,
                                              ALU.subtract).then_inc(expo.sem, 1)
                        else:
                            s = LEVELS[n]
                            g4 = cum[:].rearrange("p a (b h s) -> p (a b) h s", h=2, s=s)
                            e4 = exps[n % 2].rearrange("p a (b h s) -> p (a b) h s", h=2, s=s)
                            ref = g4[:, :, 0, s - 1:s].broadcast_to([P, 2 * S // (2 * s), s])
                            dve.tensor_tensor(e4[:, :, 0, :], ref, g4[:, :, 0, :], ALU.subtract)
                            dve.tensor_tensor(e4[:, :, 1, :], g4[:, :, 1, :], ref, ALU.subtract)\
                                .then_inc(expo.sem, 1)
                    elif kind.startswith("level_mul"):
                        dve.wait_ge(*expd.at(l, n))
                        if n > 2:
                            for hh in range(2):
                                job = f"lev{n - 2}_{hh}"
                                dve.wait_ge(*job_done[job_bank(job)].at(l, job_k(job)))
                        else:
                            for job in ("lT0", "lT1"):
                                dve.wait_ge(*job_read[job_bank(job)].at(l, job_k(job)))
                        dve.tensor_tensor(qs[:, n % 2], lqT[:], exps[n % 2], ALU.mult)
                        dve.tensor_tensor(ks[:, n % 2], lkT[:], exps[n % 2], ALU.mult).then_inc(scaled.sem, 1)
                    elif kind == "inter_mul":
                        dve.wait_ge(*eg_in.at(l, 1))
                        dve.tensor_tensor(qg[:], lqT[:], eG[:], ALU.mult)
                        dve.wait_ge(*expd.at(l, len(LEVELS)))
                        dve.tensor_tensor(ks[:, 1], lkT[:], exps[1], ALU.mult).then_inc(scaled.sem, 1)
                    elif kind == "g_rstd":
                        dve.wait_ge(*g_squares.at(l, 2))
                        m = T * GH
                        chain(dve.tensor_scalar(stats[:, 24:24 + m], stats[:, 16:16 + m], 4.0 / GDV, 4.0 * EPS,
                                                ALU.mult, ALU.add))
                        rsqrt(stats[:, 24:24 + m], stats[:, 32:32 + m], stats[:, 16:16 + m])
                    elif kind == "g_scale":
                        for hh in range(2):
                            for i in range(2 * T):
                                t, h = i // 2, 2 * (i % 2) + hh
                                blk = slr[:, t, h * GDV:(h + 1) * GDV]
                                at = 32 + 4 * hh + i
                                last = dve.scalar_tensor_tensor(
                                    out=blk, in0=job_ps(f"go{hh}")[:, i * GDV:(i + 1) * GDV],
                                    scalar=stats[:, at:at + 1], in1=blk, op0=ALU.mult, op1=ALU.mult)
                            last.then_inc(job_read[job_bank(f"go{hh}")].sem, 1)
                    elif kind.startswith("norm"):
                        dve.wait_ge(*p_exp.at(l, n + 1))
                        dve.reciprocal(stats[:, 68 + 4 * (n % 2):72 + 4 * (n % 2)],
                                       stats[:, 48 + 4 * (n % 2):52 + 4 * (n % 2)]).then_inc(p_recip.sem, 1)
                    elif kind == "tap" and arg:
                        k = arg
                        if k == 1:
                            dve.wait_ge(*tap0.at(l, 1))
                        for c in range(CC):
                            if k > 1:
                                after(tap_no[c])
                            ins = dve.scalar_tensor_tensor(
                                out=acc[:, c, k:], in0=uT[:, c, 0:S - k],
                                scalar=param("w_dw", c * TAPS + TAPS - 1 - k), in1=acc[:, c, k:], op0=ALU.mult,
                                op1=ALU.add)
                            if k == TAPS - 1 and c == CC - 1:
                                ins.then_inc(taps_in.sem, 1)
                            else:
                                tap_no[c] = step_done(ins)
                    elif kind == "ln_silu":
                        dve.wait_ge(*ln_sig.at(l, 1))
                        dve.scalar_tensor_tensor(out=acc[:], in0=square, scalar=1.0, in1=acc[:], op0=ALU.add,
                                                 op1=ALU.mult).then_inc(silu_in.sem, 1)
                    elif kind == "ln_lo":
                        dve.wait_ge(*conv_hi.at(l, 1))
                        dve.scalar_tensor_tensor(out=brT_l[1][:], in0=acc[:], scalar=0.5,
                                                 in1=brT_h[1][:].bitcast(F32), op0=ALU.mult, op1=ALU.subtract)\
                            .then_inc(conv_split.sem, 1)
                    elif kind.startswith(("post_mix", "post_mlp")):
                        m, gs = (0, ("mo0", "mo1")) if kind[:-1] == "post_mix" else (1, ("dn0", "dn1"))
                        dve.wait_ge(*gpost_in.at(l, 16 * (m + 1)))
                        k = 2 * (T * m + n)
                        for c in (1, 0):
                            group_wait(gs[c], n)
                            if c == 0:
                                dve.wait_ge(*y_squares.at(l, k + 1))
                            dve.tensor_tensor(tmp[:, c, :], group_ps(gs[c], n)[:], gpost[:, c * COLS:(c + 1) * COLS],
                                              ALU.mult).then_inc(gained.sem, 1)
                        dve.wait_ge(*y_squares.at(l, k + 2))
                        dve.wait_ge(*gained.at(l, k + 2))
                        y2 = stats[:, 4 + 2 * n:6 + 2 * n]
                        va, y, tm = (stats[:, 8 + 3 * n + i:9 + 3 * n + i] for i in range(3))
                        chain(dve.tensor_tensor(va, y2[:, 0:1], y2[:, 1:2], ALU.add))
                        for g in gs:
                            dve.sem_inc(acc_read[group_bank(g, n)].sem, 1)
                        chain(dve.tensor_scalar(va, va, 1.0 / D, EPS, ALU.mult, ALU.add))
                        rsqrt(va, y, tm)
                        dve.scalar_tensor_tensor(out=resid[:, n, :], in0=tmp[:].rearrange("p t n -> p (t n)"), scalar=y,
                                                 in1=resid[:, n, :], op0=ALU.mult, op1=ALU.add)\
                            .then_inc(resid_in.sem, 1)
                        dve.wait_ge(*resid_in.at(l, T * m + n + 1))
                        if m:
                            dve.sem_inc(layer_in.sem, 1)
                    elif kind == "use":
                        jobs = JOBS_OF[arg]
                        n = int(arg[-1]) if arg[-1].isdigit() else None
                        if arg.startswith("pre_turn"):
                            if n == 0:
                                dve.wait_ge(*pk_in.at(l, 16))
                            tile_lo(jobs, n, "g_mix_pre")
                        elif arg.startswith("mlp_turn"):
                            tile_lo(jobs, n, "g_mlp_pre")
                        elif arg.startswith("mix_turn"):
                            tile_lo(jobs, n)
                        elif arg == "decay":
                            dve.wait_ge(*u_in.at(l, 1))
                            for i, job in enumerate(jobs):
                                job_wait(job)
                                dve.tensor_scalar(decay[:, i, :], job_ps(job)[:, 0:S], param("b_gla", i), None,
                                                  ALU.add).then_inc(job_read[job_bank(job)].sem, 1)
                        elif arg.startswith("level"):
                            for hh, job in enumerate(jobs):
                                job_wait(job)
                                if n:
                                    before = f"lev{n - 1}_{hh}"
                                    dve.wait_ge(*job_read[job_bank(before)].at(l, job_k(before)))
                                dve.sem_inc(passed.sem, 1)
                                dve.copy_predicated(aT[:, hh], lmask[:, n:n + 1, :].to_broadcast([P, 2 * T, P]),
                                                    heads(job_ps(job)[:], 2 * T))\
                                    .then_inc(job_read[job_bank(job)].sem, 1)
                        elif arg.startswith("state"):
                            job_wait(f"st{n}")
                            for p in range(2):
                                ps = job_ps(f"st{n}")[:, p * P:(p + 1) * P]
                                if n == 0:
                                    last = dve.tensor_copy(state[:, 0, p, :], ps)
                                else:
                                    last = dve.scalar_tensor_tensor(
                                        out=state[:, n, p, :], in0=state[:, n - 1, p, :],
                                        scalar=eG[:, p, n * CHUNK + CHUNK - 1:n * CHUNK + CHUNK], in1=ps,
                                        op0=ALU.mult, op1=ALU.add)
                                if p == 0:
                                    step_done(last)
                            last.then_inc(state_in.sem, 1)
                            dve.wait_ge(*state_in.at(l, n + 1))
                            dve.sem_inc(job_read[job_bank(f"st{n}")].sem, 1)
                        elif arg == "g_turn":
                            turn_lo(jobs, brT_h[1], brT_l[1])
                        elif arg.startswith("scores"):
                            b = n % 2
                            for hh, job in enumerate(jobs):
                                job_wait(job)
                                dve.tensor_tensor(pr[:, b, 3 * hh:3 * hh + 3, :], heads(job_ps(job)[:, 0:3 * P], 3),
                                                  causal[:], ALU.add).then_inc(job_read[job_bank(job)].sem, 1)
                            for job in jobs:
                                dve.wait_ge(*job_read[job_bank(job)].at(l, job_k(job)))
                            rows = pr[:, b].rearrange("p (h c) n -> p h c n", h=2)
                            step_done(dve.tensor_reduce(stats[:, 56:58], rows[:, :, 0, :], AX.X, ALU.max))
                            chain(dve.tensor_reduce(stats[:, 58:60],
                                                    rows[:, :, 1:3, :].rearrange("p h c n -> p h (c n)"),
                                                    AX.X, ALU.max))
                            dve.tensor_scalar(stats[:, 40 + 4 * b:44 + 4 * b], stats[:, 56:60], -(DH ** -0.5), None,
                                              ALU.mult).then_inc(p_in.sem, 1)
                        elif arg.startswith("values"):
                            hi_count += 1
                            dve.wait_ge(*job_hi.at(l, hi_count))
                            dve.tensor_tensor(brT_l[0][:, n, :], job_ps(f"o_{n}")[:, 0:S],
                                              brT_h[0][:, n, :].bitcast(F32), ALU.subtract)\
                                .then_inc(job_read[job_bank(f"o_{n}")].sem, 1)
                        elif arg == "ln_mean":
                            job_wait("mu")
                            dve.tensor_tensor(acc[:], acc[:], job_ps("mu")[:, 0:S]
                                              .rearrange("p (a n) -> p a n", a=1)
                                              .to_broadcast([P, CC, S]), ALU.subtract).then_inc(centred.sem, 1)
                            dve.wait_ge(*centred.at(l, 1))
                            dve.sem_inc(job_read[job_bank("mu")].sem, 1)
                        elif arg == "ln_var":
                            job_wait("var")
                            dve.tensor_scalar(var, job_ps("var")[:, 0:S], EPS, None, ALU.add)\
                                .then_inc(job_read[job_bank("var")].sem, 1)
                            dve.wait_ge(*job_read[job_bank("var")].at(l, job_k("var")))
                            rsqrt(var, rst, rsc)
                            dve.tensor_tensor(acc[:], acc[:], rst.rearrange("p (a n) -> p a n", a=1)
                                              .to_broadcast([P, CC, S]), ALU.mult).then_inc(ln_in.sem, 1)
                        elif arg.startswith("hid_turn"):
                            turn_lo(jobs, hid_h[:, 4 * n:4 * n + 4], hid_l[:, 4 * n:4 * n + 4])
                after(count)
                assert count < V_STEPS, count
                dve.sem_inc(v_steps.sem, V_STEPS - count)

        @block.tensor
        def _(pe):
            pe.wait_ge(ident_in.sem, 1)
            with pe.Fori(0, DEPTH) as l:

                def job_start(job):
                    pe.wait_ge(*job_read[job_bank(job)].at(l, job_k(job) - 1))
                    return job_ps(job)

                def job_end(job, last):
                    last.then_inc(job_done[job_bank(job)].sem, 1)

                def jobs_read(jobs, before=None):
                    for job in {job_bank(j_): j_ for j_ in jobs}.values():
                        if before is None or job_bank(job) != job_bank(before):
                            pe.wait_ge(*job_read[job_bank(job)].at(l, job_k(job)))

                def turn(jobs, src):
                    for i, job in enumerate(jobs):
                        ps = job_start(job)
                        for c in range(2):
                            for t in range(T):
                                last = pe.transpose(ps[:, c * S + t * P:c * S + (t + 1) * P],
                                                    src[:, t, (2 * i + c) * P:(2 * i + c + 1) * P], ident[:])
                        job_end(job, last)

                def turn_tile(jobs, src, t):
                    for i, job in enumerate(jobs):
                        ps = job_start(job)
                        for c in range(4):
                            last = pe.transpose(ps[:, c * P:(c + 1) * P],
                                                src[:, t, (4 * i + c) * P:(4 * i + c + 1) * P], ident[:])
                        job_end(job, last)

                for step in PLAN:
                    kind, arg = step if isinstance(step, tuple) else (step, None)
                    if kind == "mm":
                        u, t = arg
                        g, j, first, last_of = STRIPS[u]
                        lhs = GROUPS[GROUP_NO[g]][4]
                        if first:
                            if lhs == "branch0":
                                jobs_read([f"o_{p}" for p in range(PAIRS)])
                            elif lhs == "branch1":
                                jobs_read(JOBS_OF["g_turn"])
                            elif lhs == "branch2":
                                pe.wait_ge(*conv_split.at(l, 1))
                            elif g in ("ca", "mo0", "up0"):
                                jobs_read(JOBS_OF[{"ca": "pre", "mo0": "mix", "up0": "mlp"}[g] + f"_turn{t}"])
                            pe.wait_ge(*acc_read[group_bank(g, t)].at(l, group_k(g) - 1))
                        if g == "dn0" and j % 2 == 0:
                            jobs_read(JOBS_OF[f"hid_turn{j // 2}"])
                        a_h, a_l = {"act": (act_h, act_l), "branch0": (brT_h[0], brT_l[0]),
                                    "branch1": (brT_h[1], brT_l[1]), "branch2": (brT_h[1], brT_l[1]),
                                    "hid": (hid_h, hid_l)}[lhs]
                        if t == 0:
                            pe.wait_ge(*strip_split.at(l, u + 1))
                        ps = group_ps(g, t)[:]
                        for c in range(2):
                            s_h = a_h[:, 2 * j + c, t * P:(t + 1) * P]
                            s_l = a_l[:, 2 * j + c, t * P:(t + 1) * P]
                            r_h = w_h[:, u % SPLIT_SLOTS, c, :]
                            r_l = w_l[:, u % SPLIT_SLOTS, c, :]
                            pe.matmul(ps, s_h, r_h, start=first and c == 0, stop=False)
                            pe.matmul(ps, s_h, r_l, start=False, stop=False)
                            last = pe.matmul(ps, s_l, r_h, start=False, stop=last_of and c == 1)
                        if t == T - 1:
                            last.then_inc(strip_used.sem, 1)
                        elif last_of:
                            last.then_inc(tile0_done.sem, 1)
                    elif kind.startswith("pre_turn"):
                        t = int(kind[-1])
                        pe.wait_ge(*layer_in.at(l, t + 1))
                        turn_tile(JOBS_OF[kind], resid, t)
                    elif kind.startswith("mlp_turn"):
                        t = int(kind[-1])
                        pe.wait_ge(*resid_in.at(l, t + 1))
                        turn_tile(JOBS_OF[kind], resid, t)
                    elif kind.startswith("mix_turn"):
                        t = int(kind[-1])
                        pe.wait_ge(*mix_in.at(l, t + 1))
                        turn_tile(JOBS_OF[kind], xs, t)
                    elif kind == "la":
                        ps = job_start("la")
                        pe.wait_ge(*la_split.at(l, 1))
                        for t in range(T):
                            for c in range(KC):
                                s_h = act_h[:, c, t * P:(t + 1) * P]
                                s_l = act_l[:, c, t * P:(t + 1) * P]
                                dst = ps[:, 2 * t * RANK:2 * (t + 1) * RANK]
                                pe.matmul(dst, s_h, la_w[:, c].rearrange("p a r -> p (a r)"), start=c == 0,
                                          stop=False, skip_group_check=True)
                                last = pe.matmul(dst[:, 0:RANK], s_l, la_w[:, c, 0, :], start=False,
                                                 stop=c == KC - 1, skip_group_check=True)
                        job_end("la", last)
                    elif kind == "la_turn":
                        ps = job_start("laT")
                        jobs_read(["la"], "laT")
                        for t in range(T):
                            last = pe.transpose(ps[0:2 * RANK, t * P:(t + 1) * P], la_nat[:, t, :], ident[:])
                        job_end("laT", last)
                    elif kind == "decay":
                        jobs_read(["laT"], "dec0")
                        pe.wait_ge(*a2_in.at(l, 32))
                        for i in range(2):
                            ps = job_start(f"dec{i}")
                            job_end(f"dec{i}", pe.matmul(ps[:, 0:S], a2[:, i * P:(i + 1) * P], laT[:],
                                                         start=True, stop=True))
                    elif kind == "u_turn":
                        pe.wait_ge(*u_in.at(l, 1))
                        turn(JOBS_OF[kind], u_nat)
                    elif kind == "l_turn":
                        for t in range(T):
                            pe.wait_ge(*acc_read[group_bank("lqk", t)].at(l, group_k("lqk")))
                        turn(JOBS_OF[kind], u_nat)
                    elif kind in JOBS_OF and kind.startswith("level"):
                        n = int(kind[5:])
                        if n:
                            pe.wait_ge(*scaled.at(l, n))
                        else:
                            jobs_read(["lT0", "lT1"], "lev0_0")
                        q_, k_ = (qs[:, n % 2], ks[:, n % 2]) if n else (lqT, lkT)
                        for hh in range(2):
                            ps = job_start(f"lev{n}_{hh}")
                            rows = slice(GDK * hh, GDK * hh + GDK)
                            for i in range(2 * T):
                                t, p = i // 2, i % 2
                                last = pe.matmul(ps[:, i * P:(i + 1) * P], k_[rows, p, t * P:(t + 1) * P],
                                                 q_[rows, p, t * P:(t + 1) * P], start=True, stop=True)
                            job_end(f"lev{n}_{hh}", last)
                    elif kind == "kd_turn":
                        pe.wait_ge(*scaled.at(l, 7))
                        ps = job_start("kdT")
                        for t in range(T):
                            for p in range(2):
                                last = pe.transpose(ps[:, t * S + p * P:t * S + (p + 1) * P],
                                                    ks[:, 1, p, t * P:(t + 1) * P], ident[:])
                        job_end("kdT", last)
                    elif kind.startswith("state"):
                        c = int(kind[5:])
                        ps = job_start(f"st{c}")
                        jobs_read(["kdT"], f"st{c}")
                        for t in range(T):
                            pe.wait_ge(*acc_read[group_bank("lv", t)].at(l, group_k("lv")))
                        pe.sem_inc(passed.sem, 1)
                        rows = slice(CHUNK * (c % 2), CHUNK * (c % 2) + CHUNK)
                        for h in range(GH):
                            p, hh = h // 2, h % 2
                            last = pe.matmul(ps[GDK * hh:GDK * hh + GDK, p * P:(p + 1) * P],
                                             kdn[rows, c // 2, h * GDK:(h + 1) * GDK],
                                             lv[rows, c // 2, h * GDV:(h + 1) * GDV], start=True, stop=True)
                        job_end(f"st{c}", last)
                    elif kind == "g_out":
                        for hh in range(2):
                            ps = job_start(f"go{hh}")
                            if hh == 0:
                                pe.wait_ge(*state_in.at(l, 3))
                                jobs_read([f"lev{len(LEVELS) - 1}_{i}" for i in range(2)], "go0")
                            rows = slice(GDK * hh, GDK * hh + GDK)
                            for i in range(2 * T):
                                t, p = i // 2, i % 2
                                h = 2 * p + hh
                                cols = slice(i * GDV, (i + 1) * GDV)
                                pe.matmul(ps[:, cols], aT[:, hh, i, :], lv[:, t, h * GDV:(h + 1) * GDV], start=True,
                                          stop=False, skip_group_check=True)
                                for c in range(2 * t, 2 * t + 2):
                                    if c:
                                        o_rows = slice(CHUNK * (c % 2), CHUNK * (c % 2) + CHUNK)
                                        last = pe.matmul(ps[o_rows, cols], qg[rows, p, c * CHUNK:(c + 1) * CHUNK],
                                                         state[rows, c - 1, p, :], start=False, stop=c % 2 == 1,
                                                         skip_group_check=True)
                            job_end(f"go{hh}", last)
                    elif kind == "g_turn":
                        jobs_read(["go0", "go1"], "gT0")
                        turn(JOBS_OF[kind], slr)
                    elif kind in ("q_turn", "k_turn"):
                        n = 0 if kind == "q_turn" else 1
                        pe.wait_ge(*rope_out.at(l, n + 1))
                        turn(JOBS_OF[kind], xs[:, :, n * 512:n * 512 + 512])
                    elif kind.startswith("scores"):
                        p = int(kind[6:])
                        if p == 0:
                            jobs_read(JOBS_OF["q_turn"] + JOBS_OF["k_turn"], "s0_0")
                        for hh in range(2):
                            job = f"s{hh}_{p}"
                            ps = job_start(job)
                            rows = slice(DH * hh, DH * hh + DH)
                            for t in range(T):
                                last = pe.matmul(ps[:, t * P:t * P + (t + 1) * P], qT[rows, p, t * P:(t + 1) * P],
                                                 kT[rows, p, 0:(t + 1) * P], start=True, stop=True)
                            job_end(job, last)
                    elif kind.startswith("probs"):
                        p = int(kind[5:])
                        pe.wait_ge(*p_norm.at(l, p + 1))
                        for job, lo, hi in ((f"pa_{p}", 0, 4), (f"pb_{p}", 4, 6)):
                            ps = job_start(job)
                            for i in range(lo, hi):
                                last = pe.transpose(ps[:, (i - lo) * P:(i - lo + 1) * P], pr[:, p % 2, i, :], ident[:])
                            job_end(job, last)
                    elif kind.startswith("values"):
                        p = int(kind[6:])
                        jobs_read([f"pa_{p}", f"pb_{p}"], f"o_{p}")
                        if p == 0:
                            for t in range(T):
                                pe.wait_ge(*acc_read[group_bank("mv", t)].at(l, group_k("mv")))
                        ps = job_start(f"o_{p}")
                        for hh in range(2):
                            h = 2 * p + hh
                            o_rows = slice(DH * hh, DH * hh + DH)
                            cols = slice(h * DH, (h + 1) * DH)
                            pe.matmul(ps[o_rows, 0:P], v[:, 0, cols], prT[:, 3 * hh, :], start=True, stop=True,
                                      skip_group_check=True)
                            pe.matmul(ps[o_rows, P:S], v[:, 0, cols], prT[:, 3 * hh + 1, :], start=True, stop=False,
                                      skip_group_check=True)
                            last = pe.matmul(ps[o_rows, P:S], v[:, 1, cols], prT[:, 3 * hh + 2, :], start=False,
                                             stop=True, skip_group_check=True)
                        job_end(f"o_{p}", last)
                    elif kind == "ln_mean":
                        pe.wait_ge(*taps_in.at(l, 1))
                        ps = job_start("mu")
                        for c in range(CC):
                            last = pe.matmul(ps[:, 0:S], over_ch[:], acc[:, c, :], start=c == 0, stop=c == CC - 1)
                        job_end("mu", last)
                    elif kind == "ln_var":
                        pe.wait_ge(*ch_sq.at(l, 1))
                        ps = job_start("var")
                        for c in range(CC):
                            last = pe.matmul(ps[:, 0:S], over_ch[:], square[:, c, :], start=c == 0,
                                             stop=c == CC - 1)
                        job_end("var", last)
                    elif kind.startswith("hid_turn"):
                        n = int(kind[8:])
                        pe.wait_ge(*hid_sq.at(l, n + 1))
                        turn(JOBS_OF[kind], hid[:, n % 2])


_IN_ORDER = ["x", "positions", "inv_freq", "packed", "w_in", "b_gate", "w_gla_a2", "g_gla_norm", "w_moba_o",
             "w_gla_o", "w_conv_o", "w_mix_out", "g_mix_post", "w_mlp_up", "w_mlp_down", "g_mlp_post"]


def kernel(**inputs):
    import numpy as np
    import concourse.bacc as bacc
    from concourse.bass_utils import run_bass_kernel_spmd

    def chunks(a):
        a = np.asarray(a)
        a = a.reshape(a.shape[:-1] + (a.shape[-1] // P, P))
        a = np.moveaxis(a, -1, 1)
        return np.moveaxis(a, -1, 2).reshape(a.shape[0], P, -1)

    data = {k: np.ascontiguousarray(v) for k, v in inputs.items()}
    data["positions"] = np.ascontiguousarray(data["positions"].reshape(T, P).T)
    freq = np.float32(10000.0) ** (-np.arange(HALF, dtype=np.float32) / np.float32(HALF))
    data["inv_freq"] = np.ascontiguousarray(np.broadcast_to(freq.astype(np.float32), (P, HALF)))
    data["packed"] = np.ascontiguousarray(np.concatenate(
        [chunks(data[n]) for n in ("g_mix_pre", "g_mlp_pre", "b_gla_a", "g_conv_ln", "b_conv_ln", "b_dw", "w_dw")],
        axis=-1))
    nc = bacc.Bacc("TRN2", target_bir_lowering=False, num_devices=1)
    arrays, args = {}, []
    for name in _IN_ORDER:
        arrays[name + "_dram"] = data[name]
        args.append(nc.dram_tensor(name + "_dram", data[name].shape, mybir.dt.from_np(data[name].dtype),
                                   kind="ExternalInput").ap())
    out = nc.dram_tensor("out_dram", (1, S, D), F32, kind="ExternalOutput").ap()
    trunk(nc, *args, out)
    r = run_bass_kernel_spmd(nc, [arrays], core_ids=[0])
    return r.results[0]["out_dram"]
```

```python
from contextlib import ExitStack

import concourse.bass as bass
from concourse import mybir

F32 = mybir.dt.float32
F32R = mybir.dt.float32r
I32 = mybir.dt.int32
I16 = mybir.dt.int16
ACT = mybir.ActivationFunctionType
ALU = mybir.AluOpType
AX = mybir.AxisListType

P = 128
D = 1024
S = 256
T = S // P
DEPTH = 2
KC = D // P
EPS = 1e-6
NEG = -1e30
HEADS = 8
DH = 64
PAIRS = HEADS // 2
GH = 4
GDK = 64
GDV = 128
RANK = 16
CHUNK = 64
CH = 512
CC = CH // P
TAPS = 31
FF = 4096
HALF = DH // 2
COLS = 512
RAW_SLOTS = 5
SPLIT_SLOTS = 5

C_Q, C_K, C_V = 0, 512, 1024
C_LQK, C_LV, C_LA, C_LR, C_CA, C_CG, C_GATES = 1536, 2048, 2560, 2576, 3088, 3600, 4112

PACKED = [("g_mix_pre", KC), ("g_mlp_pre", KC), ("b_gla", 2), ("g_ln", CC), ("b_ln", CC), ("b_dw", CC),
          ("w_dw", CC * TAPS)]
PACK_AT = {}
_at = 0
for _n, _w in PACKED:
    PACK_AT[_n] = _at
    _at += _w
PACK_W = _at

BRANCHES = (1, 0, 2)
GROUPS = (
    [("ca", "w_in", C_CA, D, "act"), ("cg", "w_in", C_CG, D, "act"), ("lqk", "w_in", C_LQK, D, "act"),
     ("lv", "w_in", C_LV, D, "act"), ("lr", "w_in", C_LR, D, "act"), ("mq", "w_in", C_Q, D, "act"),
     ("mk", "w_in", C_K, D, "act"), ("mv", "w_in", C_V, D, "act")]
    + [g for b, w in zip(BRANCHES, ("w_gla_o", "w_moba_o", "w_conv_o"))
       for g in [(f"g{b}{c}", "w_in", C_GATES + b * D + c * COLS, D, "act") for c in range(2)]
       + [(f"w{b}{c}", w, c * COLS, CH, f"branch{b}") for c in range(2)]]
    + [(f"mo{c}", "w_mix_out", c * COLS, D, "act") for c in range(2)]
    + [(f"up{c}", "w_mlp_up", c * COLS, D, "act") for c in range(FF // COLS)]
    + [(f"dn{c}", "w_mlp_down", c * COLS, FF, "hid") for c in range(2)]
)
GROUP_NO = {g[0]: i for i, g in enumerate(GROUPS)}
STRIPS = []
for _g in GROUPS[:-2]:
    _n = _g[3] // 256
    STRIPS += [(_g[0], j, j == 0, j == _n - 1) for j in range(_n)]
for _j in range(FF // 256):
    STRIPS += [(f"dn{c}", _j, _j == 0, _j == FF // 256 - 1) for c in range(2)]
NS = len(STRIPS)
LAST_STRIP = {g: u for u, (g, j, first, last) in enumerate(STRIPS) if last}
assert NS % RAW_SLOTS == 0 and NS % SPLIT_SLOTS == 0 and len(GROUPS) % 2 == 0

LEVELS = [0, 32, 16, 8, 4, 2, 1]

JOBS_OF = {
    "la": ["la"], "la_turn": ["laT"], "decay": ["dec0", "dec1"],
    "u_turn": ["uT0", "uT1"], "l_turn": ["lT0", "lT1"], "q_turn": ["qT0", "qT1"], "k_turn": ["kT0", "kT1"],
    "kd_turn": ["kdT"], "g_turn": ["gT0", "gT1"], "g_out": ["go0", "go1"], "ln_mean": ["mu"], "ln_var": ["var"],
}
for _t in range(T):
    for _name in ("pre_turn", "mix_turn", "mlp_turn"):
        JOBS_OF[f"{_name}{_t}"] = [f"{_name}{_t}_{i}" for i in range(2)]
for _i in range(len(LEVELS)):
    JOBS_OF[f"level{_i}"] = [f"lev{_i}_{hh}" for hh in range(2)]
for _i in range(3):
    JOBS_OF[f"state{_i}"] = [f"st{_i}"]
for _i in range(PAIRS):
    JOBS_OF[f"scores{_i}"] = [f"s0_{_i}", f"s1_{_i}"]
    JOBS_OF[f"probs{_i}"] = [f"pa_{_i}", f"pb_{_i}"]
    JOBS_OF[f"values{_i}"] = [f"o_{_i}"]
for _i in range(8):
    JOBS_OF[f"hid_turn{_i}"] = [f"h0_{_i}", f"h1_{_i}"]

AFTER = {}


def place(u, *steps):
    AFTER.setdefault(u, []).extend(steps)


place(2, "la_round")
place(4, "la")
place(5, ("use", "la"))
place(6, "la_turn")
place(7, ("use", "la_turn"))
place(8, "decay")
place(8, "rope_tables")
place(9, "u_turn", ("use", "decay"))
place(10, ("use", "u_turn"), ("tap", 0))
place(11, "log_decay")
place(12, "cumulate", "l_turn")
place(13, ("use", "l_turn"), "level_sub1", "level_sub2")
for _i in range(1, len(LEVELS) + 1):
    _u = 12 + 2 * _i
    if _i < len(LEVELS):
        place(_u, f"level_mul{_i}")
        place(_u + 1, f"level{_i}")
        if _i + 2 <= len(LEVELS):
            place(_u, f"level_sub{_i + 2}")
    if _i == 1:
        place(_u, "level0")
        place(_u + 1, ("use", "level0"))
    else:
        place(_u, ("use", f"level{_i - 1}"))
place(26, "q_turn", "inter_mul")
place(27, ("use", "q_turn"))
place(28, "kd_turn", ("use", "kd_turn"))
place(29, "state0")
place(30, "k_turn", ("use", "state0"), "state1")
place(31, ("use", "k_turn"), ("use", "state1"), "state2")
place(32, ("use", "state2"))
place(33, "g_out", ("use", "g_out"))
place(34, "g_rstd", "g_scale")
for _i in range(PAIRS):
    _u = 33 + 4 * _i
    place(_u, f"scores{_i}")
    place(_u + 1, ("use", f"scores{_i}"))
    place(_u + 2, f"norm{_i}")
    place(_u + 4, f"probs{_i}", ("use", f"probs{_i}"))
    place(_u + 5, f"values{_i}")
    place(_u + 6, ("use", f"values{_i}"))
place(35, "g_turn")
place(36, ("use", "g_turn"))
place(54, "ln_mean")
place(55, ("use", "ln_mean"))
place(56, "ln_var")
place(57, ("use", "ln_var"))
place(58, "ln_affine")
place(59, "ln_silu")
place(60, "ln_hi")
place(61, "ln_lo")
for _i in range(8):
    place(LAST_STRIP[f"up{_i}"] + 2, f"hid_turn{_i}", ("use", f"hid_turn{_i}"))

V_COST = {"evac_mq": 3.7, "evac_mk": 3.7, "evac_lr": 2.4, "evac_cg": 1.1, "evac_g": 1.2, "evac_w": 2.3,
          "decay": 0.8, "cumulate": 1.2, "level_sub": 0.7, "level_mul": 0.7, "level": 0.7, "inter_mul": 1.2,
          "state": 0.5, "g_rstd": 2.1, "g_scale": 2.1, "g_turn": 1.2, "scores": 2.1, "norm": 0.2, "values": 0.3}
T_COST = {"decay": 0.9, "u_turn": 0.9, "l_turn": 0.9, "q_turn": 0.9, "k_turn": 0.9, "kd_turn": 0.4, "g_turn": 0.9,
          "level": 0.9, "scores": 1.3, "probs": 1.3, "values": 0.8, "g_out": 3.3, "state": 0.6}
V_SPLIT, V_TAP, T_STRIP = 1.13, 1.4, 2.6
FIRST_TAP, LAST_TAP = 10, 53

ROW_BLOCKS = [(0, 1), (3, 4), (1, 3), (4, 6)]


LATE_EVAC = ("lr", "mq", "mk")


def tap_spots():
    load, time = {}, {}
    for u in range(FIRST_TAP, LAST_TAP + 1):
        g, _, _, last = STRIPS[u]
        names = [((s if isinstance(s, str) else s[1]).rstrip("0123456789"), s in JOBS_OF) for s in AFTER.get(u, [])
                 if s != ("tap", 0)]
        time[u] = T_STRIP + sum(T_COST.get(name, 0.0) for name, on_t in names if on_t)
        load[u] = V_SPLIT + sum(V_COST.get(name, 0.0) for name, on_t in names if not on_t)
        if last and g not in LATE_EVAC:
            load[u] += V_COST.get("evac_" + (g[0] if g[1].isdigit() else g), 0.0)
        if STRIPS[u - 1][3] and STRIPS[u - 1][0] in LATE_EVAC:
            load[u] += V_COST["evac_" + STRIPS[u - 1][0]]
    stretch = 0.8
    while True:
        spots, tap, behind = {}, 1, 0.0
        for u in load:
            behind = max(behind + load[u] - stretch * time[u], -V_TAP)
            while tap < TAPS and behind + V_TAP <= 0.5 * V_TAP:
                behind += V_TAP
                spots.setdefault(u, []).append(tap)
                tap += 1
        if tap == TAPS:
            return spots
        stretch += 0.01


def build_plan():
    between = {
        "ca": (2, ["pre_turn1", ("use", "pre_turn1"), "squares0", "rstd0"]),
        "w20": (4, [("evac", ("w20", (0,))), ("evac", ("w21", (0,)))]),
        "mo0": (3, ["mix_turn1", ("use", "mix_turn1")]),
        "mo1": (4, ["post_mix0"]),
        "up0": (3, ["mlp_turn1", ("use", "mlp_turn1"), "squares1", "rstd1"]),
        "dn0": (4, ["post_mlp0"]),
    }
    taken = {"w20": (3, ("use", "mix_turn0")), "mo1": (1, ("use", "mlp_turn0"))}
    next_turn = {"w20": "mix_turn0", "mo1": "mlp_turn0"}
    behind = {
        "w20": [("evac", ("w20", (1,))), ("evac", ("w21", (1,)))],
        "mo1": ["post_mix1", ("lo", LAST_STRIP["up0"])],
        "dn0": ["post_mlp1"],
    }
    by_tile = {LAST_STRIP[g] - 3: g for g in ("ca", "mo0", "mo1", "up0")}
    by_tile[LAST_STRIP["w21"] - 3] = "w20"
    by_tile[NS - 4] = "dn0"
    spots = tap_spots()

    def rest(u):
        steps = []
        if u + SPLIT_SLOTS < NS:
            steps.append(("hi", u + SPLIT_SLOTS))
        if u + SPLIT_SLOTS - 1 < NS and u != LAST_STRIP["mo1"]:
            steps.append(("lo", u + SPLIT_SLOTS - 1))
        g, _, _, last = STRIPS[u]
        evac = [("evac", (g, tuple(range(T))))] if last and g not in ("w20", "w21", "mo0", "mo1", "dn0", "dn1") else []
        if g[0] not in "gw":
            steps += [s for s in evac if g not in LATE_EVAC]
            evac = []
        if u and STRIPS[u - 1][3] and STRIPS[u - 1][0] in LATE_EVAC:
            evac = [("evac", (STRIPS[u - 1][0], tuple(range(T))))]
        return steps + AFTER.get(u, []) + evac + [("tap", k) for k in spots.get(u, [])]

    plan = []
    for u in range(SPLIT_SLOTS):
        plan += [("hi", u)] + ([("lo", u)] if u < SPLIT_SLOTS - 1 else [])
        if u == 0:
            plan += ["pre_turn0", ("use", "pre_turn0")]
    u = 0
    while u < NS:
        if u in by_tile:
            block, g = range(u, u + 4), by_tile[u]
            n, steps = between[g]
            plan += [("mm", (v, 0)) for v in block[:n]] + steps + [("mm", (v, 0)) for v in block[n:]]
            for v in block:
                if g in next_turn and v == block[-1]:
                    plan.append(next_turn[g])
                plan += [("mm", (v, 1))] + rest(v)
                if g in taken and v == u + taken[g][0] - 1:
                    plan.append(taken[g][1])
            plan += behind.get(g, [])
            u += 4
        else:
            plan += [("mm", (u, 0)), ("mm", (u, 1))] + rest(u)
            u += 1
    return plan


PLAN = build_plan()
JOBS = [j for step in PLAN if isinstance(step, str) for j in JOBS_OF.get(step, [])]
assert len(set(JOBS)) == len(JOBS) == sum(len(v) for v in JOBS_OF.values())
JOB_BANKS = 4
JOBS_PER_BANK = len(JOBS) // JOB_BANKS
assert len(JOBS) % JOB_BANKS == 0, len(JOBS)
JOB_NO = {j: i for i, j in enumerate(JOBS)}
for _step, _jobs in JOBS_OF.items():
    for _j in _jobs:
        if JOB_NO[_j] + JOB_BANKS < len(JOBS):
            _next = JOBS[JOB_NO[_j] + JOB_BANKS]
            _start = PLAN.index(next(s for s in JOBS_OF if _next in JOBS_OF[s]))
            assert PLAN.index("g_scale" if _step == "g_out" else ("use", _step)) < _start, (_j, _next)


NEWTON_SCALE = -1.0 / 8192


class Signal:

    def __init__(self, sem, per_layer, primed=0):
        self.sem, self.per_layer, self.primed = sem, per_layer, primed

    def at(self, layer, k):
        assert 1 <= k + self.primed
        return self.sem, layer * self.per_layer + (k + self.primed)


def trunk(nc, x, positions, inv_freq, packed, w_in, b_gate, w_a2, g_gla, w_moba_o, w_gla_o, w_conv_o,
          w_mix_out, g_mix_post, w_up, w_down, g_mlp_post, out):
    weights = {"w_in": w_in, "w_moba_o": w_moba_o, "w_gla_o": w_gla_o, "w_conv_o": w_conv_o,
               "w_mix_out": w_mix_out, "w_mlp_up": w_up, "w_mlp_down": w_down}
    ctx = ExitStack()
    with ctx:
        def sb(name, shape, dt=F32, where=ctx):
            return where.enter_context(nc.sbuf_tensor(name, shape, dt))

        def signal(name, per_layer, primed=0):
            return Signal(ctx.enter_context(nc.semaphore(name)), per_layer, primed)

        resid = sb("resid", [P, T, D])
        xs = sb("xs", [P, T, D])
        act_h = sb("act_h", [P, KC, S], F32R)
        act_l = sb("act_l", [P, KC, S], F32R)
        raw = sb("raw", [P, RAW_SLOTS, 2, COLS])
        w_h = sb("w_h", [P, SPLIT_SLOTS, 2, COLS], F32R)
        w_l = sb("w_l", [P, SPLIT_SLOTS, 2, COLS], F32R)
        pk = sb("pk", [P, PACK_W])
        a2 = sb("a2", [2 * RANK, 2 * P])
        bg = sb("bg", [P, D])
        gpost = sb("gpost", [P, D])
        ggla = sb("ggla", [P, GDV])
        la_raw = sb("la_raw", [P, KC, RANK])
        la_w = sb("la_w", [P, KC, 2, RANK], F32R)
        la_nat = sb("la_nat", [P, T, 2 * RANK])
        laT = sb("laT", [2 * RANK, S])
        ident = sb("ident", [P, P])
        over_ch = sb("over_ch", [P, P])
        causal = sb("causal", [P, 3, P])
        keep = sb("keep", [P, 2 * S])
        dmask = sb("dmask", [P, P], I16)
        lmask = sb("lmask", [P, len(LEVELS), P // 2], I16)
        ang_t = sb("ang_t", [P, 2, T, HALF])
        cos_t = sb("cos_t", [P, T, HALF])
        sin_t = sb("sin_t", [P, T, HALF])
        aT = sb("aT", [P, 2, 2 * T, P])
        tmp = sb("tmp", [P, T, COLS])
        stats = sb("stats", [P, 96])
        inv_f = sb("inv_f", [P, HALF])
        pos_i = sb("pos_i", [P, T], I32)
        pos_f = sb("pos_f", [P, T])
        rt = tmp[:].rearrange("p t n -> p (t n)")[:, 0:6 * T * HALF].rearrange("p (i t n) -> p i t n", i=6, t=T)
        mixers = ExitStack()
        qT = sb("qT", [P, PAIRS, S], where=mixers)
        kT = sb("kT", [P, PAIRS, S], where=mixers)
        v = sb("v", [P, T, COLS], where=mixers)
        brT_h = [sb(f"br{i}_h", [P, CC, S], F32R, mixers) for i in range(2)]
        brT_l = [sb(f"br{i}_l", [P, CC, S], F32R, mixers) for i in range(2)]
        lqT = sb("lqT", [P, 2, S], where=mixers)
        lkT = sb("lkT", [P, 2, S], where=mixers)
        lv = sb("lv", [P, T, COLS], where=mixers)
        cum = sb("cum", [P, 2, S], where=mixers)
        ex = sb("ex", [P, 2, S], where=mixers)
        shared = sb("shared", [P, 5 * COLS], where=mixers)
        qs = shared[:, 0:1024].rearrange("p (b n) -> p b n", b=2)
        ks = shared[:, 1024:2048].rearrange("p (b a s) -> p b a s", b=2, a=2)
        kdn = shared[:, 2048:].rearrange("p (t n) -> p t n", t=T)
        pr = shared[:, 0:12 * P].rearrange("p (b i n) -> p b i n", b=2, i=6)
        prT = shared[:, 12 * P:18 * P].rearrange("p (i n) -> p i n", i=6)
        eG = sb("eG", [P, 2, S], where=mixers)
        qg = sb("qg", [P, 2, S], where=mixers)
        state = sb("state", [P, 3, 2, P], where=mixers)
        slr = sb("slr", [P, T, COLS], where=mixers)
        u_nat = sb("u_nat", [P, T, COLS], where=mixers)
        cgs = sb("cgs", [P, T, COLS], where=mixers)
        uT = sb("uT", [P, CC, S], where=mixers)
        acc = sb("acc", [P, CC, S], where=mixers)
        gate = sb("gate", [P, T, D], where=mixers)
        mixers.close()
        hid_h = sb("hid_h", [P, FF // P, S], F32R)
        hid_l = sb("hid_l", [P, FF // P, S], F32R)
        hid = sb("hid", [P, 2, T, COLS])

        bank = [ctx.enter_context(nc.psum_tensor(f"bank{i}", [P, COLS], F32)) for i in range(8)]

        def param(name, i=0, n=1):
            return pk[:, PACK_AT[name] + i:PACK_AT[name] + i + n]

        decay = cgs[:, 0, :].rearrange("p (a s) -> p a s", a=2)
        decay_e = cgs[:, 1, :].rearrange("p (a s) -> p a s", a=2)
        square = u_nat[:, :, :].rearrange("p t n -> p (t n)").rearrange("p (c s) -> p c s", c=CC)
        exps = [ex[:], decay]
        var, rst, rsc = (cgs[:, i // 2, (i % 2) * S:(i % 2) * S + S] for i in range(3))

        x_in = [signal(f"x_in{t}", 0) for t in range(T)]
        tile0_done = signal("tile0_done", len(GROUPS))
        pos_in = signal("pos_in", 0)
        freq_in = signal("freq_in", 0)
        raw_in = [signal(f"raw_in{i}", 16 * NS // RAW_SLOTS) for i in range(RAW_SLOTS)]
        strip_hi = signal("strip_hi", NS)
        strip_split = signal("strip_split", NS, RAW_SLOTS)
        strip_used = signal("strip_used", NS, SPLIT_SLOTS)
        acc_read = [signal(f"acc_read{i}", len(GROUPS) // 2, 1) for i in range(4)]
        job_done = [signal(f"job_done{i}", JOBS_PER_BANK) for i in range(JOB_BANKS)]
        job_read = [signal(f"job_read{i}", JOBS_PER_BANK, 1) for i in range(JOB_BANKS)]
        job_hi = signal("job_hi", 3 * 2 * T + 2 + PAIRS + 16)
        pk_in = signal("pk_in", 16)
        a2_in = signal("a2_in", 32)
        bg_in = signal("bg_in", 48)
        gpost_in = signal("gpost_in", 32)
        ggla_in = signal("ggla_in", 16)
        la_in = signal("la_in", 16)
        consts = signal("consts", 1)
        ident_in = signal("ident_in", 0)
        pool_steps = signal("pool_steps", 0)
        rope_in = signal("rope_in", 2)
        passed = signal("passed", 0)
        layer_in = signal("layer_in", T)
        squares = signal("squares", 2 * T)
        rstd_in = signal("rstd_in", 2)
        la_hi = signal("la_hi", 1)
        la_split = signal("la_split", 1)
        decay_exp = signal("decay_exp", 3)
        cg_sig = signal("cg_sig", 1)
        u_in = signal("u_in", 1)
        rope_out = signal("rope_out", 2)
        expo = signal("expo", 7)
        expd = signal("expd", 7)
        cum_in = signal("cum_in", 1)
        eg_in = signal("eg_in", 1)
        scaled = signal("scaled", 7)
        state_in = signal("state_in", 3)
        p_in = signal("p_in", PAIRS)
        p_exp = signal("p_exp", PAIRS)
        p_recip = signal("p_recip", PAIRS)
        p_norm = signal("p_norm", PAIRS)
        tap0 = signal("tap0", 1)
        g_squares = signal("g_squares", 2)
        lr_sig = signal("lr_sig", T)
        g_ready = signal("g_ready", 1)
        gate_in = signal("gate_in", 6)
        gate_sig = signal("gate_sig", 6)
        mix_in = signal("mix_in", T)
        taps_in = signal("taps_in", 1)
        centred = signal("centred", 1)
        ch_sq = signal("ch_sq", 1)
        ln_in = signal("ln_in", 1)
        ln_sig = signal("ln_sig", 1)
        silu_in = signal("silu_in", 1)
        conv_hi = signal("conv_hi", 1)
        conv_split = signal("conv_split", 1)
        y_squares = signal("y_squares", 4 * T)
        gained = signal("gained", 4 * T)
        resid_in = signal("resid_in", 2 * T)
        hid_sq = signal("hid_sq", 8)
        out_in = signal("out_in", 0)
        V_STEPS, A_STEPS = 420, 30
        v_steps = signal("v_steps", V_STEPS)
        a_steps = signal("a_steps", A_STEPS)

        def job_bank(job):
            return JOB_NO[job] % JOB_BANKS

        def job_ps(job):
            return bank[4 + job_bank(job)]

        def job_k(job):
            return JOB_NO[job] // JOB_BANKS + 1

        def group_bank(g, t):
            return 2 * (GROUP_NO[g] % 2) + t

        def group_ps(g, t):
            return bank[group_bank(g, t)]

        def group_k(g):
            return GROUP_NO[g] // 2 + 1

        def heads(ap, n):
            return ap.rearrange("p (h n) -> p h n", h=n)

        block = ctx.enter_context(nc.Block())

        @block.sync
        def _(sp):
            for t in range(T):
                sp.dma_start(resid[:, t, :], x[0, t * P:(t + 1) * P, :]).then_inc(x_in[t].sem, 16)
            with sp.Fori(0, DEPTH) as l:
                for u, (g, j, first, last) in enumerate(STRIPS):
                    _, w, c0, _, _ = GROUPS[GROUP_NO[g]]
                    sp.wait_ge(*strip_split.at(l, u + 1 - RAW_SLOTS))
                    sp.sem_inc(passed.sem, 1)
                    src = weights[w][bass.ds(l, 1), 256 * j:256 * j + 256, c0:c0 + COLS]
                    sp.dma_start(raw[:, u % RAW_SLOTS], src.rearrange("l (c p) n -> p (l c) n", p=P))\
                        .then_inc(raw_in[u % RAW_SLOTS].sem, 16)
            for t in range(T):
                sp.wait_ge(*resid_in.at(DEPTH - 1, T + t + 1))
                sp.dma_start(out[0, t * P:(t + 1) * P, :], resid[:, t, :]).then_inc(out_in.sem, 16)
            sp.wait_ge(out_in.sem, 16 * T)

        @block.gpsimd
        def _(pool):

            def load_first(l, first):
                if not first:
                    pool.wait_ge(*la_split.at(l - 1, 1))
                pool.dma_start(la_raw[:], w_in[bass.ds(l, 1), :, C_LA:C_LA + RANK]
                               .rearrange("l (c p) n -> p (l c) n", p=P)).then_inc(la_in.sem, 16)
                if not first:
                    pool.wait_ge(*strip_split.at(l - 1, LAST_STRIP["up7"] + 1))
                pool.dma_start(pk[:], packed[bass.ds(l, 1)].rearrange("l p n -> p (l n)")).then_inc(pk_in.sem, 16)

            def load_rest(l, first):
                for i in range(2):
                    pool.dma_start(a2[i * RANK:(i + 1) * RANK, :], w_a2[bass.ds(l, 1)].rearrange("l r n -> r (l n)"))\
                        .then_inc(a2_in.sem, 16)
                pool.dma_start(ggla[:], g_gla[bass.ds(l, 1), :].partition_broadcast(P)).then_inc(ggla_in.sem, 16)
                for n, b in enumerate(BRANCHES):
                    if n:
                        g = f"g{BRANCHES[n - 1]}1"
                        for t in range(T):
                            pool.wait_ge(*acc_read[group_bank(g, t)].at(l, group_k(g)))
                    pool.dma_start(bg[:], b_gate[bass.ds(l, 1), b * D:(b + 1) * D].partition_broadcast(P))\
                        .then_inc(bg_in.sem, 16)
                    if n == 0:
                        if not first:
                            pool.wait_ge(*resid_in.at(l - 1, 2 * T))
                        pool.dma_start(gpost[:], g_mix_post[bass.ds(l, 1), :].partition_broadcast(P))\
                            .then_inc(gpost_in.sem, 16)
                pool.wait_ge(*resid_in.at(l, T))
                pool.dma_start(gpost[:], g_mlp_post[bass.ds(l, 1), :].partition_broadcast(P))\
                    .then_inc(gpost_in.sem, 16)

            steps = 0

            def own(ins):
                nonlocal steps
                ins.then_inc(pool_steps.sem, 1)
                steps += 1
                pool.wait_ge(pool_steps.sem, steps)

            load_first(0, True)
            own(pool.memset(ident[:], 0.0))
            own(pool.affine_select(out=ident[:], in_=ident[:], compare_op=ALU.not_equal, fill=1.0, base=0,
                                   pattern=[[-1, P]], channel_multiplier=1))
            pool.sem_inc(ident_in.sem, 1)
            for t in range(T):
                pool.wait_ge(x_in[t].sem, 16)
                pool.sem_inc(layer_in.sem, 1)
            own(pool.memset(over_ch[:], 1.0 / CH))
            own(pool.memset(causal[:], 0.0))
            for i in (0, 2):
                own(pool.affine_select(out=causal[:, i, :], in_=causal[:, i, :], compare_op=ALU.is_ge, fill=NEG,
                                       base=0, pattern=[[-1, P]], channel_multiplier=1))
            own(pool.memset(keep[:], 1.0))
            own(pool.memset(heads(keep[:], 2 * S // CHUNK)[:, :, 0:1], 0.0))
            own(pool.memset(aT[:], 0.0))
            own(pool.memset(dmask[:], 1))
            own(pool.affine_select(out=dmask[:], in_=dmask[:], compare_op=ALU.is_equal, fill=0.0, base=0,
                                   pattern=[[-1, P]], channel_multiplier=1))
            own(pool.memset(lmask[:], 1))
            for n, s in enumerate(LEVELS):
                if s == 0:
                    continue
                m = lmask[:, n, :].rearrange("p (b s) -> p b s", s=s)
                own(pool.affine_select(out=m, in_=m, compare_op=ALU.is_ge, fill=0.0, base=0,
                                       pattern=[[-2 * s, P // (2 * s)], [0, s]], channel_multiplier=1))
                own(pool.affine_select(out=m, in_=m, compare_op=ALU.is_ge, fill=0.0, base=s - 1,
                                       pattern=[[2 * s, P // (2 * s)], [0, s]], channel_multiplier=-1))
            TWO_PI = 6.283185307179586
            SMALL = 710.0 - 113 * TWO_PI
            ROUND = 12582912.0
            C1 = 6.28125
            C2 = 0.0019350051879882812
            C3 = TWO_PI - C1 - C2
            LIMIT = 3.1415925
            pool.wait_ge(freq_in.sem, 16)
            pool.wait_ge(pos_in.sem, 16)
            own(pool.tensor_copy(pos_f[:], pos_i[:]))
            ang, k0, k1, kk, off, part = (rt[:, i] for i in range(6))

            def add_scaled(dst, src, scale, other):
                own(pool.tensor_scalar(part, src, scale, None, ALU.mult))
                own(pool.tensor_tensor(dst, part, other, ALU.add))

            for t in range(T):
                own(pool.tensor_scalar(ang[:, t, :], inv_f[:], pos_f[:, t:t + 1], None, ALU.mult))
            big = 710.0 * 4096
            own(pool.tensor_scalar(k0, ang, 1.0 / big, ROUND, ALU.mult, ALU.add))
            own(pool.tensor_scalar(k0, k0, ROUND, None, ALU.subtract))
            add_scaled(ang, k0, -big, ang)
            own(pool.tensor_scalar(k1, ang, 1.0 / 710.0, ROUND, ALU.mult, ALU.add))
            own(pool.tensor_scalar(k1, k1, ROUND, None, ALU.subtract))
            add_scaled(ang, k1, -710.0, ang)
            add_scaled(kk, k0, 4096.0, k1)
            own(pool.tensor_scalar(kk, kk, SMALL, None, ALU.mult))
            own(pool.tensor_tensor(k1, ang, kk, ALU.add))
            for dst, turn, shift in ((0, 0.0, 0.0), (1, 0.25, TWO_PI / 4)):
                own(pool.tensor_scalar(k0, k1, 1.0 / TWO_PI, turn, ALU.mult, ALU.add))
                own(pool.tensor_scalar(k0, k0, ROUND, ROUND, ALU.add, ALU.subtract))
                add_scaled(off, k0, -C1, ang)
                add_scaled(off, k0, -C2, off)
                add_scaled(off, k0, -C3, off)
                own(pool.tensor_tensor(off, off, kk, ALU.add))
                own(pool.tensor_scalar(off, off, shift, LIMIT, ALU.add, ALU.min))
                own(pool.tensor_scalar(ang_t[:, dst], off, -LIMIT, None, ALU.max))
            pool.sem_inc(consts.sem, 1)
            load_rest(0, True)
            with pool.Fori(1, DEPTH) as l:
                load_first(l, False)
                pool.sem_inc(consts.sem, 1)
                load_rest(l, False)

        @block.scalar
        def _(act):
            act.dma_start(pos_i[:], positions).then_inc(pos_in.sem, 16)
            act.dma_start(inv_f[:], inv_freq).then_inc(freq_in.sem, 16)
            act.sem_inc(strip_used.sem, SPLIT_SLOTS)
            with act.Fori(0, DEPTH) as l:
                a_count = 0
                hi_count = 0

                def job_wait(job):
                    act.wait_ge(*job_done[job_bank(job)].at(l, job_k(job)))

                def group_wait(g, t):
                    if t == 0:
                        act.wait_ge(*tile0_done.at(l, GROUP_NO[g] + 1))
                    else:
                        act.wait_ge(*strip_used.at(l, LAST_STRIP[g] + 1))

                def own(ins):
                    nonlocal a_count
                    ins.then_inc(a_steps.sem, 1)
                    a_count += 1
                    act.wait_ge(*a_steps.at(l, a_count))

                def row_squares(src, t, c, dst):
                    return act.activation(xs[:, t, c:c + src.shape[-1]], src, ACT.Square, accum_out=dst)

                def turn_hi(jobs, dst):
                    for i, job in enumerate(jobs):
                        job_wait(job)
                        act.activation(dst[:, 2 * i:2 * i + 2, :], heads(job_ps(job)[:], 2), ACT.Copy)\
                            .then_inc(job_hi.sem, 1)

                def tile_hi(jobs, t, scale):
                    for i, job in enumerate(jobs):
                        job_wait(job)
                        if not isinstance(scale, str):
                            last = act.activation(act_h[:, 4 * i:4 * i + 4, t * P:(t + 1) * P],
                                                  heads(job_ps(job)[:], 4), ACT.Copy, scale=scale)
                        else:
                            for c in range(4):
                                last = act.activation(act_h[:, 4 * i + c, t * P:(t + 1) * P],
                                                      job_ps(job)[:, c * P:(c + 1) * P], ACT.Copy,
                                                      scale=param(scale, 4 * i + c))
                        last.then_inc(job_hi.sem, 1)

                def rstd(t):
                    return stats[:, 64 + t:65 + t]

                def half_rstd(t):
                    return stats[:, 66 + t:67 + t]

                for step in PLAN:
                    kind, arg = step if isinstance(step, tuple) else (step, None)
                    n = int(kind[-1]) if kind[-1].isdigit() else None
                    if kind == "hi":
                        act.wait_ge(*raw_in[arg % RAW_SLOTS].at(l, 16 * (arg // RAW_SLOTS + 1)))
                        act.wait_ge(*strip_used.at(l, arg + 1 - SPLIT_SLOTS))
                        g, j, _, _ = STRIPS[arg]
                        if g.startswith("up"):
                            for c in range(2):
                                last = act.activation(w_h[:, arg % SPLIT_SLOTS, c], raw[:, arg % RAW_SLOTS, c],
                                                      ACT.Copy, scale=param("g_mlp_pre", 2 * j + c))
                        else:
                            last = act.activation(w_h[:, arg % SPLIT_SLOTS], raw[:, arg % RAW_SLOTS], ACT.Copy)
                        last.then_inc(strip_hi.sem, 1)
                    elif kind == "evac":
                        g, tiles = arg
                        if g == "ca":
                            act.wait_ge(*rstd_in.at(l, 1))
                        elif g == "up0":
                            act.wait_ge(*rstd_in.at(l, 2))
                        if g in ("ca", "lqk", "lv", "mv"):
                            dst = {"ca": u_nat, "lqk": u_nat, "lv": lv, "mv": v}[g]
                            for t in tiles:
                                group_wait(g, t)
                                act.activation(dst[:, t, :], group_ps(g, t)[:], ACT.Copy, scale=rstd(t))\
                                    .then_inc(acc_read[group_bank(g, t)].sem, 1)
                        elif g == "cg":
                            for t in tiles:
                                group_wait(g, t)
                                act.activation(cgs[:, t, :], group_ps(g, t)[:], ACT.Tanh, scale=half_rstd(t))\
                                    .then_inc(acc_read[group_bank(g, t)].sem, 1)
                        elif g == "lr":
                            for t in tiles:
                                group_wait(g, t)
                                act.activation(slr[:, t, :], group_ps(g, t)[:], ACT.Tanh, scale=half_rstd(t))\
                                    .then_inc(lr_sig.sem, 1)
                        elif g[0] == "g":
                            c = int(g[2])
                            act.wait_ge(*gate_in.at(l, 2 * BRANCHES.index(int(g[1])) + c + 1))
                            act.activation(gate[:, :, c * COLS:(c + 1) * COLS], gate[:, :, c * COLS:(c + 1) * COLS],
                                           ACT.Tanh, scale=0.5).then_inc(gate_sig.sem, 1)
                        elif g.startswith("up"):
                            for t in tiles:
                                group_wait(g, t)
                                act.activation(hid[:, int(g[2]) % 2, t, :], group_ps(g, t)[:], ACT.Relu,
                                               scale=rstd(t)).then_inc(acc_read[group_bank(g, t)].sem, 1)
                    elif kind.startswith("squares"):
                        for t in range(T):
                            if n:
                                act.wait_ge(*resid_in.at(l, t + 1))
                            else:
                                act.wait_ge(*layer_in.at(l, t + 1))
                            row_squares(resid[:, t, :], t, 0, stats[:, t:t + 1]).then_inc(squares.sem, 1)
                            act.wait_ge(*squares.at(l, T * n + t + 1))
                    elif kind == "rope_tables":
                        act.wait_ge(*consts.at(l, 1))
                        act.activation(sin_t[:], ang_t[:, 0], ACT.Sin).then_inc(rope_in.sem, 1)
                        act.activation(cos_t[:], ang_t[:, 1], ACT.Sin).then_inc(rope_in.sem, 1)
                    elif kind == "la_round":
                        act.wait_ge(*la_in.at(l, 16))
                        act.activation(la_w[:, :, 0, :], la_raw[:], ACT.Copy).then_inc(la_hi.sem, 1)
                    elif kind == "log_decay":
                        for i in range(2):
                            act.wait_ge(*job_read[job_bank(f"dec{i}")].at(l, job_k(f"dec{i}")))
                        act.activation(decay_e, decay, ACT.Abs).then_inc(decay_exp.sem, 1)
                        act.wait_ge(*decay_exp.at(l, 1))
                        act.activation(decay_e, decay_e, ACT.Exp, scale=-1.0).then_inc(decay_exp.sem, 1)
                        act.wait_ge(*decay_exp.at(l, 2))
                        act.activation(decay_e, decay_e, ACT.Ln, bias=1.0).then_inc(decay_exp.sem, 1)
                    elif kind == "tap" and arg == 0:
                        for c in range(CC):
                            last = act.activation(acc[:, c, :], uT[:, c, :], ACT.Identity,
                                                  scale=param("w_dw", c * TAPS + TAPS - 1), bias=param("b_dw", c))
                        last.then_inc(tap0.sem, 1)
                    elif kind.startswith("level_sub"):
                        act.wait_ge(*expo.at(l, n))
                        act.activation(exps[n % 2], exps[n % 2], ACT.Exp, scale=1.0 / 16.0).then_inc(expd.sem, 1)
                        if n == len(LEVELS):
                            act.activation(eG[:], cum[:], ACT.Exp, scale=1.0 / 16.0).then_inc(eg_in.sem, 1)
                    elif kind.startswith("norm"):
                        act.wait_ge(*p_recip.at(l, n + 1))
                        for i, (lo, hi) in enumerate(ROW_BLOCKS):
                            last = act.activation(pr[:, n % 2, lo:hi, :], pr[:, n % 2, lo:hi, :], ACT.Copy,
                                                  scale=stats[:, 68 + 4 * (n % 2) + i:69 + 4 * (n % 2) + i])
                        last.then_inc(p_norm.sem, 1)
                    elif kind == "ln_affine":
                        act.wait_ge(*ln_in.at(l, 1))
                        for c in range(CC):
                            last = act.activation(acc[:, c, :], acc[:, c, :], ACT.Identity,
                                                  scale=param("g_ln", c), bias=param("b_ln", c))
                        own(last)
                        act.activation(square, acc[:], ACT.Tanh, scale=0.5).then_inc(ln_sig.sem, 1)
                    elif kind == "ln_hi":
                        act.wait_ge(*silu_in.at(l, 1))
                        act.wait_ge(*strip_used.at(l, LAST_STRIP["w11"] + 1))
                        act.activation(brT_h[1][:], acc[:], ACT.Copy, scale=0.5).then_inc(conv_hi.sem, 1)
                    elif kind.startswith(("post_mix", "post_mlp")):
                        m, gs = (0, ("mo0", "mo1")) if kind[:-1] == "post_mix" else (1, ("dn0", "dn1"))
                        k = 2 * (T * m + n)
                        for c, g in enumerate(gs):
                            group_wait(g, n)
                            if c:
                                act.wait_ge(*gained.at(l, k + 1))
                            row_squares(group_ps(g, n)[:], n, c * COLS, stats[:, 4 + 2 * n + c:5 + 2 * n + c])\
                                .then_inc(y_squares.sem, 1)
                        act.wait_ge(*y_squares.at(l, k + 2))
                    elif kind == "use":
                        jobs = JOBS_OF[arg]
                        n = int(arg[-1]) if arg[-1].isdigit() else None
                        if arg.startswith("pre_turn"):
                            if n == 0:
                                act.wait_ge(*pk_in.at(l, 16))
                            tile_hi(jobs, n, "g_mix_pre")
                        elif arg.startswith("mlp_turn"):
                            tile_hi(jobs, n, 1.0)
                        elif arg.startswith("mix_turn"):
                            tile_hi(jobs, n, 0.5)
                        elif arg == "la":
                            job_wait("la")
                            for t in range(T):
                                last = act.activation(la_nat[:, t, :], job_ps("la")[:, 2 * t * RANK:2 * (t + 1) * RANK],
                                                      ACT.Copy, scale=rstd(t))
                            last.then_inc(job_read[job_bank("la")].sem, 1)
                        elif arg == "la_turn":
                            job_wait("laT")
                            act.activation(laT[:], job_ps("laT")[0:2 * RANK, 0:S], ACT.Copy)\
                                .then_inc(job_read[job_bank("laT")].sem, 1)
                        elif arg in ("u_turn", "q_turn", "k_turn"):
                            dst = {"u_turn": uT, "q_turn": qT, "k_turn": kT}[arg]
                            for i, job in enumerate(jobs):
                                job_wait(job)
                                last = act.activation(dst[:, 2 * i:2 * i + 2, :], heads(job_ps(job)[:], 2), ACT.Copy,
                                                      scale=0.5 if arg == "u_turn" else 1.0)
                                last.then_inc(job_read[job_bank(job)].sem, 1)
                            if arg == "u_turn":
                                for job in jobs:
                                    act.wait_ge(*job_read[job_bank(job)].at(l, job_k(job)))
                        elif arg == "l_turn":
                            job_wait("lT0")
                            act.activation(lqT[:], heads(job_ps("lT0")[:], 2), ACT.Copy, scale=GDK ** -0.5)\
                                .then_inc(job_read[job_bank("lT0")].sem, 1)
                            job_wait("lT1")
                            act.activation(lkT[:], heads(job_ps("lT1")[:], 2), ACT.Copy)\
                                .then_inc(job_read[job_bank("lT1")].sem, 1)
                        elif arg == "kd_turn":
                            job_wait("kdT")
                            act.activation(kdn, heads(job_ps("kdT")[:], T), ACT.Copy)\
                                .then_inc(job_read[job_bank("kdT")].sem, 1)
                        elif arg == "g_out":
                            for hh in range(2):
                                job_wait(f"go{hh}")
                                for i in range(2 * T):
                                    last = act.activation(tmp[:, hh, i * GDV:(i + 1) * GDV],
                                                          job_ps(f"go{hh}")[:, i * GDV:(i + 1) * GDV], ACT.Square,
                                                          accum_out=stats[:, 16 + 4 * hh + i:17 + 4 * hh + i])
                                last.then_inc(g_squares.sem, 1)
                        elif arg == "g_turn":
                            turn_hi(jobs, brT_h[1])
                        elif arg.startswith("scores"):
                            b = n % 2
                            act.wait_ge(*p_in.at(l, n + 1))
                            for i, (lo, hi) in enumerate(ROW_BLOCKS):
                                last = act.activation(pr[:, b, lo:hi, :], pr[:, b, lo:hi, :], ACT.Exp,
                                                      bias=stats[:, 40 + 4 * b + i:41 + 4 * b + i],
                                                      scale=DH ** -0.5,
                                                      accum_out=stats[:, 48 + 4 * b + i:49 + 4 * b + i])
                            last.then_inc(p_exp.sem, 1)
                        elif arg.startswith("probs"):
                            for job, lo, hi in ((f"pa_{n}", 0, 4), (f"pb_{n}", 4, 6)):
                                job_wait(job)
                                act.activation(prT[:, lo:hi, :], heads(job_ps(job)[:, 0:(hi - lo) * P], hi - lo),
                                               ACT.Copy).then_inc(job_read[job_bank(job)].sem, 1)
                        elif arg.startswith("values"):
                            job_wait(f"o_{n}")
                            act.activation(brT_h[0][:, n, :], job_ps(f"o_{n}")[:, 0:S], ACT.Copy)\
                                .then_inc(job_hi.sem, 1)
                        elif arg == "ln_mean":
                            act.wait_ge(*centred.at(l, 1))
                            act.activation(square, acc[:], ACT.Square).then_inc(ch_sq.sem, 1)
                        elif arg.startswith("hid_turn"):
                            turn_hi(jobs, hid_h[:, 4 * n:4 * n + 4])
                act.wait_ge(*a_steps.at(l, a_count))
                act.sem_inc(a_steps.sem, A_STEPS - a_count)

        @block.vector
        def _(dve):
            dve.sem_inc(strip_split.sem, RAW_SLOTS)
            for i in range(4):
                dve.sem_inc(acc_read[i].sem, 1)
                dve.sem_inc(job_read[i].sem, 1)

            with dve.Fori(0, DEPTH) as l:
                count = 0
                hi_count = 0

                def step_done(ins):
                    nonlocal count
                    ins.then_inc(v_steps.sem, 1)
                    count += 1
                    return count

                def after(k):
                    dve.wait_ge(*v_steps.at(l, k))

                def chain(ins):
                    after(step_done(ins))

                def job_wait(job):
                    dve.wait_ge(*job_done[job_bank(job)].at(l, job_k(job)))

                def group_wait(g, t):
                    if t == 0:
                        dve.wait_ge(*tile0_done.at(l, GROUP_NO[g] + 1))
                    else:
                        dve.wait_ge(*strip_used.at(l, LAST_STRIP[g] + 1))

                def rstd(t):
                    return stats[:, 64 + t:65 + t]

                def rsqrt(v_, y, s_):
                    chain(dve.tensor_scalar(y.bitcast(I32), v_.bitcast(I32), -0.5, 1597463007.0,
                                            ALU.mult, ALU.add))
                    for _ in range(3):
                        chain(dve.scalar_tensor_tensor(out=s_, in0=v_, scalar=-0.5, in1=y, op0=ALU.mult,
                                                       op1=ALU.mult))
                        chain(dve.tensor_tensor(s_, s_, y, ALU.mult))
                        chain(dve.scalar_tensor_tensor(out=y, in0=s_, scalar=1.5, in1=y, op0=ALU.add,
                                                       op1=ALU.mult))

                def turn_lo(jobs, hi, lo):
                    nonlocal hi_count
                    for i, job in enumerate(jobs):
                        hi_count += 1
                        dve.wait_ge(*job_hi.at(l, hi_count))
                        dve.tensor_tensor(lo[:, 2 * i:2 * i + 2, :], heads(job_ps(job)[:], 2),
                                          hi[:, 2 * i:2 * i + 2, :].bitcast(F32), ALU.subtract)\
                            .then_inc(job_read[job_bank(job)].sem, 1)

                def tile_lo(jobs, t, scale):
                    nonlocal hi_count
                    for i, job in enumerate(jobs):
                        hi_count += 1
                        dve.wait_ge(*job_hi.at(l, hi_count))
                        cols = slice(t * P, (t + 1) * P)
                        if not isinstance(scale, str):
                            last = dve.scalar_tensor_tensor(
                                out=act_l[:, 4 * i:4 * i + 4, cols], in0=heads(job_ps(job)[:], 4), scalar=scale,
                                in1=act_h[:, 4 * i:4 * i + 4, cols].bitcast(F32), op0=ALU.mult, op1=ALU.subtract)
                        else:
                            for c in range(4):
                                last = dve.scalar_tensor_tensor(
                                    out=act_l[:, 4 * i + c, cols], in0=job_ps(job)[:, c * P:(c + 1) * P],
                                    scalar=param(scale, 4 * i + c), in1=act_h[:, 4 * i + c, cols].bitcast(F32),
                                    op0=ALU.mult, op1=ALU.subtract)
                        last.then_inc(job_read[job_bank(job)].sem, 1)

                tap_no = {}
                for step in PLAN:
                    kind, arg = step if isinstance(step, tuple) else (step, None)
                    n = int(kind[-1]) if kind[-1].isdigit() else None
                    if kind == "lo":
                        dve.wait_ge(*strip_hi.at(l, arg + 1))
                        g, j, _, _ = STRIPS[arg]
                        slot = arg % SPLIT_SLOTS
                        if g.startswith("up"):
                            for c in range(2):
                                last = dve.scalar_tensor_tensor(
                                    out=w_l[:, slot, c], in0=raw[:, arg % RAW_SLOTS, c],
                                    scalar=param("g_mlp_pre", 2 * j + c), in1=w_h[:, slot, c].bitcast(F32),
                                    op0=ALU.mult, op1=ALU.subtract)
                        else:
                            last = dve.tensor_tensor(w_l[:, slot], raw[:, arg % RAW_SLOTS],
                                                     w_h[:, slot].bitcast(F32), ALU.subtract)
                        last.then_inc(strip_split.sem, 1)
                    elif kind == "evac":
                        g, tiles = arg
                        if g == "cg":
                            for t in tiles:
                                dve.wait_ge(*acc_read[group_bank("ca", t)].at(l, group_k("ca")))
                                dve.wait_ge(*acc_read[group_bank("cg", t)].at(l, group_k("cg")))
                            dve.scalar_tensor_tensor(out=u_nat[:], in0=cgs[:], scalar=1.0, in1=u_nat[:], op0=ALU.add,
                                                     op1=ALU.mult).then_inc(u_in.sem, 1)
                        elif g in ("mq", "mk"):
                            dve.wait_ge(*rope_in.at(l, 2))
                            at = 0 if g == "mq" else 512
                            for t in tiles:
                                src = heads(group_ps(g, t)[:], 2 * HEADS)
                                c_b = cos_t[:, t:t + 1, :].to_broadcast([P, 2 * HEADS, HALF])
                                s_b = sin_t[:, t:t + 1, :].to_broadcast([P, 2 * HEADS, HALF])
                                xc = tmp[:, 0, :]
                                xn = tmp[:, 1, :]
                                if t:
                                    after(count)
                                elif g == "mk":
                                    dve.wait_ge(*rope_out.at(l, 1))
                                group_wait(g, t)
                                step_done(dve.scalar_tensor_tensor(out=heads(xc, 2 * HEADS), in0=src, scalar=rstd(t),
                                                                   in1=c_b, op0=ALU.mult, op1=ALU.mult))
                                dve.scalar_tensor_tensor(out=heads(xn, 2 * HEADS), in0=src, scalar=rstd(t), in1=s_b,
                                                         op0=ALU.mult, op1=ALU.mult)\
                                    .then_inc(acc_read[group_bank(g, t)].sem, 1)
                                after(count)
                                dve.wait_ge(*acc_read[group_bank(g, t)].at(l, group_k(g)))
                                xc4 = xc.rearrange("p (h two n) -> p h two n", two=2, n=HALF)
                                xn4 = xn.rearrange("p (h two n) -> p h two n", two=2, n=HALF)
                                dst = xs[:, t, at:at + 512].rearrange("p (h two n) -> p h two n", two=2, n=HALF)
                                dve.tensor_tensor(dst[:, :, 0, :], xc4[:, :, 0, :], xn4[:, :, 1, :], ALU.subtract)
                                last = dve.tensor_tensor(dst[:, :, 1, :], xc4[:, :, 1, :], xn4[:, :, 0, :],
                                                         ALU.add)
                                if t == 0:
                                    step_done(last)
                            last.then_inc(rope_out.sem, 1)
                        elif g == "lr":
                            dve.wait_ge(*ggla_in.at(l, 16))
                            for t in tiles:
                                dve.wait_ge(*lr_sig.at(l, t + 1))
                                step_done(dve.scalar_tensor_tensor(
                                    out=heads(slr[:, t, :], GH), in0=heads(slr[:, t, :], GH), scalar=1.0,
                                    in1=ggla[:, :].rearrange("p (a n) -> p a n", a=1).to_broadcast([P, GH, GDV]),
                                    op0=ALU.add, op1=ALU.mult))
                            for t in tiles:
                                after(count - T + 1 + t)
                                dve.scalar_tensor_tensor(out=slr[:, t, :], in0=group_ps(g, t)[:], scalar=rstd(t),
                                                         in1=slr[:, t, :], op0=ALU.mult, op1=ALU.mult)\
                                    .then_inc(acc_read[group_bank(g, t)].sem, 1)
                        elif g[0] == "g":
                            b, c = BRANCHES.index(int(g[1])), int(g[2])
                            dve.wait_ge(*bg_in.at(l, 16 * (b + 1)))
                            for t in tiles:
                                group_wait(g, t)
                                dve.scalar_tensor_tensor(out=gate[:, t, c * COLS:(c + 1) * COLS],
                                                         in0=group_ps(g, t)[:], scalar=rstd(t),
                                                         in1=bg[:, c * COLS:(c + 1) * COLS], op0=ALU.mult,
                                                         op1=ALU.add).then_inc(acc_read[group_bank(g, t)].sem, 1)
                            for t in tiles:
                                dve.wait_ge(*acc_read[group_bank(g, t)].at(l, group_k(g)))
                            dve.sem_inc(gate_in.sem, 1)
                        elif g[0] == "w":
                            b, c = BRANCHES.index(int(g[1])), int(g[2])
                            dve.wait_ge(*gate_sig.at(l, 2 * b + c + 1))
                            for t in tiles:
                                group_wait(g, t)
                                dve.scalar_tensor_tensor(
                                    out=tmp[:, t, :] if b else xs[:, t, c * COLS:(c + 1) * COLS],
                                    in0=gate[:, t, c * COLS:(c + 1) * COLS], scalar=1.0, in1=group_ps(g, t)[:],
                                    op0=ALU.add, op1=ALU.mult).then_inc(acc_read[group_bank(g, t)].sem, 1)
                            for t in tiles:
                                mix = xs[:, t, c * COLS:(c + 1) * COLS]
                                dve.wait_ge(*acc_read[group_bank(g, t)].at(l, group_k(g)))
                                if b:
                                    last = dve.tensor_tensor(mix, mix, tmp[:, t, :], ALU.add)
                                    if (b, c) == (2, 1):
                                        last.then_inc(mix_in.sem, 1)
                                    else:
                                        chain(last)
                        elif g.startswith("up"):
                            for t in tiles:
                                dve.wait_ge(*acc_read[group_bank(g, t)].at(l, group_k(g)))
                            h = hid[:, int(g[2]) % 2]
                            dve.tensor_tensor(h, h, h, ALU.mult).then_inc(hid_sq.sem, 1)
                    elif kind.startswith("rstd"):
                        dve.wait_ge(*squares.at(l, T * (n + 1)))
                        chain(dve.tensor_scalar(stats[:, 2:4], stats[:, 0:2], 1.0 / D, EPS, ALU.mult, ALU.add))
                        rsqrt(stats[:, 2:4], stats[:, 64:66], stats[:, 66:68])
                        chain(dve.tensor_scalar(stats[:, 66:68], stats[:, 64:66], 0.5, None, ALU.mult))
                        dve.sem_inc(rstd_in.sem, 1)
                    elif kind == "la_round":
                        dve.wait_ge(*la_hi.at(l, 1))
                        dve.tensor_tensor(la_w[:, :, 1, :], la_raw[:], la_w[:, :, 0, :].bitcast(F32), ALU.subtract)\
                            .then_inc(la_split.sem, 1)
                    elif kind == "cumulate":
                        dve.wait_ge(*decay_exp.at(l, 3))
                        chain(dve.scalar_tensor_tensor(out=ex[:], in0=decay, scalar=0.0, in1=decay_e,
                                                       op0=ALU.min, op1=ALU.subtract))
                        dve.wait_ge(*consts.at(l, 1))
                        dve.tensor_tensor_scan(cum[:].rearrange("p a s -> p (a s)"), keep[:],
                                               ex[:].rearrange("p a s -> p (a s)"), 0.0, ALU.mult, ALU.add)\
                            .then_inc(cum_in.sem, 1)
                        dve.wait_ge(*cum_in.at(l, 1))
                    elif kind.startswith("level_sub"):
                        if n > 2:
                            dve.wait_ge(*scaled.at(l, n - 2))
                        if n == len(LEVELS):
                            g3 = cum[:].rearrange("p a (b c) -> p (a b) c", c=CHUNK)
                            end = g3[:, :, CHUNK - 1:CHUNK].broadcast_to([P, 2 * S // CHUNK, CHUNK])
                            dve.tensor_tensor(exps[n % 2].rearrange("p a (b c) -> p (a b) c", c=CHUNK), end, g3,
                                              ALU.subtract).then_inc(expo.sem, 1)
                        else:
                            s = LEVELS[n]
                            g4 = cum[:].rearrange("p a (b h s) -> p (a b) h s", h=2, s=s)
                            e4 = exps[n % 2].rearrange("p a (b h s) -> p (a b) h s", h=2, s=s)
                            ref = g4[:, :, 0, s - 1:s].broadcast_to([P, 2 * S // (2 * s), s])
                            dve.tensor_tensor(e4[:, :, 0, :], ref, g4[:, :, 0, :], ALU.subtract)
                            dve.tensor_tensor(e4[:, :, 1, :], g4[:, :, 1, :], ref, ALU.subtract)\
                                .then_inc(expo.sem, 1)
                    elif kind.startswith("level_mul"):
                        dve.wait_ge(*expd.at(l, n))
                        if n > 2:
                            for hh in range(2):
                                job = f"lev{n - 2}_{hh}"
                                dve.wait_ge(*job_done[job_bank(job)].at(l, job_k(job)))
                        else:
                            for job in ("lT0", "lT1"):
                                dve.wait_ge(*job_read[job_bank(job)].at(l, job_k(job)))
                        s = LEVELS[n]
                        q4, k4, o4, e4 = (a.rearrange("p a (b h s) -> p (a b) h s", h=2, s=s)
                                          for a in (lqT[:], lkT[:], ks[:, n % 2], exps[n % 2]))
                        dve.tensor_tensor(qs[:, n % 2, 0:S].rearrange("p (b s) -> p b s", s=s), q4[:, :, 1, :],
                                          e4[:, :, 1, :], ALU.mult)
                        if n <= 2:
                            last = dve.tensor_tensor(ks[:, n % 2], lkT[:], exps[n % 2], ALU.mult)
                        else:
                            last = dve.tensor_tensor(o4[:, :, 0, :], k4[:, :, 0, :], e4[:, :, 0, :], ALU.mult)
                        last.then_inc(scaled.sem, 1)
                    elif kind == "inter_mul":
                        dve.wait_ge(*eg_in.at(l, 1))
                        dve.tensor_tensor(qg[:], lqT[:], eG[:], ALU.mult)
                        dve.wait_ge(*expd.at(l, len(LEVELS)))
                        dve.tensor_tensor(ks[:, 1], lkT[:], exps[1], ALU.mult).then_inc(scaled.sem, 1)
                    elif kind == "g_rstd":
                        dve.wait_ge(*g_squares.at(l, 2))
                        m = T * GH
                        chain(dve.tensor_scalar(stats[:, 24:24 + m], stats[:, 16:16 + m], 4.0 / GDV, 4.0 * EPS,
                                                ALU.mult, ALU.add))
                        rsqrt(stats[:, 24:24 + m], stats[:, 32:32 + m], stats[:, 16:16 + m])
                    elif kind == "g_scale":
                        for hh in range(2):
                            for i in range(2 * T):
                                t, h = i // 2, 2 * (i % 2) + hh
                                blk = slr[:, t, h * GDV:(h + 1) * GDV]
                                at = 32 + 4 * hh + i
                                last = dve.scalar_tensor_tensor(
                                    out=blk, in0=job_ps(f"go{hh}")[:, i * GDV:(i + 1) * GDV],
                                    scalar=stats[:, at:at + 1], in1=blk, op0=ALU.mult, op1=ALU.mult)
                            last.then_inc(job_read[job_bank(f"go{hh}")].sem, 1)
                    elif kind.startswith("norm"):
                        dve.wait_ge(*p_exp.at(l, n + 1))
                        dve.reciprocal(stats[:, 68 + 4 * (n % 2):72 + 4 * (n % 2)],
                                       stats[:, 48 + 4 * (n % 2):52 + 4 * (n % 2)]).then_inc(p_recip.sem, 1)
                    elif kind == "tap" and arg:
                        k = arg
                        if k == 1:
                            dve.wait_ge(*tap0.at(l, 1))
                        for c in range(CC):
                            if k > 1:
                                after(tap_no[c])
                            ins = dve.scalar_tensor_tensor(
                                out=acc[:, c, k:], in0=uT[:, c, 0:S - k],
                                scalar=param("w_dw", c * TAPS + TAPS - 1 - k), in1=acc[:, c, k:], op0=ALU.mult,
                                op1=ALU.add)
                            if k == TAPS - 1 and c == CC - 1:
                                ins.then_inc(taps_in.sem, 1)
                            else:
                                tap_no[c] = step_done(ins)
                    elif kind == "ln_silu":
                        dve.wait_ge(*ln_sig.at(l, 1))
                        dve.scalar_tensor_tensor(out=acc[:], in0=square, scalar=1.0, in1=acc[:], op0=ALU.add,
                                                 op1=ALU.mult).then_inc(silu_in.sem, 1)
                    elif kind == "ln_lo":
                        dve.wait_ge(*conv_hi.at(l, 1))
                        dve.scalar_tensor_tensor(out=brT_l[1][:], in0=acc[:], scalar=0.5,
                                                 in1=brT_h[1][:].bitcast(F32), op0=ALU.mult, op1=ALU.subtract)\
                            .then_inc(conv_split.sem, 1)
                    elif kind.startswith(("post_mix", "post_mlp")):
                        m, gs = (0, ("mo0", "mo1")) if kind[:-1] == "post_mix" else (1, ("dn0", "dn1"))
                        dve.wait_ge(*gpost_in.at(l, 16 * (m + 1)))
                        k = 2 * (T * m + n)
                        for c in (1, 0):
                            group_wait(gs[c], n)
                            if c == 0:
                                dve.wait_ge(*y_squares.at(l, k + 1))
                            dve.scalar_tensor_tensor(out=tmp[:, c, :], in0=group_ps(gs[c], n)[:],
                                                     scalar=D ** 0.5 * NEWTON_SCALE,
                                                     in1=gpost[:, c * COLS:(c + 1) * COLS], op0=ALU.mult,
                                                     op1=ALU.mult).then_inc(gained.sem, 1)
                        dve.wait_ge(*y_squares.at(l, k + 2))
                        dve.wait_ge(*gained.at(l, k + 2))
                        y2 = stats[:, 4 + 2 * n:6 + 2 * n]
                        va, y, tm = (stats[:, 8 + 3 * n + i:9 + 3 * n + i] for i in range(3))
                        chain(dve.tensor_scalar(va, y2[:, 0:1], y2[:, 1:2], D * EPS, ALU.add, ALU.add))
                        for g in gs:
                            dve.sem_inc(acc_read[group_bank(g, n)].sem, 1)
                        chain(dve.tensor_scalar(y.bitcast(I32), va.bitcast(I32), -0.5, 1597463007.0,
                                                ALU.mult, ALU.add))
                        for three in (3.0, 12.0, 768.0):
                            chain(dve.scalar_tensor_tensor(out=tm, in0=y, scalar=va, in1=y, op0=ALU.mult, op1=ALU.mult))
                            chain(dve.scalar_tensor_tensor(out=y, in0=tm, scalar=three, in1=y, op0=ALU.subtract,
                                                           op1=ALU.mult))
                        dve.scalar_tensor_tensor(out=resid[:, n, :], in0=tmp[:].rearrange("p t n -> p (t n)"), scalar=y,
                                                 in1=resid[:, n, :], op0=ALU.mult, op1=ALU.add)\
                            .then_inc(resid_in.sem, 1)
                        dve.wait_ge(*resid_in.at(l, T * m + n + 1))
                        if m:
                            dve.sem_inc(layer_in.sem, 1)
                    elif kind == "use":
                        jobs = JOBS_OF[arg]
                        n = int(arg[-1]) if arg[-1].isdigit() else None
                        if arg.startswith("pre_turn"):
                            if n == 0:
                                dve.wait_ge(*pk_in.at(l, 16))
                            tile_lo(jobs, n, "g_mix_pre")
                        elif arg.startswith("mlp_turn"):
                            tile_lo(jobs, n, 1.0)
                        elif arg.startswith("mix_turn"):
                            tile_lo(jobs, n, 0.5)
                        elif arg == "decay":
                            dve.wait_ge(*u_in.at(l, 1))
                            for i, job in enumerate(jobs):
                                job_wait(job)
                                dve.tensor_scalar(decay[:, i, :], job_ps(job)[:, 0:S], param("b_gla", i), None,
                                                  ALU.add).then_inc(job_read[job_bank(job)].sem, 1)
                        elif arg.startswith("level"):
                            for hh, job in enumerate(jobs):
                                job_wait(job)
                                if n:
                                    before = f"lev{n - 1}_{hh}"
                                    dve.wait_ge(*job_read[job_bank(before)].at(l, job_k(before)))
                                dve.sem_inc(passed.sem, 1)
                                if n == 0:
                                    dst, src = aT[:, hh], heads(job_ps(job)[:], 2 * T)
                                    mask = dmask[:].rearrange("p (o n) -> p o n", o=1).to_broadcast([P, 2 * T, P])
                                else:
                                    s = LEVELS[n]
                                    nb = P // (2 * s)
                                    dst = aT[:, hh].rearrange("p i (b h s) -> p i b h s", h=2, s=s)[:, :, :, 1, :]
                                    src = job_ps(job)[:, 0:S].rearrange("p (i b s) -> p i b s", i=2 * T, s=s)
                                    mask = lmask[:, n, :].rearrange("p (o b s) -> p o b s", o=1, s=s)\
                                        .to_broadcast([P, 2 * T, nb, s])
                                dve.copy_predicated(dst, mask, src).then_inc(job_read[job_bank(job)].sem, 1)
                        elif arg.startswith("state"):
                            job_wait(f"st{n}")
                            for p in range(2):
                                ps = job_ps(f"st{n}")[:, p * P:(p + 1) * P]
                                if n == 0:
                                    last = dve.tensor_copy(state[:, 0, p, :], ps)
                                else:
                                    last = dve.scalar_tensor_tensor(
                                        out=state[:, n, p, :], in0=state[:, n - 1, p, :],
                                        scalar=eG[:, p, n * CHUNK + CHUNK - 1:n * CHUNK + CHUNK], in1=ps,
                                        op0=ALU.mult, op1=ALU.add)
                                if p == 0:
                                    step_done(last)
                            last.then_inc(state_in.sem, 1)
                            dve.wait_ge(*state_in.at(l, n + 1))
                            dve.sem_inc(job_read[job_bank(f"st{n}")].sem, 1)
                        elif arg == "g_turn":
                            turn_lo(jobs, brT_h[1], brT_l[1])
                        elif arg.startswith("scores"):
                            b = n % 2
                            for hh, job in enumerate(jobs):
                                job_wait(job)
                                dve.tensor_tensor(pr[:, b, 3 * hh:3 * hh + 3, :], heads(job_ps(job)[:, 0:3 * P], 3),
                                                  causal[:], ALU.add).then_inc(job_read[job_bank(job)].sem, 1)
                            for job in jobs:
                                dve.wait_ge(*job_read[job_bank(job)].at(l, job_k(job)))
                            rows = pr[:, b].rearrange("p (h c) n -> p h c n", h=2)
                            step_done(dve.tensor_reduce(stats[:, 56:58], rows[:, :, 0, :], AX.X, ALU.max))
                            chain(dve.tensor_reduce(stats[:, 58:60],
                                                    rows[:, :, 1:3, :].rearrange("p h c n -> p h (c n)"),
                                                    AX.X, ALU.max))
                            dve.tensor_scalar(stats[:, 40 + 4 * b:44 + 4 * b], stats[:, 56:60], -(DH ** -0.5), None,
                                              ALU.mult).then_inc(p_in.sem, 1)
                        elif arg.startswith("values"):
                            hi_count += 1
                            dve.wait_ge(*job_hi.at(l, hi_count))
                            dve.tensor_tensor(brT_l[0][:, n, :], job_ps(f"o_{n}")[:, 0:S],
                                              brT_h[0][:, n, :].bitcast(F32), ALU.subtract)\
                                .then_inc(job_read[job_bank(f"o_{n}")].sem, 1)
                        elif arg == "ln_mean":
                            job_wait("mu")
                            dve.tensor_tensor(acc[:], acc[:], job_ps("mu")[:, 0:S]
                                              .rearrange("p (a n) -> p a n", a=1)
                                              .to_broadcast([P, CC, S]), ALU.subtract).then_inc(centred.sem, 1)
                            dve.wait_ge(*centred.at(l, 1))
                            dve.sem_inc(job_read[job_bank("mu")].sem, 1)
                        elif arg == "ln_var":
                            job_wait("var")
                            dve.tensor_scalar(var, job_ps("var")[:, 0:S], EPS, None, ALU.add)\
                                .then_inc(job_read[job_bank("var")].sem, 1)
                            dve.wait_ge(*job_read[job_bank("var")].at(l, job_k("var")))
                            rsqrt(var, rst, rsc)
                            dve.tensor_tensor(acc[:], acc[:], rst.rearrange("p (a n) -> p a n", a=1)
                                              .to_broadcast([P, CC, S]), ALU.mult).then_inc(ln_in.sem, 1)
                        elif arg.startswith("hid_turn"):
                            turn_lo(jobs, hid_h[:, 4 * n:4 * n + 4], hid_l[:, 4 * n:4 * n + 4])
                after(count)
                assert count < V_STEPS, count
                dve.sem_inc(v_steps.sem, V_STEPS - count)

        @block.tensor
        def _(pe):
            pe.wait_ge(ident_in.sem, 1)
            with pe.Fori(0, DEPTH) as l:

                def job_start(job):
                    pe.wait_ge(*job_read[job_bank(job)].at(l, job_k(job) - 1))
                    return job_ps(job)

                def job_end(job, last):
                    last.then_inc(job_done[job_bank(job)].sem, 1)

                def jobs_read(jobs, before=None):
                    for job in {job_bank(j_): j_ for j_ in jobs}.values():
                        if before is None or job_bank(job) != job_bank(before):
                            pe.wait_ge(*job_read[job_bank(job)].at(l, job_k(job)))

                def turn(jobs, src):
                    for i, job in enumerate(jobs):
                        ps = job_start(job)
                        for c in range(2):
                            for t in range(T):
                                last = pe.transpose(ps[:, c * S + t * P:c * S + (t + 1) * P],
                                                    src[:, t, (2 * i + c) * P:(2 * i + c + 1) * P], ident[:])
                        job_end(job, last)

                def turn_tile(jobs, src, t):
                    for i, job in enumerate(jobs):
                        ps = job_start(job)
                        for c in range(4):
                            last = pe.transpose(ps[:, c * P:(c + 1) * P],
                                                src[:, t, (4 * i + c) * P:(4 * i + c + 1) * P], ident[:])
                        job_end(job, last)

                for step in PLAN:
                    kind, arg = step if isinstance(step, tuple) else (step, None)
                    if kind == "mm":
                        u, t = arg
                        g, j, first, last_of = STRIPS[u]
                        lhs = GROUPS[GROUP_NO[g]][4]
                        if first:
                            if lhs == "branch0":
                                jobs_read([f"o_{p}" for p in range(PAIRS)])
                            elif lhs == "branch1":
                                jobs_read(JOBS_OF["g_turn"])
                            elif lhs == "branch2":
                                pe.wait_ge(*conv_split.at(l, 1))
                            elif g in ("ca", "mo0", "up0"):
                                jobs_read(JOBS_OF[{"ca": "pre", "mo0": "mix", "up0": "mlp"}[g] + f"_turn{t}"])
                            pe.wait_ge(*acc_read[group_bank(g, t)].at(l, group_k(g) - 1))
                        if g == "dn0" and j % 2 == 0:
                            jobs_read(JOBS_OF[f"hid_turn{j // 2}"])
                        a_h, a_l = {"act": (act_h, act_l), "branch0": (brT_h[0], brT_l[0]),
                                    "branch1": (brT_h[1], brT_l[1]), "branch2": (brT_h[1], brT_l[1]),
                                    "hid": (hid_h, hid_l)}[lhs]
                        if t == 0:
                            pe.wait_ge(*strip_split.at(l, u + 1))
                        ps = group_ps(g, t)[:]
                        for c in range(2):
                            s_h = a_h[:, 2 * j + c, t * P:(t + 1) * P]
                            s_l = a_l[:, 2 * j + c, t * P:(t + 1) * P]
                            r_h = w_h[:, u % SPLIT_SLOTS, c, :]
                            r_l = w_l[:, u % SPLIT_SLOTS, c, :]
                            pe.matmul(ps, s_h, r_h, start=first and c == 0, stop=False)
                            pe.matmul(ps, s_h, r_l, start=False, stop=False)
                            last = pe.matmul(ps, s_l, r_h, start=False, stop=last_of and c == 1)
                        if t == T - 1:
                            last.then_inc(strip_used.sem, 1)
                        elif last_of:
                            last.then_inc(tile0_done.sem, 1)
                    elif kind.startswith("pre_turn"):
                        t = int(kind[-1])
                        pe.wait_ge(*layer_in.at(l, t + 1))
                        turn_tile(JOBS_OF[kind], resid, t)
                    elif kind.startswith("mlp_turn"):
                        t = int(kind[-1])
                        pe.wait_ge(*resid_in.at(l, t + 1))
                        turn_tile(JOBS_OF[kind], resid, t)
                    elif kind.startswith("mix_turn"):
                        t = int(kind[-1])
                        pe.wait_ge(*mix_in.at(l, t + 1))
                        turn_tile(JOBS_OF[kind], xs, t)
                    elif kind == "la":
                        ps = job_start("la")
                        pe.wait_ge(*la_split.at(l, 1))
                        for t in range(T):
                            for c in range(KC):
                                s_h = act_h[:, c, t * P:(t + 1) * P]
                                s_l = act_l[:, c, t * P:(t + 1) * P]
                                dst = ps[:, 2 * t * RANK:2 * (t + 1) * RANK]
                                pe.matmul(dst, s_h, la_w[:, c].rearrange("p a r -> p (a r)"), start=c == 0,
                                          stop=False, skip_group_check=True)
                                last = pe.matmul(dst[:, 0:RANK], s_l, la_w[:, c, 0, :], start=False,
                                                 stop=c == KC - 1, skip_group_check=True)
                        job_end("la", last)
                    elif kind == "la_turn":
                        ps = job_start("laT")
                        jobs_read(["la"], "laT")
                        for t in range(T):
                            last = pe.transpose(ps[0:2 * RANK, t * P:(t + 1) * P], la_nat[:, t, :], ident[:])
                        job_end("laT", last)
                    elif kind == "decay":
                        jobs_read(["laT"], "dec0")
                        pe.wait_ge(*a2_in.at(l, 32))
                        for i in range(2):
                            ps = job_start(f"dec{i}")
                            job_end(f"dec{i}", pe.matmul(ps[:, 0:S], a2[:, i * P:(i + 1) * P], laT[:],
                                                         start=True, stop=True))
                    elif kind == "u_turn":
                        pe.wait_ge(*u_in.at(l, 1))
                        turn(JOBS_OF[kind], u_nat)
                    elif kind == "l_turn":
                        for t in range(T):
                            pe.wait_ge(*acc_read[group_bank("lqk", t)].at(l, group_k("lqk")))
                        turn(JOBS_OF[kind], u_nat)
                    elif kind in JOBS_OF and kind.startswith("level"):
                        n = int(kind[5:])
                        if n:
                            pe.wait_ge(*scaled.at(l, n))
                        else:
                            jobs_read(["lT0", "lT1"], "lev0_0")
                        k_ = ks[:, n % 2] if n else lkT
                        w = P // 2 if n else P
                        for hh in range(2):
                            ps = job_start(f"lev{n}_{hh}")
                            rows = slice(GDK * hh, GDK * hh + GDK)
                            for i in range(2 * T):
                                t, p = i // 2, i % 2
                                q_ = qs[rows, n % 2, p * P + t * w:p * P + (t + 1) * w] if n else \
                                    lqT[rows, p, t * P:(t + 1) * P]
                                last = pe.matmul(ps[:, i * w:(i + 1) * w], k_[rows, p, t * P:(t + 1) * P], q_,
                                                 start=True, stop=True)
                            job_end(f"lev{n}_{hh}", last)
                    elif kind == "kd_turn":
                        pe.wait_ge(*scaled.at(l, 7))
                        ps = job_start("kdT")
                        for t in range(T):
                            for p in range(2):
                                last = pe.transpose(ps[:, t * S + p * P:t * S + (p + 1) * P],
                                                    ks[:, 1, p, t * P:(t + 1) * P], ident[:])
                        job_end("kdT", last)
                    elif kind.startswith("state"):
                        c = int(kind[5:])
                        ps = job_start(f"st{c}")
                        jobs_read(["kdT"], f"st{c}")
                        for t in range(T):
                            pe.wait_ge(*acc_read[group_bank("lv", t)].at(l, group_k("lv")))
                        pe.sem_inc(passed.sem, 1)
                        rows = slice(CHUNK * (c % 2), CHUNK * (c % 2) + CHUNK)
                        for h in range(GH):
                            p, hh = h // 2, h % 2
                            last = pe.matmul(ps[GDK * hh:GDK * hh + GDK, p * P:(p + 1) * P],
                                             kdn[rows, c // 2, h * GDK:(h + 1) * GDK],
                                             lv[rows, c // 2, h * GDV:(h + 1) * GDV], start=True, stop=True)
                        job_end(f"st{c}", last)
                    elif kind == "g_out":
                        for hh in range(2):
                            ps = job_start(f"go{hh}")
                            if hh == 0:
                                pe.wait_ge(*state_in.at(l, 3))
                                jobs_read([f"lev{len(LEVELS) - 1}_{i}" for i in range(2)], "go0")
                            rows = slice(GDK * hh, GDK * hh + GDK)
                            for i in range(2 * T):
                                t, p = i // 2, i % 2
                                h = 2 * p + hh
                                cols = slice(i * GDV, (i + 1) * GDV)
                                pe.matmul(ps[:, cols], aT[:, hh, i, :], lv[:, t, h * GDV:(h + 1) * GDV], start=True,
                                          stop=False, skip_group_check=True)
                                for c in range(2 * t, 2 * t + 2):
                                    if c:
                                        o_rows = slice(CHUNK * (c % 2), CHUNK * (c % 2) + CHUNK)
                                        last = pe.matmul(ps[o_rows, cols], qg[rows, p, c * CHUNK:(c + 1) * CHUNK],
                                                         state[rows, c - 1, p, :], start=False, stop=c % 2 == 1,
                                                         skip_group_check=True)
                            job_end(f"go{hh}", last)
                    elif kind == "g_turn":
                        jobs_read(["go0", "go1"], "gT0")
                        turn(JOBS_OF[kind], slr)
                    elif kind in ("q_turn", "k_turn"):
                        n = 0 if kind == "q_turn" else 1
                        pe.wait_ge(*rope_out.at(l, n + 1))
                        turn(JOBS_OF[kind], xs[:, :, n * 512:n * 512 + 512])
                    elif kind.startswith("scores"):
                        p = int(kind[6:])
                        if p == 0:
                            jobs_read(JOBS_OF["q_turn"] + JOBS_OF["k_turn"], "s0_0")
                        for hh in range(2):
                            job = f"s{hh}_{p}"
                            ps = job_start(job)
                            rows = slice(DH * hh, DH * hh + DH)
                            for t in range(T):
                                last = pe.matmul(ps[:, t * P:t * P + (t + 1) * P], qT[rows, p, t * P:(t + 1) * P],
                                                 kT[rows, p, 0:(t + 1) * P], start=True, stop=True)
                            job_end(job, last)
                    elif kind.startswith("probs"):
                        p = int(kind[5:])
                        pe.wait_ge(*p_norm.at(l, p + 1))
                        for job, lo, hi in ((f"pa_{p}", 0, 4), (f"pb_{p}", 4, 6)):
                            ps = job_start(job)
                            for i in range(lo, hi):
                                last = pe.transpose(ps[:, (i - lo) * P:(i - lo + 1) * P], pr[:, p % 2, i, :], ident[:])
                            job_end(job, last)
                    elif kind.startswith("values"):
                        p = int(kind[6:])
                        jobs_read([f"pa_{p}", f"pb_{p}"], f"o_{p}")
                        if p == 0:
                            for t in range(T):
                                pe.wait_ge(*acc_read[group_bank("mv", t)].at(l, group_k("mv")))
                        ps = job_start(f"o_{p}")
                        for hh in range(2):
                            h = 2 * p + hh
                            o_rows = slice(DH * hh, DH * hh + DH)
                            cols = slice(h * DH, (h + 1) * DH)
                            pe.matmul(ps[o_rows, 0:P], v[:, 0, cols], prT[:, 3 * hh, :], start=True, stop=True,
                                      skip_group_check=True)
                            pe.matmul(ps[o_rows, P:S], v[:, 0, cols], prT[:, 3 * hh + 1, :], start=True, stop=False,
                                      skip_group_check=True)
                            last = pe.matmul(ps[o_rows, P:S], v[:, 1, cols], prT[:, 3 * hh + 2, :], start=False,
                                             stop=True, skip_group_check=True)
                        job_end(f"o_{p}", last)
                    elif kind == "ln_mean":
                        pe.wait_ge(*taps_in.at(l, 1))
                        ps = job_start("mu")
                        for c in range(CC):
                            last = pe.matmul(ps[:, 0:S], over_ch[:], acc[:, c, :], start=c == 0, stop=c == CC - 1)
                        job_end("mu", last)
                    elif kind == "ln_var":
                        pe.wait_ge(*ch_sq.at(l, 1))
                        ps = job_start("var")
                        for c in range(CC):
                            last = pe.matmul(ps[:, 0:S], over_ch[:], square[:, c, :], start=c == 0,
                                             stop=c == CC - 1)
                        job_end("var", last)
                    elif kind.startswith("hid_turn"):
                        n = int(kind[8:])
                        pe.wait_ge(*hid_sq.at(l, n + 1))
                        turn(JOBS_OF[kind], hid[:, n % 2])


_IN_ORDER = ["x", "positions", "inv_freq", "packed", "w_in", "b_gate", "w_gla_a2", "g_gla_norm", "w_moba_o",
             "w_gla_o", "w_conv_o", "w_mix_out", "g_mix_post", "w_mlp_up", "w_mlp_down", "g_mlp_post"]


def kernel(**inputs):
    import numpy as np
    import concourse.bacc as bacc
    from concourse.bass_utils import run_bass_kernel_spmd

    def chunks(a):
        a = np.asarray(a)
        a = a.reshape(a.shape[:-1] + (a.shape[-1] // P, P))
        a = np.moveaxis(a, -1, 1)
        return np.moveaxis(a, -1, 2).reshape(a.shape[0], P, -1)

    data = {k: np.ascontiguousarray(v) for k, v in inputs.items()}
    data["positions"] = np.ascontiguousarray(data["positions"].reshape(T, P).T)
    freq = np.float32(10000.0) ** (-np.arange(HALF, dtype=np.float32) / np.float32(HALF))
    data["inv_freq"] = np.ascontiguousarray(np.broadcast_to(freq.astype(np.float32), (P, HALF)))
    data["packed"] = np.ascontiguousarray(np.concatenate(
        [chunks(data[n]) for n in ("g_mix_pre", "g_mlp_pre", "b_gla_a", "g_conv_ln", "b_conv_ln", "b_dw", "w_dw")],
        axis=-1))
    nc = bacc.Bacc("TRN2", target_bir_lowering=False, num_devices=1)
    arrays, args = {}, []
    for name in _IN_ORDER:
        arrays[name + "_dram"] = data[name]
        args.append(nc.dram_tensor(name + "_dram", data[name].shape, mybir.dt.from_np(data[name].dtype),
                                   kind="ExternalInput").ap())
    out = nc.dram_tensor("out_dram", (1, S, D), F32, kind="ExternalOutput").ap()
    trunk(nc, *args, out)
    r = run_bass_kernel_spmd(nc, [arrays], core_ids=[0])
    return r.results[0]["out_dram"]
```
